# Optimizing a Trainium2 kernel written in Bass

```python
import math
import jax
import jax.numpy as jnp
from jax import lax
import numpy as np

D_MODEL = 1024
BATCH = 1
SEQ = 512
DEPTH = 2

GDN_HEADS = D_MODEL // 256
GDN_DK = 128
GDN_DV = 128
GDN_QK_W = GDN_HEADS * GDN_DK
GDN_W = GDN_HEADS * GDN_DV
CONV_K = 4
CHUNK = 64
DIFF_HEADS = D_MODEL // 256
DIFF_D = 64
DIFF_W = DIFF_HEADS * 2 * DIFF_D
Q_BLOCK = 128
MIX_W = GDN_W + DIFF_W
D_FF = ((8 * D_MODEL // 3 + 127) // 128) * 128
ROPE_THETA = 10000.0
EPS = 1e-6
IN_SPLITS = (2 * GDN_QK_W + GDN_W,
             GDN_W,
             GDN_HEADS,
             GDN_HEADS,
             DIFF_W,
             DIFF_W,
             DIFF_W)
N_IN = sum(IN_SPLITS)

kernel_name = 'hybrid_gdn_diffattn_macaron'

def lambda_init(layer):
    return 0.8 - 0.6 * math.exp(-0.3 * layer)

def rms_norm(x, w):
    xf = x.astype(jnp.float32)
    y = xf * lax.rsqrt(jnp.mean(xf * xf, axis=-1, keepdims=True) + EPS)
    return (y * w.astype(jnp.float32)).astype(x.dtype)

def l2norm(x):
    return x * lax.rsqrt(jnp.sum(x * x, axis=-1, keepdims=True) + EPS)

def swiglu(h, w_gate, w_up, w_down):
    return (jax.nn.silu(h @ w_gate) * (h @ w_up)) @ w_down

def rope_tables(seq):
    inv = 1.0 / (ROPE_THETA ** (jnp.arange(0, DIFF_D, 2, dtype=jnp.float32) / DIFF_D))
    ang = jnp.arange(seq, dtype=jnp.float32)[:, None] * inv[None, :]
    return jnp.cos(ang), jnp.sin(ang)

def apply_rope(x, cos, sin):
    xf = x.astype(jnp.float32)
    x1, x2 = jnp.split(xf, 2, axis=-1)
    c = cos[None, :, None, None, :]
    s = sin[None, :, None, None, :]
    return jnp.concatenate([x1 * c - x2 * s, x2 * c + x1 * s], axis=-1).astype(x.dtype)

def causal_conv_silu(x, w):
    c = x.shape[-1]
    y = lax.conv_general_dilated(x, w[:, None, :].astype(x.dtype), window_strides=(1,),
                                 padding=[(CONV_K - 1, 0)],
                                 dimension_numbers=('NWC', 'WIO', 'NWC'),
                                 feature_group_count=c)
    return jax.nn.silu(y)

def chunk_gated_delta_rule(q, k, v, g, beta):
    b, h, s, dk = q.shape
    dv = v.shape[-1]
    n = s // CHUNK
    q = q.reshape(b, h, n, CHUNK, dk)
    k = k.reshape(b, h, n, CHUNK, dk)
    v = v.reshape(b, h, n, CHUNK, dv)
    gc = jnp.cumsum(g.reshape(b, h, n, CHUNK), axis=-1)
    beta = beta.reshape(b, h, n, CHUNK)
    idx = jnp.arange(CHUNK)
    lower = idx[:, None] >= idx[None, :]
    strict = idx[:, None] > idx[None, :]
    decay_mat = jnp.exp(jnp.where(lower, gc[..., :, None] - gc[..., None, :], -jnp.inf))
    k_beta = k * beta[..., None]
    m = jnp.where(strict, jnp.einsum('bhncd,bhnmd->bhncm', k_beta, k) * decay_mat, 0.0)
    eye = jnp.eye(CHUNK, dtype=q.dtype)
    rhs = jnp.concatenate([v * beta[..., None], k_beta * jnp.exp(gc)[..., None]], axis=-1)
    sol = lax.linalg.triangular_solve(eye + m, rhs, left_side=True, lower=True, unit_diagonal=True)
    u, w = sol[..., :dv], sol[..., dv:]
    qk = jnp.einsum('bhncd,bhnmd->bhncm', q, k) * decay_mat
    q_dec = q * jnp.exp(gc)[..., None]
    g_last = gc[..., -1]
    k_dec = k * jnp.exp(g_last[..., None] - gc)[..., None]

    def step(state, xs):
        q_i, k_i, u_i, w_i, qk_i, gl_i = xs
        v_new = u_i - jnp.einsum('bhcd,bhde->bhce', w_i, state)
        o_i = jnp.einsum('bhcd,bhde->bhce', q_i, state) + jnp.einsum('bhcm,bhme->bhce', qk_i, v_new)
        state = state * jnp.exp(gl_i)[..., None, None] + jnp.einsum('bhcd,bhce->bhde', k_i, v_new)
        return state, o_i

    xs = tuple(jnp.moveaxis(t, 2, 0) for t in (q_dec, k_dec, u, w, qk, g_last))
    state0 = jnp.zeros((b, h, dk, dv), q.dtype)
    _, o = lax.scan(step, state0, xs)
    return jnp.moveaxis(o, 0, 2).reshape(b, h, s, dv)

def gdn_group(qkv, gate, alpha, beta_logit, conv_w, a_log, dt_bias, norm_w):
    f32 = jnp.float32
    b, s, _ = qkv.shape
    out_dtype = qkv.dtype
    qkv = causal_conv_silu(qkv, conv_w).astype(f32)
    q, k, v = jnp.split(qkv, [GDN_QK_W, 2 * GDN_QK_W], axis=-1)
    q = l2norm(q.reshape(b, s, GDN_HEADS, GDN_DK).transpose(0, 2, 1, 3)) * GDN_DK ** -0.5
    k = l2norm(k.reshape(b, s, GDN_HEADS, GDN_DK).transpose(0, 2, 1, 3))
    v = v.reshape(b, s, GDN_HEADS, GDN_DV).transpose(0, 2, 1, 3)
    g = (-jnp.exp(a_log.astype(f32)) * jax.nn.softplus(alpha.astype(f32) + dt_bias.astype(f32))).transpose(0, 2, 1)
    beta = jax.nn.sigmoid(beta_logit.astype(f32)).transpose(0, 2, 1)
    o = chunk_gated_delta_rule(q, k, v, g, beta).transpose(0, 2, 1, 3)
    o = rms_norm(o, norm_w) * jax.nn.silu(gate.astype(f32).reshape(b, s, GDN_HEADS, GDN_DV))
    return o.reshape(b, s, GDN_W).astype(out_dtype)

def diff_group(q, k, v, lq1, lk1, lq2, lk2, norm_w, cos, sin, lam_init):
    f32 = jnp.float32
    b, s, _ = q.shape
    q = apply_rope(q.reshape(b, s, DIFF_HEADS, 2, DIFF_D), cos, sin).transpose(0, 2, 3, 1, 4)
    k = apply_rope(k.reshape(b, s, DIFF_HEADS, 2, DIFF_D), cos, sin).transpose(0, 2, 3, 1, 4)
    v = v.reshape(b, s, DIFF_HEADS, 2 * DIFF_D).transpose(0, 2, 1, 3)
    lam = (jnp.exp(jnp.sum(lq1.astype(f32) * lk1.astype(f32)))
           - jnp.exp(jnp.sum(lq2.astype(f32) * lk2.astype(f32))) + lam_init)
    n_blk = s // Q_BLOCK
    q_blocks = q.reshape(b, DIFF_HEADS, 2, n_blk, Q_BLOCK, DIFF_D).transpose(3, 0, 1, 2, 4, 5)
    key_pos = jnp.arange(s)
    scale = DIFF_D ** -0.5

    def attend(args):
        q_b, start = args
        sc = jnp.einsum('bhcqd,bhckd->bhcqk', q_b, k, preferred_element_type=f32) * scale
        q_pos = start + jnp.arange(Q_BLOCK)
        sc = jnp.where(key_pos[None, :] <= q_pos[:, None], sc, -jnp.inf)
        p = jax.nn.softmax(sc, axis=-1)
        a = p[:, :, 0] - lam * p[:, :, 1]
        return jnp.einsum('bhqk,bhke->bhqe', a.astype(v.dtype), v)

    o = lax.map(attend, (q_blocks, jnp.arange(n_blk) * Q_BLOCK))
    o = o.transpose(1, 0, 3, 2, 4).reshape(b, s, DIFF_HEADS, 2 * DIFF_D)
    o = rms_norm(o, norm_w) * (1.0 - lam_init)
    return o.reshape(b, s, DIFF_W)

def setup_inputs(seed: int = 0) -> dict:
    key = jax.random.key(seed)
    ks = iter(jax.random.split(key, 32))
    L = DEPTH
    conv_c = 2 * GDN_QK_W + GDN_W

    def nrm(k, shape, s):
        return jax.random.normal(k, shape, jnp.float32) * s

    def gain(k, shape):
        return 1.0 + 0.02 * jax.random.normal(k, shape, jnp.float32)

    dt = jnp.exp(jax.random.uniform(next(ks), (L, GDN_HEADS), jnp.float32,
                                    minval=math.log(1e-3), maxval=math.log(1e-1)))
    a_init = jax.random.uniform(next(ks), (L, GDN_HEADS), jnp.float32, minval=1.0, maxval=16.0)
    return {
        'x': nrm(next(ks), (BATCH, SEQ, D_MODEL), 1.0),
        'ffn1_norm': gain(next(ks), (L, D_MODEL)),
        'ffn1_w_gate': nrm(next(ks), (L, D_MODEL, D_FF), D_MODEL ** -0.5),
        'ffn1_w_up': nrm(next(ks), (L, D_MODEL, D_FF), D_MODEL ** -0.5),
        'ffn1_w_down': nrm(next(ks), (L, D_FF, D_MODEL), D_FF ** -0.5),
        'mix_norm': gain(next(ks), (L, D_MODEL)),
        'w_in': nrm(next(ks), (L, D_MODEL, N_IN), D_MODEL ** -0.5),
        'conv_w': nrm(next(ks), (L, CONV_K, conv_c), CONV_K ** -0.5),
        'a_log': jnp.log(a_init),
        'dt_bias': dt + jnp.log(-jnp.expm1(-dt)),
        'gdn_norm': gain(next(ks), (L, GDN_DV)),
        'lambda_q1': nrm(next(ks), (L, DIFF_D), 0.1),
        'lambda_k1': nrm(next(ks), (L, DIFF_D), 0.1),
        'lambda_q2': nrm(next(ks), (L, DIFF_D), 0.1),
        'lambda_k2': nrm(next(ks), (L, DIFF_D), 0.1),
        'diff_norm': gain(next(ks), (L, 2 * DIFF_D)),
        'w_out': nrm(next(ks), (L, MIX_W, D_MODEL), MIX_W ** -0.5),
        'ffn2_norm': gain(next(ks), (L, D_MODEL)),
        'ffn2_w_gate': nrm(next(ks), (L, D_MODEL, D_FF), D_MODEL ** -0.5),
        'ffn2_w_up': nrm(next(ks), (L, D_MODEL, D_FF), D_MODEL ** -0.5),
        'ffn2_w_down': nrm(next(ks), (L, D_FF, D_MODEL), D_FF ** -0.5),
        'final_norm': gain(next(ks), (D_MODEL,)),
    }

def reference(x, ffn1_norm, ffn1_w_gate, ffn1_w_up, ffn1_w_down, mix_norm, w_in, conv_w,
              a_log, dt_bias, gdn_norm, lambda_q1, lambda_k1, lambda_q2, lambda_k2, diff_norm,
              w_out, ffn2_norm, ffn2_w_gate, ffn2_w_up, ffn2_w_down, final_norm):
    _, s, _ = x.shape
    cos, sin = rope_tables(s)
    split_at = np.cumsum(IN_SPLITS)[:-1].tolist()
    for l in range(DEPTH):
        x = x + 0.5 * swiglu(rms_norm(x, ffn1_norm[l]), ffn1_w_gate[l], ffn1_w_up[l], ffn1_w_down[l])
        h = rms_norm(x, mix_norm[l])
        proj = h @ w_in[l]
        qkv_a, gate_a, alpha_a, beta_a, q_d, k_d, v_d = jnp.split(proj, split_at, axis=-1)
        o_a = gdn_group(qkv_a, gate_a, alpha_a, beta_a, conv_w[l], a_log[l], dt_bias[l], gdn_norm[l])
        o_d = diff_group(q_d, k_d, v_d, lambda_q1[l], lambda_k1[l], lambda_q2[l], lambda_k2[l],
                         diff_norm[l], cos, sin, lambda_init(l))
        x = x + jnp.concatenate([o_a, o_d], axis=-1) @ w_out[l]
        x = x + 0.5 * swiglu(rms_norm(x, ffn2_norm[l]), ffn2_w_gate[l], ffn2_w_up[l], ffn2_w_down[l])
    return rms_norm(x, final_norm)


_drawn_inputs = setup_inputs


def setup_inputs(seed=0):
    import zlib

    import numpy as np

    out = dict(_drawn_inputs(seed))
    spreads = {}
    factors = {'ffn1_norm': 4.02,
     'gdn_norm': 22.509,
     'diff_norm': 19.321,
     'ffn2_norm': 5.942,
     'final_norm': 7.504,
     'lambda_q1': 3.331}
    for name, (base, spread) in spreads.items():
        noise = np.random.default_rng([zlib.crc32(name.encode()), seed]).standard_normal(out[name].shape)
        drawn = base * np.exp(spread * noise) if base else spread * noise
        out[name] = jnp.asarray(drawn.astype(out[name].dtype))
    for name, factor in factors.items():
        out[name] = (out[name] * factor).astype(out[name].dtype)
    return out
```

```python
import math
from contextlib import ExitStack

import numpy as np

import concourse.bass as bass
from concourse import mybir

F32 = mybir.dt.float32
F32R = mybir.dt.float32r
ACT = mybir.ActivationFunctionType
ALU = mybir.AluOpType
AX = mybir.AxisListType

P = 128
D = 1024
S = 512
DEPTH = 2
DFF = ((8 * D // 3 + 127) // 128) * 128
H = 4
DV = 128
CH = 64
DD = 64
EPS = 1e-6
KD = D // P
KF = DFF // P
NT = S // P
NCH = S // CH
COL_Q, COL_GATE = 0, 3 * H * P
COL_AB = COL_GATE + H * P
COL_DQ = COL_AB + 2 * H
COL_DV = COL_DQ + 2 * H * P
CONV_K = 4

UP_PAIRS = KF
DOWN_PAIRS = KF // 2
PROJ_PAIRS = 14
OUT_PAIRS = KD // 2
OUT_ORDER = [2, 3, 0, 1]
PAIR_UP = [0, UP_PAIRS + DOWN_PAIRS + PROJ_PAIRS + OUT_PAIRS]
PAIR_DOWN = [PAIR_UP[0] + UP_PAIRS, PAIR_UP[1] + UP_PAIRS]
PAIR_PROJ = PAIR_DOWN[0] + DOWN_PAIRS
PAIR_OUT = PAIR_PROJ + PROJ_PAIRS
PAIRS = PAIR_DOWN[1] + DOWN_PAIRS

ROW_CONV, ROW_G1, ROW_GM, ROW_G2, ROW_GDN, ROW_DIFF, ROW_FINAL = 0, 48, 56, 64, 72, 73, 74
ROWS = 82

CONSTS = ["ones", "ident", "tri", "suffix", "rot", "causal"] + [f"level{i}" for i in range(6)]


def shape_constants():
    i = np.arange(P)
    same = (i[:, None] // CH) == (i[None, :] // CH)
    c = {
        "ones": np.ones((P, P)),
        "ident": np.eye(P),
        "tri": same & (i[:, None] <= i[None, :]),
        "suffix": same & (i[:, None] > i[None, :]),
        "causal": np.where(i[None, :] > i[:, None], -1e30, 0.0),
    }
    rot = np.zeros((P, P))
    half = DD // 2
    for o in range(P):
        if o % DD < half:
            rot[o + half, o] = -1.0
        else:
            rot[o - half, o] = 1.0
    c["rot"] = rot
    for lv in range(6):
        b = 1 << lv
        c[f"level{lv}"] = (i[:, None] // (2 * b) == i[None, :] // (2 * b)) & (i[:, None] % (2 * b) >= b) & (i[None, :] % (2 * b) < b)
    masks = np.stack([np.asarray(c[n], np.float32) for n in CONSTS], 1)
    inv = (1.0 / (np.float32(10000.0) ** (np.arange(0, DD, 2, dtype=np.float32) / np.float32(DD)))).astype(np.float32)
    ang = (np.arange(S, dtype=np.float32)[:, None] * inv[None, :]).astype(np.float32)
    angle = np.stack([np.tile(np.cos(ang).T, (4, 1)), np.tile(np.sin(ang).T, (4, 1))], 1).astype(np.float32)
    init = [0.8 - 0.6 * math.exp(-0.3 * layer) for layer in range(DEPTH)]
    lam = np.tile(np.array([[v, 1.0 - v] for v in init], np.float32)[:, None, :], (1, P, 1))
    return masks, angle, lam


def mixer_steps():
    steps = [("first",), ("proj", 0, 0), ("proj", 0, 1), ("decay",)]
    for p in range(1, 7):
        steps += [("proj", p, 0), ("proj", p, 1)]
    steps += [("l2", c) for c in range(2 * H)]
    solve = []
    for g in range(2):
        solve += [("prep", g), ("level0", g)] + [("level", g, lv) for lv in range(1, 6)] + [("solved", g)]
    rope = 0
    for p in range(7, PROJ_PAIRS):
        for j in range(2):
            if solve:
                steps.append(solve.pop(0))
            for _ in range(2 if rope < 2 * H else 0):
                if rope < min(2 * (p - 6) + j, 2 * H):
                    steps.append(("rope", rope))
                    rope += 1
            steps.append(("proj", p, j))
    steps += solve
    for j in range(NCH):
        steps.append(("scan", j))
        for i in (2 * j, 2 * j + 1):
            steps.append(("attend", i))
            if i % NT == NT - 1:
                steps.append(("headnorm", H + i // NT))
    return steps + [("headnorm", h) for h in range(H)]


def build(nc, x_in, ffn1_w_gate, ffn1_w_up, ffn1_w_down, w_in, w_out, ffn2_w_gate, ffn2_w_up, ffn2_w_down,
          ffn1_norm, mix_norm, ffn2_norm, final_norm, conv_w, a_log, dt_bias, gdn_norm, diff_norm,
          lambda_q1, lambda_k1, lambda_q2, lambda_k2, masks_in, angle_in, lam_in, out):
    ctx = ExitStack()
    with ctx:
        top = [16512]

        def at(name, cols, dt=F32, where=None):
            n = math.prod(cols)
            place = top[0] if where is None else where[0]
            t = nc.alloc_sbuf_tensor_at(name, [P] + list(cols), dt, offset=place)
            size = -(-n * 4 // 32) * 32
            if where is None:
                top[0] += size
            else:
                where[0] += size
            return t

        def sem(name):
            s = ctx.enter_context(nc.semaphore(name))
            layer_sems.append(s)
            return s

        layer_sems = []
        x = at("x", [KD, S])
        xh = at("xh", [KD, S], F32R)
        xl = at("xl", [KD, S], F32R)
        raw = at("raw", [2, 16, P])
        wh = at("wh", [2, 16, P], F32R)
        wl = at("wl", [2, 16, P], F32R)
        rstd = at("rstd", [S])
        acc = at("acc", [S])
        sq = at("sq", [S])
        ones = at("ones", [P])
        par = at("par", [ROWS])
        eps_c = at("eps_c", [2])
        w = [top[0]]
        hh = at("hh", [KF, S], F32R, w)
        hl = at("hl", [KF, S], F32R, w)
        tg = at("tg", [S], F32, w)
        tu = at("tu", [S], F32, w)
        ffn_end = w[0]
        w = [top[0]]
        qkv = at("qkv", [3 * H, S], F32, w)
        wT = at("wT", [NT, H, P], F32, w)
        qkT = at("qkT", [NT, H, P], F32, w)
        dqk = at("dqk", [2 * H, S], F32, w)
        V = at("V", [NT, H * P], F32, w)
        gate = at("gate", [H, S], F32, w)
        state = at("state", [H, P], F32, w)
        vnew = at("vnew", [H, P], F32, w)
        angle = at("angle", [2, S], F32, w)
        masks = at("masks", [len(CONSTS) - 1, P], F32, w)
        solve = [w[0]]
        bM = [at(f"bM{s}", [H, P], F32, w) for s in range(2)]
        bB = [at(f"bB{s}", [H, P], F32, w) for s in range(2)]
        bT = [at(f"bT{s}", [H, P], F32, w) for s in range(2)]
        bU = [at(f"bU{s}", [H, P], F32, w) for s in range(2)]
        mixer_end = w[0]
        xin = at("xin", [S + CONV_K], F32, solve)
        yconv = [at(f"yconv{s}", [S], F32, solve) for s in range(2)]
        abw = at("abw", [KD, 2 * H], F32, solve)
        abh = at("abh", [KD, 2 * H], F32R, solve)
        abl = at("abl", [KD, 2 * H], F32R, solve)
        assert solve[0] <= mixer_end
        solve = [top[0] + (mixer_end - 8 * S * 4 - top[0])]
        prob = [[at(f"prob{b}{s}", [S], F32, solve) for s in range(2)] for b in range(2)]
        attT = [at(f"attT{b}", [NT, P], F32, solve) for b in range(2)]
        assert solve[0] <= mixer_end
        w = [max(ffn_end, mixer_end)]
        rtok = at("rtok", [NT], F32, w)
        ab = at("ab", [NT, 2 * H], F32, w)
        gl = at("gl", [NT, H], F32, w)
        gt = at("gt", [NT, H], F32, w)
        beta = at("beta", [NT, H], F32, w)
        gcol = at("gcol", [NT, H], F32, w)
        ecol = at("ecol", [NT, H], F32, w)
        esuf = at("esuf", [NT, H], F32, w)
        egl = at("egl", [NT, H, 2], F32, w)
        hpar = at("hpar", [2, H], F32, w)
        lam = at("lam", [4], F32, w)
        lsum = at("lsum", [2], F32, w)
        dnorm = at("dnorm", [1], F32, w)
        mx = at("mx", [2, 2], F32, w)
        ssum = at("ssum", [2, 2], F32, w)
        rsum = at("rsum", [2, 2], F32, w)
        assert w[0] <= nc.sbuf_usable_end, (w[0], nc.sbuf_usable_end)

        def mask(name):
            return masks[:, CONSTS.index(name) - 1, :]

        def over_heads(ap):
            return ap.unsqueeze(1).broadcast_to([P, H, P])

        def over_cols(ap):
            return ap.unsqueeze(2).broadcast_to([P, H, P])

        ps = [ctx.enter_context(nc.psum_tensor(f"ps{i}", [P, S], F32)) for i in range(8)]

        def heads(bank):
            return ps[bank][:].rearrange("p (h c) -> p h c", h=H)

        xtok = hh[:, 0:8, :].bitcast(F32)

        s_in = [ctx.enter_context(nc.semaphore(f"x_loaded{t}")) for t in range(NT)]
        s_const = ctx.enter_context(nc.semaphore("const_loaded"))
        s_turn = ctx.enter_context(nc.semaphore("turned"))
        s_kept = ctx.enter_context(nc.semaphore("turned_kept"))
        s_memset = ctx.enter_context(nc.semaphore("memset_done"))
        xstage = nc.alloc_sbuf_tensor_at("xstage", [P, NT, D], F32, offset=top[0])
        ident0 = nc.alloc_sbuf_tensor_at("ident0", [P, P], F32, offset=top[0] + NT * D * 4)
        with nc.Block() as block:
            @block.sync
            def _(sp):
                sp.dma_start(ident0[:], masks_in[:, CONSTS.index("ident"), :]).then_inc(s_const, 16)
                sp.dma_start(ones[:], masks_in[:, CONSTS.index("ones"), :]).then_inc(s_const, 16)
                for t in range(NT):
                    sp.dma_start(xstage[:, t, :], x_in[t * P:(t + 1) * P, :]).then_inc(s_in[t], 16)

            @block.tensor
            def _(pe):
                pe.wait_ge(s_const, 32)
                for t in range(NT):
                    pe.wait_ge(s_in[t], 16)
                    for q in range(2):
                        for j in range(4):
                            last = pe.transpose(ps[2 * t + q][:, j * P:(j + 1) * P],
                                                xstage[:, t, (4 * q + j) * P:(4 * q + j + 1) * P], ident0[:])
                        last.then_inc(s_turn, 1)

            @block.vector
            def _(dve):
                dve.memset(eps_c[:, 0:1], EPS).then_inc(s_memset, 1)
                dve.memset(eps_c[:, 1:2], -0.5 * math.log(P)).then_inc(s_memset, 1)
                for t in range(NT):
                    for q in range(2):
                        dve.wait_ge(s_turn, 2 * t + q + 1)
                        dve.tensor_copy(x[:, 4 * q:4 * q + 4, t * P:(t + 1) * P],
                                        ps[2 * t + q][:].rearrange("p (j c) -> p j c", j=4)).then_inc(s_kept, 1)

        raw_in = [sem(f"raw_in{s}") for s in range(2)]
        hi_done = sem("hi_done")
        lo_done = sem("lo_done")
        pair_done = sem("pair_done")
        down_done = sem("down_done")
        out_done = sem("out_done")
        half_done = sem("half_done")
        x_new = sem("x_new")
        xh_done = sem("xh_done")
        x_chunk = sem("x_chunk")
        sq_done = sem("sq_done")
        acc_done = sem("acc_done")
        norm_mm = sem("norm_mm")
        ln_done = sem("ln_done")
        rstd_done = sem("rstd_done")
        tg_done, sg_done, up_evac = sem("tg_done"), sem("sg_done"), sem("up_evac")
        h_new, hh_done, h_done = sem("h_new"), sem("hh_done"), sem("h_done")
        par_in, par_turn, par_done = sem("par_in"), sem("par_turn"), sem("par_done")
        mix_in = sem("mix_in")
        act_chain, dve_chain, pool_chain = sem("act_chain"), sem("dve_chain"), sem("pool_chain")
        ab_split, ab_mm, ab_evac = sem("ab_split"), sem("ab_mm"), sem("ab_evac")
        rtok_done, spe_in, spe_exp, spe_ln = sem("rtok_done"), sem("spe_in"), sem("spe_exp"), sem("spe_ln")
        g_done, gcol_mm, gcol_exp, gcol_done = sem("g_done"), sem("gcol_mm"), sem("gcol_exp"), sem("gcol_done")
        ab_hi = sem("ab_hi")
        mix_evac, v_evac = sem("mix_evac"), sem("v_evac")
        conv_done, silu_done, gate_done = sem("conv_done"), sem("silu_done"), sem("gate_done")
        rope_mm, rope_done = sem("rope_mm"), sem("rope_done")
        l2_sq, l2_mm, l2_r, l2_done = sem("l2_sq"), sem("l2_mm"), sem("l2_r"), sem("l2_done")
        gu_done, grow_mm, e_done = sem("gu_done"), sem("grow_mm"), sem("e_done")
        dx_done, dmin_done, dexp_done = sem("dx_done"), sem("dmin_done"), sem("dexp_done")
        dmask_done, kk_mm, qk_mm, m_done, qdec_done = (sem("dmask_done"), sem("kk_mm"), sem("qk_mm"), sem("m_done"),
                                                       sem("qdec_done"))
        qkT_done = sem("qkT_done")
        t0_done, t0_turn, u0_done = sem("t0_done"), sem("t0_turn"), sem("u0_done")
        b_done, r_mm, r_done, dt_mm, du_mm, tu_done = (sem("b_done"), sem("r_mm"), sem("r_done"), sem("dt_mm"),
                                                       sem("du_mm"), sem("tu_done"))
        kturn, vturn, kb_done, vb_done = sem("kturn"), sem("vturn"), sem("kb_done"), sem("vb_done")
        w_mm, u_mm, w_done, u_done = sem("w_mm"), sem("u_mm"), sem("w_done"), sem("u_done")
        ws_mm, vnew_done, sup_mm, s_done, o_mm, o_done = (sem("ws_mm"), sem("vnew_done"), sem("sup_mm"),
                                                          sem("s_done"), sem("o_mm"), sem("o_done"))
        sc_mm, mx_done, p_done, a_done = sem("sc_mm"), sem("mx_done"), sem("p_done"), sem("a_done")
        at_mm, at_done, pv_mm, pv_done = sem("at_mm"), sem("at_done"), sem("pv_mm"), sem("pv_done")
        hn_sq, hn_mm, hn_r, hn_out, hn_hi, hn_done = (sem("hn_sq"), sem("hn_mm"), sem("hn_r"), sem("hn_out"),
                                                      sem("hn_hi"), sem("hn_done"))
        lam_prod, lam_exp, lam_done = sem("lam_prod"), sem("lam_exp"), sem("lam_done")

        steps = mixer_steps()
        MIX_PARTS = 2 + 2 + 1 + 4 + 1

        def headnorm_order(hd):
            return hd - H if hd >= H else H + hd

        def tmp_of(o):
            return vnew[:].rearrange("p h c -> p (h c)") if o >= H else angle[:, 0]

        def body(l):
            with nc.Block() as block:
                @block.sync
                def _(sp):
                    rows = [(conv_w[l].rearrange("k (c p) -> (k c) p", p=P), ROW_CONV, 48),
                            (ffn1_norm[l].rearrange("(c p) -> c p", p=P), ROW_G1, KD),
                            (mix_norm[l].rearrange("(c p) -> c p", p=P), ROW_GM, KD),
                            (ffn2_norm[l].rearrange("(c p) -> c p", p=P), ROW_G2, KD),
                            (gdn_norm[l].unsqueeze(0), ROW_GDN, 1),
                            (diff_norm[l].unsqueeze(0), ROW_DIFF, 1),
                            (final_norm.rearrange("(c p) -> c p", p=P), ROW_FINAL, KD)]
                    for src, r, n in rows:
                        sp.dma_start(acc[r:r + n, 0:P], src).then_inc(par_in, 16)
                    sp.dma_start(acc[:, P:2 * P], masks_in[:, CONSTS.index("ident"), :]).then_inc(par_in, 16)

                    def load(n, slot, parts):
                        sp.wait_ge(lo_done, n + 1)
                        for dst, src in parts:
                            sp.dma_start(dst, src).then_inc(raw_in[slot], 16)

                    def load_up(f, i, slot):
                        mats = (ffn1_w_gate, ffn1_w_up) if f == 0 else (ffn2_w_gate, ffn2_w_up)
                        load(i + PAIR_UP[f], slot, [
                            (raw[:, slot, KD * a:KD * a + KD, :],
                             m[l].rearrange("(k p) (n c) -> n p k c", p=P, c=P)[i]) for a, m in enumerate(mats)])

                    def load_rows(n, slot, m, j):
                        rows_of = m[l].rearrange("(j k p) n -> j k p n", k=2, p=P)[j]
                        load(n, slot, [
                            (raw[:, slot, KD * a:KD * a + KD, :].rearrange("p m c -> p (m c)"), rows_of[a])
                            for a in range(2)])

                    def load_cols(n, slot, mat, col):
                        src = mat[l].rearrange("(k p) n -> p k n", p=P)
                        dst = raw[:, slot, :, :].rearrange("p (k a) c -> p k (a c)", a=2)
                        load(n, slot, [(dst[:, 4 * a:4 * a + 4, :], src[:, 4 * a:4 * a + 4, col:col + 2 * P])
                                       for a in range(2)])

                    def ffn(f):
                        down = ffn1_w_down if f == 0 else ffn2_w_down
                        with sp.Fori(0, UP_PAIRS // 2) as it:
                            for u in range(2):
                                load_up(f, it * 2 + u, (PAIR_UP[f] + u) % 2)
                        with sp.Fori(0, DOWN_PAIRS // 2) as it:
                            for u in range(2):
                                load_rows(it * 2 + u + PAIR_DOWN[f], (PAIR_DOWN[f] + u) % 2, down, it * 2 + u)
                        last = PAIR_DOWN[f] + DOWN_PAIRS - 1
                        load_rows(last, last % 2, down, DOWN_PAIRS - 1)

                    ffn(0)
                    sp.wait_ge(pair_done, 2 + PAIR_PROJ)
                    sp.dma_start(masks[:], masks_in[:, 1:, :]).then_inc(mix_in, 16)
                    sp.dma_start(angle[:], angle_in).then_inc(mix_in, 16)
                    sp.dma_start(abw[:], w_in[l].rearrange("(k p) n -> p k n", p=P)[:, :, COL_AB:COL_AB + 2 * H])\
                      .then_inc(mix_in, 16)
                    sp.dma_start(hpar[:, 0, :], a_log[l].unsqueeze(0).broadcast_to([P, H])).then_inc(mix_in, 16)
                    sp.dma_start(hpar[:, 1, :], dt_bias[l].unsqueeze(0).broadcast_to([P, H])).then_inc(mix_in, 16)
                    sp.dma_start(lam[:, 0:2], lam_in[l]).then_inc(mix_in, 16)
                    for i, v in enumerate((lambda_q1, lambda_k1, lambda_q2, lambda_k2)):
                        sp.dma_start(state[:, i, 0:DD], v[l].unsqueeze(0).broadcast_to([P, DD])).then_inc(mix_in, 16)
                    for p in range(PROJ_PAIRS):
                        col = 2 * P * p if p < 6 else COL_DQ + 2 * P * (p - 6) if p < 12 else COL_GATE + 2 * P * (p - 12)
                        load_cols(PAIR_PROJ + p, (PAIR_PROJ + p) % 2, w_in, col)
                    for p in range(OUT_PAIRS):
                        load_rows(PAIR_OUT + p, (PAIR_OUT + p) % 2, w_out, OUT_ORDER[p])
                    ffn(1)

                @block.scalar
                def _(act):
                    def chained(counter=[0]):
                        counter[0] += 1
                        act.wait_ge(act_chain, counter[0])

                    def split(n, slot, k):
                        act.wait_ge(raw_in[slot], (k + 1) * 32)
                        act.wait_ge(pair_done, n + 1)
                        act.activation(wh[:, slot], raw[:, slot], ACT.Copy).then_inc(hi_done, 1)

                    def split_static(n):
                        if n < PAIRS:
                            split(n, n % 2, n // 2)

                    def heads_of_x(s, gain_row):
                        for m in range(KD):
                            if s:
                                act.wait_ge(x_new, KD * (s - 1) + m + 1)
                            if s == 2 and m == 0:
                                act.wait_ge(pair_done, 2 + PAIR_OUT + OUT_PAIRS)
                            act.activation(xh[:, m], x[:, m], ACT.Copy, scale=par[:, gain_row + m:gain_row + m + 1])\
                               .then_inc(xh_done, 1)

                    def norm_factor(s):
                        act.wait_ge(norm_mm, s + 1)
                        act.activation(sq[:], ps[7][:], ACT.Ln, scale=1.0 / D, bias=eps_c[:, 0:1]).then_inc(ln_done, 1)
                        act.wait_ge(ln_done, s + 1)
                        act.activation(rstd[:], sq[:], ACT.Exp, scale=-0.5).then_inc(rstd_done, 1)

                    def up_step(f, i):
                        q = i + UP_PAIRS * f
                        act.wait_ge(tg_done, q + 1)
                        act.activation(tg[:], tg[:], ACT.Silu).then_inc(sg_done, 1)
                        act.wait_ge(h_new, q + 1)
                        at_i = hh[:, i] if isinstance(i, int) else hh[:, bass.ds(i, 1)].rearrange("p a c -> p (a c)")
                        act.activation(at_i, tu[:], ACT.Copy).then_inc(hh_done, 1)

                    def ffn(f):
                        norm_factor(2 * f)
                        for i in range(2):
                            up_step(f, i)
                            split_static(PAIR_UP[f] + i + 2)
                        with act.Fori(1, UP_PAIRS // 2) as it:
                            for u in range(2):
                                n = PAIR_UP[f] + u + 2
                                up_step(f, it * 2 + u)
                                split(it * 2 + n, n % 2, it + n // 2)
                        for j in range(DOWN_PAIRS - 1):
                            split_static(PAIR_DOWN[f] + j + 2)

                    act.wait_ge(par_turn, 1)
                    act.activation(par[:], ps[0][:, 0:ROWS], ACT.Copy).then_inc(par_done, 1)
                    act.wait_ge(par_done, 1)
                    split_static(0)
                    heads_of_x(0, ROW_G1)
                    split_static(1)
                    ffn(0)
                    heads_of_x(1, ROW_GM)
                    split_static(PAIR_PROJ + 1)

                    def act_step(kind, *a):
                        if kind == "first":
                            norm_factor(1)
                        elif kind == "proj":
                            p, j = a
                            if p < 6:
                                c = 2 * p + j
                                act.wait_ge(conv_done, c + 1)
                                act.activation(qkv[:, c], yconv[c % 2][:], ACT.Silu).then_inc(silu_done, 1)
                            elif p in (10, 11):
                                if j == 0:
                                    act.wait_ge(half_done, p + 1)
                                else:
                                    act.wait_ge(pair_done, 2 + PAIR_PROJ + p + 1)
                                for b in range(2):
                                    i = act.activation(V[:, 2 * j + b, (p - 10) * 256:(p - 9) * 256],
                                                       ps[2 * (p % 2) + j][:, b * 256:(b + 1) * 256], ACT.Copy,
                                                       scale=rtok[:, 2 * j + b:2 * j + b + 1])
                                i.then_inc(v_evac, 1)
                            elif p >= 12:
                                c = 2 * (p - 12) + j
                                act.wait_ge(mix_evac, 20 + c + 1)
                                act.activation(gate[:, c], gate[:, c], ACT.Silu).then_inc(gate_done, 1)
                            if j == 1:
                                split_static(PAIR_PROJ + p + 2)
                        elif kind == "decay":
                            act.wait_ge(mix_in, 16 * MIX_PARTS)
                            act.activation(abh[:], abw[:], ACT.Copy).then_inc(ab_hi, 1)
                            act.activation(hpar[:, 0, :], hpar[:, 0, :], ACT.Exp).then_inc(spe_exp, 1)
                            act.wait_ge(lam_prod, 2)
                            act.activation(lsum[:], lsum[:], ACT.Exp).then_inc(lam_exp, 1)
                            act.wait_ge(ab_mm, 1)
                            act.activation(gt[:, :, 0], ps[6][:, 64:64 + NT], ACT.Ln, scale=1.0 / D,
                                           bias=eps_c[:, 0:1]).then_inc(act_chain, 1)
                            chained()
                            act.activation(rtok[:], gt[:, :, 0], ACT.Exp, scale=-0.5).then_inc(rtok_done, 1)
                            act.wait_ge(spe_in, 1)
                            act.activation(gt[:], gt[:], ACT.Exp, scale=-1.0).then_inc(act_chain, 1)
                            chained()
                            act.activation(gt[:], gt[:], ACT.Ln, bias=1.0).then_inc(spe_ln, 1)
                            act.activation(beta[:], ab[:, :, H:2 * H], ACT.Exp, scale=-1.0).then_inc(spe_exp, 1)
                            act.wait_ge(gcol_mm, 1)
                            act.activation(ecol[:], ps[6][:, 128:128 + NT * H].rearrange("p (t h) -> p t h", h=H),
                                           ACT.Exp).then_inc(gcol_exp, 1)
                            act.activation(gcol[:], ps[6][:, 128:128 + NT * H].rearrange("p (t h) -> p t h", h=H),
                                           ACT.Copy).then_inc(gcol_exp, 1)
                            act.activation(esuf[:], ps[6][:, 192:192 + NT * H].rearrange("p (t h) -> p t h", h=H),
                                           ACT.Exp).then_inc(gcol_exp, 1)
                        elif kind == "l2":
                            c, = a
                            if c == 0:
                                act.wait_ge(silu_done, 3 * H)
                            if c >= 1:
                                act.wait_ge(l2_mm, c)
                                act.wait_ge(l2_done, c)
                            act.activation(sq[:], qkv[:, c], ACT.Square).then_inc(l2_sq, 1)
                            act.wait_ge(l2_mm, c + 1)
                            act.activation(acc[:], ps[4 + c % 4][:], ACT.Ln, bias=eps_c[:, 0:1]).then_inc(act_chain, 1)
                            chained()
                            bias = eps_c[:, 1:2] if c < H else 0.0
                            act.activation(acc[:], acc[:], ACT.Exp, scale=-0.5, bias=bias).then_inc(l2_r, 1)
                        elif kind == "prep":
                            g, = a
                            for s in range(2):
                                t, o = 2 * g + s, 2 * g + s
                                act.wait_ge(grow_mm, o + 1)
                                act.activation(bB[s][:], heads(4 + 2 * s), ACT.Exp).then_inc(e_done, 1)
                                act.wait_ge(dmin_done, 2 * (o + 1))
                                act.activation(bT[s][:], bT[s][:], ACT.Exp).then_inc(dexp_done, 1)
                                act.activation(bM[s][:], bM[s][:], ACT.Exp, scale=-1.0).then_inc(dexp_done, 1)
                        elif kind == "level0":
                            g, = a
                            for s in range(2):
                                o = 2 * g + s
                                act.wait_ge(t0_turn, o + 1)
                                act.activation(bU[s][:], heads(4 + 2 * s), ACT.Copy).then_inc(u0_done, 1)
                        elif kind == "level":
                            g, lv = a
                            for s in range(2):
                                o = (g * 5 + lv - 1) * 2 + s
                                act.wait_ge(r_mm, o + 1)
                                act.activation(wT[:, 2 * g + s], heads(4 + 2 * s), ACT.Copy).then_inc(r_done, 1)
                        elif kind == "solved":
                            g, = a
                            for s in range(2):
                                t, o = 2 * g + s, 2 * g + s
                                act.wait_ge(w_mm, o + 1)
                                act.activation(wT[:, t], heads(4 + 2 * s), ACT.Copy).then_inc(w_done, 1)
                                act.wait_ge(u_mm, o + 1)
                                act.activation(qkv[:, 2 * H:3 * H, t * P:(t + 1) * P], heads(5 + 2 * s), ACT.Copy)\
                                   .then_inc(u_done, 1)
                        elif kind == "scan":
                            j, = a
                            act.wait_ge(o_mm, j + 1)
                            act.activation(qkv[:, 0:H, j * CH:(j + 1) * CH],
                                           ps[6][:, 0:H * CH].rearrange("p (h c) -> p h c", h=H), ACT.Copy)\
                               .then_inc(o_done, 1)
                        elif kind == "attend":
                            i, = a
                            h, t = divmod(i, NT)
                            n, b = (t + 1) * P, i % 2
                            act.wait_ge(mx_done, i + 1)
                            if i >= 2:
                                act.wait_ge(a_done, i - 1)
                                act.wait_ge(at_mm, i - 1)
                            for s in range(2):
                                act.activation(prob[b][s][:, 0:n], ps[s][:, 0:n], ACT.Exp, scale=DD ** -0.5,
                                               bias=mx[:, b, s:s + 1], accum_out=ssum[:, b, s:s + 1]).then_inc(p_done, 1)
                            if i >= 2:
                                act.wait_ge(pv_mm, i - 1)
                            act.wait_ge(at_mm, i + 1)
                            act.activation(attT[b][:, 0:t + 1, :],
                                           ps[2][:, 0:n].rearrange("p (k c) -> p k c", c=P), ACT.Copy).then_inc(at_done, 1)
                            act.wait_ge(pv_mm, i + 1)
                            act.activation(dqk[:, h, t * P:(t + 1) * P], ps[3][:, 0:P], ACT.Copy).then_inc(pv_done, 1)
                        elif kind == "headnorm":
                            hd, = a
                            o = headnorm_order(hd)
                            src = qkv[:, hd] if hd < H else dqk[:, hd - H]
                            act.wait_ge(o_done if hd < H else pv_done, NCH if hd < H else NT * (hd - H + 1))
                            if o >= 1:
                                act.wait_ge(hn_out, o)
                            act.activation(sq[:], src, ACT.Square).then_inc(hn_sq, 1)
                            act.wait_ge(hn_mm, o + 1)
                            act.activation(acc[:], ps[5][:], ACT.Ln, scale=1.0 / P, bias=eps_c[:, 0:1])\
                               .then_inc(act_chain, 1)
                            chained()
                            act.activation(acc[:], acc[:], ACT.Exp, scale=-0.5).then_inc(hn_r, 1)
                            act.wait_ge(hn_out, o + 1)
                            act.activation(xh[:, hd], tmp_of(o), ACT.Copy).then_inc(hn_hi, 1)

                    for st in steps:
                        act_step(*st)
                    for p in range(OUT_PAIRS - 1):
                        split_static(PAIR_OUT + p + 2)
                    heads_of_x(2, ROW_G2)
                    split_static(PAIR_OUT + OUT_PAIRS + 1)
                    ffn(1)

                @block.vector
                def _(dve):
                    counter = [0]

                    def link(ins):
                        counter[0] += 1
                        ins.then_inc(dve_chain, 1)
                        dve.wait_ge(dve_chain, counter[0])

                    def split(n, slot):
                        dve.wait_ge(hi_done, n + 1)
                        dve.tensor_tensor(wl[:, slot], raw[:, slot], wh[:, slot].bitcast(F32), ALU.subtract)\
                           .then_inc(lo_done, 1)

                    def split_static(n):
                        if n < PAIRS:
                            split(n, n % 2)

                    def rest_of_x(s, gain_row, m):
                        dve.wait_ge(xh_done, KD * s + m + 1)
                        dve.scalar_tensor_tensor(xl[:, m], x[:, m], par[:, gain_row + m:gain_row + m + 1],
                                                 xh[:, m].bitcast(F32), ALU.mult, ALU.subtract).then_inc(x_chunk, 1)

                    def add_to_x(s, factor, gain_row, ready, lag=1):
                        for m in range(KD):
                            ready(m)
                            dve.scalar_tensor_tensor(x[:, m], ps[m][:], factor, x[:, m], ALU.mult, ALU.add)\
                               .then_inc(x_new, 1)
                            if gain_row is not None and m >= lag:
                                rest_of_x(s, gain_row, m - lag)
                        if gain_row is not None:
                            for m in range(KD - lag, KD):
                                rest_of_x(s, gain_row, m)

                    def up_step(f, i, n):
                        q = i + UP_PAIRS * f
                        bank = 2 * ((n - PAIR_UP[f]) % 2)
                        dve.wait_ge(pair_done, (i + PAIR_UP[f]) + 3)
                        dve.tensor_tensor(tg[:], ps[bank][:], rstd[:], ALU.mult).then_inc(tg_done, 1)
                        dve.wait_ge(h_done, q)
                        dve.tensor_tensor(tu[:], ps[bank + 1][:], rstd[:], ALU.mult).then_inc(up_evac, 1)
                        dve.wait_ge(sg_done, q + 1)
                        dve.wait_ge(up_evac, q + 1)
                        dve.tensor_tensor(tu[:], tg[:], tu[:], ALU.mult).then_inc(h_new, 1)
                        dve.wait_ge(hh_done, q + 1)
                        if isinstance(i, int):
                            hi_i, lo_i = hh[:, i], hl[:, i]
                        else:
                            hi_i, lo_i = (b[:, bass.ds(i, 1)].rearrange("p a c -> p (a c)") for b in (hh, hl))
                        dve.tensor_tensor(lo_i, tu[:], hi_i.bitcast(F32), ALU.subtract).then_inc(h_done, 1)

                    def ffn(f, s, gain_row):
                        dve.wait_ge(rstd_done, 2 * f + 1)
                        for i in range(2):
                            up_step(f, i, PAIR_UP[f] + i)
                            split_static(PAIR_UP[f] + i + 2)
                        with dve.Fori(1, UP_PAIRS // 2) as it:
                            for u in range(2):
                                n = PAIR_UP[f] + u
                                up_step(f, it * 2 + u, n)
                                split(it * 2 + (n + 2), n % 2)
                        for j in range(DOWN_PAIRS - 1):
                            split_static(PAIR_DOWN[f] + j + 2)

                        def ready(m):
                            if m < KD - 1:
                                dve.wait_ge(down_done, (KD - 1) * f + m + 1)
                            else:
                                dve.wait_ge(pair_done, 2 + PAIR_DOWN[f] + DOWN_PAIRS)

                        add_to_x(s, 0.5, gain_row, ready)

                    dve.sem_inc(lo_done, 2)
                    split_static(0)
                    for m in range(KD):
                        rest_of_x(0, ROW_G1, m)
                    split_static(1)
                    ffn(0, 1, ROW_GM)
                    split_static(PAIR_PROJ + 1)

                    def dve_step(kind, *a):
                        if kind == "proj":
                            p, j = a
                            bank = 2 * (p % 2) + j
                            if p not in (10, 11):
                                if j == 0:
                                    dve.wait_ge(half_done, p + 1)
                                else:
                                    dve.wait_ge(pair_done, 2 + PAIR_PROJ + p + 1)
                            if p < 6:
                                c = 2 * p + j
                                y = yconv[c % 2]
                                if c == 0:
                                    dve.wait_ge(rstd_done, 2)
                                    link(dve.memset(xin[:, 0:CONV_K], 0.0))
                                else:
                                    dve.wait_ge(conv_done, c)
                                ins = dve.tensor_tensor(xin[:, CONV_K:CONV_K + S], ps[bank][:], rstd[:], ALU.mult)
                                ins.then_inc(mix_evac, 1)
                                dve.wait_ge(mix_evac, c + 1)
                                if c >= 2:
                                    dve.wait_ge(silu_done, c - 1)
                                for k in range(CONV_K):
                                    tap = par[:, ROW_CONV + 12 * k + c:ROW_CONV + 12 * k + c + 1]
                                    src = xin[:, k + 1:k + 1 + S]
                                    if k == 0:
                                        ins = dve.tensor_scalar(y[:], src, tap, None, ALU.mult)
                                    else:
                                        ins = dve.scalar_tensor_tensor(y[:], src, tap, y[:], ALU.mult, ALU.add)
                                    if k < CONV_K - 1:
                                        link(ins)
                                ins.then_inc(conv_done, 1)
                            elif p < 10:
                                c = 2 * (p - 6) + j
                                dve.tensor_tensor(dqk[:, c], ps[bank][:], rstd[:], ALU.mult).then_inc(mix_evac, 1)
                            elif p >= 12:
                                c = 2 * (p - 12) + j
                                dve.tensor_tensor(gate[:, c], ps[bank][:], rstd[:], ALU.mult).then_inc(mix_evac, 1)
                            if j == 1:
                                split_static(PAIR_PROJ + p + 2)
                        elif kind == "rope":
                            c, = a
                            bank = 2 * ((6 + c // 2) % 2) + c % 2
                            dve.wait_ge(rope_mm, c + 1)
                            dve.wait_ge(rope_done, c)
                            link(dve.tensor_tensor(sq[:], ps[bank][:], angle[:, 1], ALU.mult))
                            link(dve.tensor_tensor(dqk[:, c], dqk[:, c], angle[:, 0], ALU.mult))
                            dve.tensor_tensor(dqk[:, c], dqk[:, c], sq[:], ALU.add).then_inc(rope_done, 1)
                        elif kind == "decay":
                            dve.wait_ge(ab_hi, 1)
                            dve.tensor_tensor(abl[:], abw[:], abh[:].bitcast(F32), ALU.subtract).then_inc(ab_split, 1)
                            for i in range(2):
                                link(dve.tensor_tensor(state[:, 2 * i, 0:DD], state[:, 2 * i, 0:DD],
                                                       state[:, 2 * i + 1, 0:DD], ALU.mult))
                                dve.reduce_sum(lsum[:, i:i + 1], state[:, 2 * i, 0:DD], AX.X).then_inc(lam_prod, 1)
                            dve.wait_ge(lam_exp, 1)
                            link(dve.tensor_tensor(lam[:, 2:3], lsum[:, 1:2], lsum[:, 0:1], ALU.subtract))
                            link(dve.tensor_tensor(lam[:, 2:3], lam[:, 2:3], lam[:, 0:1], ALU.subtract))
                            link(dve.tensor_tensor(dnorm[:], par[:, ROW_DIFF:ROW_DIFF + 1], lam[:, 1:2], ALU.mult))
                            dve.wait_ge(rtok_done, 1)
                            link(dve.tensor_tensor(ab[:], ps[6][:, 0:NT * 2 * H].rearrange("p (t c) -> p t c", t=NT),
                                                   rtok[:].unsqueeze(2).broadcast_to([P, NT, 2 * H]), ALU.mult))
                            alpha = ab[:, :, 0:H]
                            link(dve.tensor_tensor(alpha, alpha, hpar[:, 1, :].unsqueeze(1).broadcast_to([P, NT, H]),
                                                   ALU.add))
                            dve.scalar_tensor_tensor(gt[:], alpha, -1.0, alpha, ALU.mult, ALU.max).then_inc(spe_in, 1)
                            dve.wait_ge(spe_ln, 1)
                            link(dve.scalar_tensor_tensor(gl[:], alpha, 0.0, gt[:], ALU.max, ALU.add))
                            dve.wait_ge(spe_exp, 2)
                            dve.scalar_tensor_tensor(gl[:], gl[:], -1.0, hpar[:, 0, :].unsqueeze(1).broadcast_to([P, NT, H]),
                                                     ALU.mult, ALU.mult).then_inc(g_done, 1)
                            link(dve.tensor_scalar(beta[:], beta[:], 1.0, None, ALU.add))
                            link(dve.reciprocal(beta[:], beta[:]))
                            dve.wait_ge(gcol_exp, 3)
                            dve.tensor_tensor(ecol[:], ecol[:], beta[:], ALU.mult).then_inc(gcol_done, 1)
                        elif kind == "l2":
                            c, = a
                            dve.wait_ge(l2_r, c + 1)
                            dve.tensor_tensor(qkv[:, c], qkv[:, c], acc[:], ALU.mult).then_inc(l2_done, 1)
                        elif kind == "prep":
                            g, = a
                            for s in range(2):
                                t, o = 2 * g + s, 2 * g + s
                                dve.wait_ge(grow_mm, o + 1)
                                if o == 0:
                                    dve.wait_ge(gcol_done, 1)
                                dve.wait_ge(e_done, o + 1)
                                dve.tensor_tensor(bM[s][:], heads(4 + 2 * s), over_cols(gcol[:, t]), ALU.subtract)\
                                   .then_inc(dx_done, 1)
                                dve.wait_ge(dx_done, o + 1)
                                dve.tensor_scalar(bT[s][:], bM[s][:], 0.0, None, ALU.min).then_inc(dmin_done, 1)
                                dve.wait_ge(dmin_done, 2 * o + 1)
                                dve.tensor_scalar(bM[s][:], bM[s][:], 0.0, None, ALU.max).then_inc(dmin_done, 1)
                                dve.wait_ge(dexp_done, 2 * (o + 1))
                                link(dve.tensor_tensor(bT[s][:], bT[s][:], over_heads(mask("tri")), ALU.mult))
                                link(dve.tensor_tensor(bM[s][:], bM[s][:], over_heads(mask("suffix")), ALU.mult))
                                link(dve.tensor_tensor(bM[s][:], bM[s][:], over_cols(beta[:, t]), ALU.mult))
                                dve.wait_ge(kk_mm, o + 1)
                                link(dve.tensor_tensor(bM[s][:], heads(5 + 2 * s), bM[s][:], ALU.mult))
                                dve.wait_ge(qk_mm, o + 1)
                                dve.tensor_tensor(qkT[:, t], heads(4 + 2 * s), bT[s][:], ALU.mult).then_inc(qkT_done, 1)
                                dve.tensor_tensor(qkv[:, 0:H, t * P:(t + 1) * P], qkv[:, 0:H, t * P:(t + 1) * P],
                                                  bB[s][:], ALU.mult).then_inc(qdec_done, 1)
                                dve.tensor_copy(egl[:, t], bB[s][:, :, CH - 1:P:CH]).then_inc(qdec_done, 1)
                        elif kind == "level0":
                            g, = a
                            for s in range(2):
                                o = 2 * g + s
                                dve.wait_ge(qdec_done, 2 * (o + 1))
                                dve.wait_ge(qkT_done, o + 1)
                                link(dve.tensor_tensor(bB[s][:], bM[s][:], over_heads(mask("level0")), ALU.mult))
                                dve.tensor_tensor(bT[s][:], over_heads(mask("ident")), bB[s][:], ALU.subtract)\
                                   .then_inc(t0_done, 1)
                                dve.wait_ge(t0_done, o + 1)
                        elif kind == "level":
                            g, lv = a
                            for s in range(2):
                                o = (g * 5 + lv - 1) * 2 + s
                                if lv >= 2:
                                    dve.wait_ge(r_mm, o - 1)
                                dve.tensor_tensor(bB[s][:], bM[s][:], over_heads(mask(f"level{lv}")), ALU.mult)\
                                   .then_inc(b_done, 1)
                            for s in range(2):
                                o = (g * 5 + lv - 1) * 2 + s
                                dve.wait_ge(du_mm, o + 1)
                                if lv == 1:
                                    dve.wait_ge(u0_done, 2 * g + s + 1)
                                if lv < 5:
                                    dve.tensor_tensor(bT[s][:], bT[s][:], heads(5 + 2 * s), ALU.subtract).then_inc(tu_done, 1)
                                    dve.tensor_tensor(bU[s][:], bU[s][:], heads(4 + 2 * s), ALU.subtract).then_inc(tu_done, 1)
                                    dve.wait_ge(tu_done, g * 18 + (lv - 1) * 4 + 2 * s + 2)
                                else:
                                    dve.tensor_tensor(bU[s][:], bU[s][:], heads(4 + 2 * s), ALU.subtract).then_inc(tu_done, 1)
                        elif kind == "solved":
                            g, = a
                            for s in range(2):
                                t, o = 2 * g + s, 2 * g + s
                                dve.wait_ge(kturn, o + 1)
                                dve.tensor_tensor(bB[s][:], heads(4 + 2 * s), over_cols(ecol[:, t]), ALU.mult).then_inc(kb_done, 1)
                                dve.tensor_tensor(qkv[:, H:2 * H, t * P:(t + 1) * P], heads(4 + 2 * s),
                                                  over_cols(esuf[:, t]), ALU.mult).then_inc(kb_done, 1)
                                dve.wait_ge(vturn, o + 1)
                                dve.tensor_tensor(qkv[:, 2 * H:3 * H, t * P:(t + 1) * P], heads(5 + 2 * s),
                                                  over_cols(beta[:, t]), ALU.mult).then_inc(vb_done, 1)
                        elif kind == "scan":
                            j, = a
                            t, r = j // 2, CH * (j % 2)
                            if j == 0:
                                dve.memset(state[:], 0.0).then_inc(s_done, 1)
                            dve.wait_ge(ws_mm, j + 1)
                            if j % 2 == 0:
                                dve.wait_ge(u_done, t + 1)
                            if j >= 2:
                                dve.wait_ge(o_mm, j - 1)
                            dve.tensor_tensor(vnew[r:r + CH], qkv[r:r + CH, 2 * H:3 * H, t * P:(t + 1) * P],
                                              ps[4][r:r + CH, :].rearrange("p (h c) -> p h c", h=H), ALU.subtract)\
                               .then_inc(vnew_done, 1)
                            dve.wait_ge(sup_mm, j + 1)
                            dve.wait_ge(s_done, j + 1)
                            for h in range(H):
                                ins = dve.scalar_tensor_tensor(state[:, h], state[:, h], egl[:, t, h, j % 2:j % 2 + 1],
                                                               ps[7][:, h * P:(h + 1) * P], ALU.mult, ALU.add)
                            ins.then_inc(s_done, 1)
                        elif kind == "attend":
                            i, = a
                            h, t = divmod(i, NT)
                            n, b = (t + 1) * P, i % 2
                            dve.wait_ge(sc_mm, i + 1)
                            for s in range(2):
                                link(dve.tensor_tensor(ps[s][:, t * P:n], ps[s][:, t * P:n], mask("causal"), ALU.add))
                                link(dve.reduce_max(mx[:, b, s:s + 1], ps[s][:, 0:n], AX.X))
                            dve.tensor_scalar(mx[:, b, :], mx[:, b, :], -DD ** -0.5, None, ALU.mult).then_inc(mx_done, 1)
                            dve.wait_ge(p_done, 2 * (i + 1))
                            link(dve.reciprocal(rsum[:, b, :], ssum[:, b, :]))
                            link(dve.tensor_tensor(rsum[:, b, 1:2], rsum[:, b, 1:2], lam[:, 2:3], ALU.mult))
                            link(dve.tensor_scalar(prob[b][0][:, 0:n], prob[b][0][:, 0:n], rsum[:, b, 0:1], None, ALU.mult))
                            dve.scalar_tensor_tensor(prob[b][0][:, 0:n], prob[b][1][:, 0:n], rsum[:, b, 1:2],
                                                     prob[b][0][:, 0:n], ALU.mult, ALU.add).then_inc(a_done, 1)
                        elif kind == "headnorm":
                            hd, = a
                            o = headnorm_order(hd)
                            src = qkv[:, hd] if hd < H else dqk[:, hd - H]
                            gain = par[:, ROW_GDN:ROW_GDN + 1] if hd < H else dnorm[:, 0:1]
                            dve.wait_ge(hn_r, o + 1)
                            if hd == 0:
                                dve.wait_ge(s_done, NCH + 1)
                            if hd < H:
                                dve.wait_ge(gate_done, H)
                                link(dve.tensor_tensor(src, src, gate[:, hd], ALU.mult))
                            dve.wait_ge(hn_done, o)
                            dve.scalar_tensor_tensor(tmp_of(o), src, gain, acc[:], ALU.mult, ALU.mult).then_inc(hn_out, 1)
                            dve.wait_ge(hn_hi, o + 1)
                            dve.tensor_tensor(xl[:, hd], tmp_of(o), xh[:, hd].bitcast(F32), ALU.subtract).then_inc(hn_done, 1)

                    for st in steps:
                        dve_step(*st)
                    for p in range(OUT_PAIRS - 1):
                        split_static(PAIR_OUT + p + 2)
                    add_to_x(2, 1.0, ROW_G2,
                             lambda m: dve.wait_ge(out_done, m + 1) if m < KD - 1
                             else dve.wait_ge(pair_done, 2 + PAIR_OUT + OUT_PAIRS), lag=KD)
                    split_static(PAIR_OUT + OUT_PAIRS + 1)
                    ffn(1, 3, None)

                @block.gpsimd
                def _(pool):
                    pool.wait_ge(par_turn, 1)
                    for s in range(3):
                        if s:
                            pool.wait_ge(rstd_done, s)
                        if s == 2:
                            pool.wait_ge(hn_done, 2 * H)
                        for m in range(KD):
                            if s:
                                pool.wait_ge(x_new, KD * (s - 1) + m + 1)
                            dst = acc if m == 0 else sq
                            pool.tensor_tensor(dst[:], x[:, m], x[:, m], ALU.mult).then_inc(sq_done, 1)
                            pool.wait_ge(sq_done, KD * s + m + 1)
                            if m:
                                pool.tensor_tensor(acc[:], acc[:], sq[:], ALU.add).then_inc(acc_done, 1)
                                pool.wait_ge(acc_done, (KD - 1) * s + m)

                @block.tensor
                def _(pe):
                    def three(o, wh_t, wl_t, mh, ml, start, stop):
                        pe.matmul(o, wh_t, mh, start=start, stop=False)
                        pe.matmul(o, wh_t, ml, start=False, stop=False)
                        return pe.matmul(o, wl_t, mh, start=False, stop=stop)

                    def up_pair(f, i, n, first=False):
                        slot, bank = n % 2, 2 * ((n - PAIR_UP[f]) % 2)
                        pe.wait_ge(lo_done, (i + PAIR_UP[f]) + 3)
                        if not first and not (isinstance(i, int) and i < 2):
                            pe.wait_ge(up_evac, i + UP_PAIRS * f - 1)
                        for k in range(KD):
                            for a in range(2):
                                if first:
                                    pe.wait_ge(x_chunk, KD * 2 * f + min(max(k + 1, a + 1), KD))
                                last = three(ps[bank + a][:], wh[:, slot, KD * a + k], wl[:, slot, KD * a + k],
                                             xh[:, k], xl[:, k], k == 0, k == KD - 1)
                        last.then_inc(pair_done, 1)

                    def down_pair(f, j, n, first=False, final=False):
                        slot = n % 2
                        pe.wait_ge(lo_done, (j + PAIR_DOWN[f]) + 3)
                        pe.wait_ge(h_done, KF * f + 2 * j + 2)
                        for m in range(KD):
                            if first and m == 0:
                                pe.wait_ge(up_evac, UP_PAIRS * f + UP_PAIRS - 1)
                            if first and m == 2:
                                pe.wait_ge(up_evac, UP_PAIRS * f + UP_PAIRS)
                            for a in range(2):
                                k = 2 * j + a
                                if isinstance(j, int):
                                    mh, ml = hh[:, k], hl[:, k]
                                else:
                                    mh, ml = (b[:, bass.ds(k, 1)].rearrange("p a c -> p (a c)") for b in (hh, hl))
                                last = three(ps[m][:], wh[:, slot, KD * a + m], wl[:, slot, KD * a + m], mh, ml,
                                             first and a == 0, final and a == 1)
                            if final and m < KD - 1:
                                last.then_inc(down_done, 1)
                        last.then_inc(pair_done, 1)

                    def norm_product(s):
                        pe.wait_ge(acc_done, (KD - 1) * (s + 1))
                        pe.matmul(ps[7][:], ones[:], acc[:], start=True, stop=True).then_inc(norm_mm, 1)

                    def ffn(f):
                        up_pair(f, 0, PAIR_UP[f], first=True)
                        norm_product(2 * f)
                        up_pair(f, 1, PAIR_UP[f] + 1)
                        with pe.Fori(1, UP_PAIRS // 2) as it:
                            for u in range(2):
                                up_pair(f, it * 2 + u, PAIR_UP[f] + u)
                        down_pair(f, 0, PAIR_DOWN[f], first=True)
                        for j in range(1, DOWN_PAIRS - 1):
                            down_pair(f, j, PAIR_DOWN[f] + j)
                        down_pair(f, DOWN_PAIRS - 1, PAIR_DOWN[f] + DOWN_PAIRS - 1, final=True)

                    pe.sem_inc(pair_done, 2)
                    pe.wait_ge(par_in, 16 * 8)
                    pe.transpose(ps[0][:, 0:ROWS], acc[0:ROWS, 0:P], acc[0:ROWS, P:P + ROWS]).then_inc(par_turn, 1)
                    pe.wait_ge(par_done, 1)
                    ffn(0)

                    def pe_step(kind, *a):
                        if kind == "first":
                            n = PAIR_PROJ
                            pe.wait_ge(lo_done, n + 3)
                            ch, cl = (wt[:, n % 2].rearrange("p (k a) c -> p k (a c)", a=2) for wt in (wh, wl))
                            for k in range(KD):
                                for b in range(2):
                                    pe.wait_ge(x_chunk, KD + min(max(k + 1, b + 1), KD))
                                    last = three(ps[b][:], ch[:, k, b * P:(b + 1) * P], cl[:, k, b * P:(b + 1) * P],
                                                 xh[:, k], xl[:, k], k == 0, k == KD - 1)
                                    if k == KD - 1:
                                        last.then_inc(half_done if b == 0 else pair_done, 1)
                            norm_product(1)
                        elif kind == "proj":
                            p, j = a
                            if p == 0:
                                return
                            n = PAIR_PROJ + p
                            slot, bank = n % 2, 2 * (p % 2) + j
                            if j == 0:
                                pe.wait_ge(lo_done, n + 3)
                            q = p - 2
                            if 0 <= q < 6:
                                pe.wait_ge(mix_evac, 2 * q + j + 1)
                            elif 6 <= q < 10:
                                pe.wait_ge(rope_done, 2 * (q - 6) + j + 1)
                            elif q >= 10:
                                pe.wait_ge(v_evac, 2 * (q - 10) + j + 1)
                            ch, cl = (wt[:, slot].rearrange("p (k a) c -> p k (a c)", a=2) for wt in (wh, wl))
                            if p in (10, 11):
                                for b in range(2):
                                    tt = 2 * j + b
                                    for k in range(KD):
                                        tok = slice(tt * P, (tt + 1) * P)
                                        last = three(ps[bank][:, b * 256:(b + 1) * 256], xh[:, k, tok], xl[:, k, tok],
                                                     ch[:, k, :], cl[:, k, :], k == 0, k == KD - 1)
                            else:
                                for k in range(KD):
                                    last = three(ps[bank][:], ch[:, k, j * P:(j + 1) * P], cl[:, k, j * P:(j + 1) * P],
                                                 xh[:, k], xl[:, k], k == 0, k == KD - 1)
                            last.then_inc(half_done if j == 0 else pair_done, 1)
                        elif kind == "rope":
                            c, = a
                            bank = 2 * ((6 + c // 2) % 2) + c % 2
                            pe.wait_ge(mix_evac, 12 + c + 1)
                            pe.matmul(ps[bank][:], mask("rot"), dqk[:, c], start=True, stop=True).then_inc(rope_mm, 1)
                        elif kind == "decay":
                            for tt in range(NT):
                                pe.matmul(ps[6][:, 64 + tt:65 + tt], acc[:, tt * P:(tt + 1) * P], ones[:, 0:1],
                                          start=True, stop=True)
                            pe.wait_ge(ab_split, 1)
                            for tt in range(NT):
                                for k in range(KD):
                                    tok = slice(tt * P, (tt + 1) * P)
                                    last = three(ps[6][:, 8 * tt:8 * tt + 8], xh[:, k, tok], xl[:, k, tok], abh[:, k],
                                                 abl[:, k], k == 0, k == KD - 1)
                            last.then_inc(ab_mm, 1)
                            pe.wait_ge(g_done, 1)
                            pe.matmul(ps[6][:, 128:128 + NT * H], mask("tri"), gl[:].rearrange("p t h -> p (t h)"),
                                      start=True, stop=True)
                            pe.matmul(ps[6][:, 192:192 + NT * H], mask("suffix"), gl[:].rearrange("p t h -> p (t h)"),
                                      start=True, stop=True).then_inc(gcol_mm, 1)
                        elif kind == "l2":
                            c, = a
                            pe.wait_ge(l2_sq, c + 1)
                            if c >= 4:
                                pe.wait_ge(l2_r, c - 3)
                            if c == 0:
                                pe.wait_ge(gcol_exp, 3)
                            pe.matmul(ps[4 + c % 4][:], ones[:], sq[:], start=True, stop=True).then_inc(l2_mm, 1)
                        elif kind == "prep":
                            g, = a
                            if g == 0:
                                pe.wait_ge(l2_done, 2 * H)
                            for s in range(2):
                                t, o = 2 * g + s, 2 * g + s
                                if g:
                                    pe.wait_ge(w_done, o - 1)
                                    pe.wait_ge(u_done, o - 1)
                                for h in range(H):
                                    last = pe.matmul(ps[4 + 2 * s][:, h * P:(h + 1) * P],
                                                     gl[:, t, h:h + 1].broadcast_to([P, P]), mask("tri"),
                                                     start=True, stop=True)
                                last.then_inc(grow_mm, 1)
                                tok = slice(t * P, (t + 1) * P)
                                for h in range(H):
                                    last = pe.matmul(ps[5 + 2 * s][:, h * P:(h + 1) * P], qkv[:, H + h, tok],
                                                     qkv[:, H + h, tok], start=True, stop=True)
                                last.then_inc(kk_mm, 1)
                            for s in range(2):
                                t, o = 2 * g + s, 2 * g + s
                                tok = slice(t * P, (t + 1) * P)
                                pe.wait_ge(dx_done, o + 1)
                                for h in range(H):
                                    last = pe.matmul(ps[4 + 2 * s][:, h * P:(h + 1) * P], qkv[:, H + h, tok],
                                                     qkv[:, h, tok], start=True, stop=True)
                                last.then_inc(qk_mm, 1)
                        elif kind == "level0":
                            g, = a
                            for s in range(2):
                                o = 2 * g + s
                                pe.wait_ge(t0_done, o + 1)
                                for h in range(H):
                                    last = pe.transpose(ps[4 + 2 * s][:, h * P:(h + 1) * P], bT[s][:, h], mask("ident"))
                                last.then_inc(t0_turn, 1)
                        elif kind == "level":
                            g, lv = a
                            for s in range(2):
                                o = (g * 5 + lv - 1) * 2 + s
                                pe.wait_ge(b_done, o + 1)
                                if lv == 1:
                                    pe.wait_ge(u0_done, 2 * g + s + 1)
                                else:
                                    pe.wait_ge(tu_done, g * 18 + (lv - 2) * 4 + 2 * s + 2)
                                for h in range(H):
                                    last = pe.matmul(ps[4 + 2 * s][:, h * P:(h + 1) * P], bB[s][:, h], bU[s][:, h],
                                                     start=True, stop=True)
                                last.then_inc(r_mm, 1)
                            for s in range(2):
                                t, o = 2 * g + s, (g * 5 + lv - 1) * 2 + s
                                pe.wait_ge(r_done, o + 1)
                                if lv < 5:
                                    for h in range(H):
                                        pe.matmul(ps[5 + 2 * s][:, h * P:(h + 1) * P], wT[:, t, h], bT[s][:, h],
                                                  start=True, stop=True)
                                for h in range(H):
                                    last = pe.matmul(ps[4 + 2 * s][:, h * P:(h + 1) * P], bT[s][:, h], wT[:, t, h],
                                                     start=True, stop=True)
                                last.then_inc(du_mm, 1)
                        elif kind == "solved":
                            g, = a
                            for s in range(2):
                                t, o = 2 * g + s, 2 * g + s
                                tok = slice(t * P, (t + 1) * P)
                                pe.wait_ge(tu_done, g * 18 + 16 + s + 1)
                                for h in range(H):
                                    last = pe.transpose(ps[4 + 2 * s][:, h * P:(h + 1) * P], qkv[:, H + h, tok], mask("ident"))
                                last.then_inc(kturn, 1)
                                for h in range(H):
                                    last = pe.transpose(ps[5 + 2 * s][:, h * P:(h + 1) * P], qkv[:, 2 * H + h, tok], mask("ident"))
                                last.then_inc(vturn, 1)
                            for s in range(2):
                                t, o = 2 * g + s, 2 * g + s
                                tok = slice(t * P, (t + 1) * P)
                                pe.wait_ge(kb_done, 2 * (o + 1))
                                for h in range(H):
                                    last = pe.matmul(ps[4 + 2 * s][:, h * P:(h + 1) * P], bB[s][:, h], bU[s][:, h],
                                                     start=True, stop=True)
                                last.then_inc(w_mm, 1)
                                pe.wait_ge(vb_done, o + 1)
                                for h in range(H):
                                    last = pe.matmul(ps[5 + 2 * s][:, h * P:(h + 1) * P], bU[s][:, h], qkv[:, 2 * H + h, tok],
                                                     start=True, stop=True)
                                last.then_inc(u_mm, 1)
                        elif kind == "scan":
                            j, = a
                            t, r = j // 2, CH * (j % 2)
                            rows, cols = slice(r, r + CH), slice(j * CH, (j + 1) * CH)
                            tok = slice(t * P, (t + 1) * P)
                            if j == 0:
                                pe.wait_ge(w_done, NT)
                                pe.wait_ge(u_done, NT)
                            if j >= 1:
                                pe.wait_ge(o_done, j)
                            pe.wait_ge(s_done, j + 1)
                            for h in range(H):
                                last = pe.matmul(ps[4][rows, h * P:(h + 1) * P], wT[:, t, h, rows], state[:, h],
                                                 start=True, stop=True)
                            last.then_inc(ws_mm, 1)
                            for h in range(H):
                                pe.matmul(ps[6][:, h * CH:(h + 1) * CH], state[:, h], qkv[:, h, cols], start=h == 0,
                                          stop=False, skip_group_check=True)
                            pe.wait_ge(vnew_done, j + 1)
                            for h in range(H):
                                last = pe.matmul(ps[7][:, h * P:(h + 1) * P], qkv[rows, H + h, tok], vnew[rows, h],
                                                 start=True, stop=True)
                            last.then_inc(sup_mm, 1)
                            for h in range(H):
                                last = pe.matmul(ps[6][:, h * CH:(h + 1) * CH], vnew[rows, h], qkT[rows, t, h, rows],
                                                 start=False, stop=h == H - 1, skip_group_check=True)
                            last.then_inc(o_mm, 1)
                        elif kind == "attend":
                            i, = a

                            def scores(i):
                                h, t = divmod(i, NT)
                                if i == 0:
                                    pe.wait_ge(mix_evac, 24)
                                    pe.wait_ge(rope_done, 2 * H)
                                else:
                                    pe.wait_ge(p_done, 2 * i)
                                for s in range(2):
                                    half = slice(DD * s, DD * s + DD)
                                    last = pe.matmul(ps[s][:, 0:(t + 1) * P], dqk[half, h, t * P:(t + 1) * P],
                                                     dqk[half, H + h, 0:(t + 1) * P], start=True, stop=True)
                                last.then_inc(sc_mm, 1)

                            if i == 0:
                                scores(0)
                            if i + 1 < H * NT:
                                scores(i + 1)
                            h, t = divmod(i, NT)
                            pe.wait_ge(a_done, i + 1)
                            if i >= 1:
                                pe.wait_ge(at_done, i)
                            for k in range(t + 1):
                                last = pe.transpose(ps[2][:, k * P:(k + 1) * P], prob[i % 2][0][:, k * P:(k + 1) * P],
                                                    mask("ident"))
                            last.then_inc(at_mm, 1)
                            pe.wait_ge(at_done, i + 1)
                            if i >= 1:
                                pe.wait_ge(pv_done, i)
                            else:
                                pe.wait_ge(v_evac, 4)
                            for k in range(t + 1):
                                last = pe.matmul(ps[3][:, 0:P], V[:, k, h * P:(h + 1) * P], attT[i % 2][:, k], start=k == 0,
                                                 stop=k == t)
                            last.then_inc(pv_mm, 1)
                        elif kind == "headnorm":
                            hd, = a
                            o = headnorm_order(hd)
                            pe.wait_ge(hn_sq, o + 1)
                            pe.matmul(ps[5][:], ones[:], sq[:], start=True, stop=True).then_inc(hn_mm, 1)

                    for st in steps:
                        pe_step(*st)
                    for p in range(OUT_PAIRS):
                        n = PAIR_OUT + p
                        pe.wait_ge(lo_done, n + 3)
                        pe.wait_ge(hn_done, 2 * p + 2)
                        if p == 0:
                            pe.wait_ge(hn_done, 2 * H)
                        for m in range(KD):
                            for a in range(2):
                                k = 2 * OUT_ORDER[p] + a
                                last = three(ps[m][:], wh[:, n % 2, KD * a + m], wl[:, n % 2, KD * a + m], xh[:, k],
                                             xl[:, k], p == 0 and a == 0, p == OUT_PAIRS - 1 and a == 1)
                            if p == OUT_PAIRS - 1 and m < KD - 1:
                                last.then_inc(out_done, 1)
                        last.then_inc(pair_done, 1)
                    ffn(1)

        with nc.Fori(0, DEPTH) as l:
            body(l)
            nc.all_engine_barrier()
            for s in layer_sems:
                nc.sync.sem_clear(s)
            nc.all_engine_barrier()

        f_sq, f_acc, f_mm, f_ln, f_r, f_y, f_turn, f_kept, f_out, f_id = (
            ctx.enter_context(nc.semaphore(n)) for n in
            ("f_sq", "f_acc", "f_mm", "f_ln", "f_r", "f_y", "f_turn", "f_kept", "f_out", "f_id"))
        with nc.Block() as block:
            @block.sync
            def _(sp):
                sp.dma_start(ident0[:], masks_in[:, CONSTS.index("ident"), :]).then_inc(f_id, 16)
                for t in range(NT):
                    sp.wait_ge(f_kept, 2 * (t + 1))
                    sp.dma_start(out[t * P:(t + 1) * P, :], xstage[:, t, :]).then_inc(f_out, 16)
                sp.wait_ge(f_out, 16 * NT)

            @block.scalar
            def _(act):
                for m in range(KD):
                    if m >= 2:
                        act.wait_ge(f_acc, m - 1)
                    dst = (sq, rstd)[m % 2]
                    act.activation(dst[:], x[:, m], ACT.Square).then_inc(f_sq, 1)
                act.wait_ge(f_mm, 1)
                act.wait_ge(f_acc, KD)
                act.activation(sq[:], ps[0][:], ACT.Ln, scale=1.0 / D, bias=eps_c[:, 0:1]).then_inc(f_ln, 1)
                act.wait_ge(f_ln, 1)
                act.activation(rstd[:], sq[:], ACT.Exp, scale=-0.5).then_inc(f_r, 1)

            @block.vector
            def _(dve):
                for m in range(KD):
                    dve.wait_ge(f_sq, m + 1)
                    src = (sq, rstd)[m % 2]
                    if m == 0:
                        dve.tensor_copy(acc[:], src[:]).then_inc(f_acc, 1)
                    else:
                        dve.wait_ge(f_acc, m)
                        dve.tensor_tensor(acc[:], acc[:], src[:], ALU.add).then_inc(f_acc, 1)
                dve.wait_ge(f_r, 1)
                for m in range(KD):
                    dve.scalar_tensor_tensor(x[:, m], x[:, m], par[:, ROW_FINAL + m:ROW_FINAL + m + 1], rstd[:],
                                             ALU.mult, ALU.mult).then_inc(f_y, 1)
                for t in range(NT):
                    for q in range(2):
                        dve.wait_ge(f_turn, 2 * t + q + 1)
                        dve.tensor_copy(xstage[:, t, 4 * q * P:4 * (q + 1) * P], ps[2 * t + q][:]).then_inc(f_kept, 1)

            @block.tensor
            def _(pe):
                pe.wait_ge(f_acc, KD)
                pe.matmul(ps[0][:], ones[:], acc[:], start=True, stop=True).then_inc(f_mm, 1)
                pe.wait_ge(f_id, 16)
                pe.wait_ge(f_ln, 1)
                for t in range(NT):
                    for q in range(2):
                        pe.wait_ge(f_y, 4 * (q + 1))
                        for j in range(4):
                            last = pe.transpose(ps[2 * t + q][:, j * P:(j + 1) * P], x[:, 4 * q + j, t * P:(t + 1) * P],
                                                ident0[:])
                        last.then_inc(f_turn, 1)


_INS = ["x", "ffn1_w_gate", "ffn1_w_up", "ffn1_w_down", "w_in", "w_out", "ffn2_w_gate", "ffn2_w_up", "ffn2_w_down",
        "ffn1_norm", "mix_norm", "ffn2_norm", "final_norm", "conv_w", "a_log", "dt_bias", "gdn_norm", "diff_norm",
        "lambda_q1", "lambda_k1", "lambda_q2", "lambda_k2"]


def kernel(**inputs):
    import concourse.bacc as bacc
    from concourse.bass_utils import run_bass_kernel_spmd

    nc = bacc.Bacc("TRN2", target_bir_lowering=False, num_devices=1)
    arrays, args = {}, []
    masks, angle, lam = shape_constants()
    given = [(n, np.ascontiguousarray(inputs[n])) for n in _INS]
    given[0] = ("x", given[0][1].reshape(S, D))
    for name, a in given + [("masks", masks), ("angle", angle), ("lam", lam)]:
        arrays[f"in_{name}"] = a
        args.append(nc.dram_tensor(f"in_{name}", a.shape, mybir.dt.from_np(a.dtype), kind="ExternalInput").ap())
    args.append(nc.dram_tensor("out", [S, D], F32, kind="ExternalOutput").ap())
    build(nc, *args)
    r = run_bass_kernel_spmd(nc, [arrays], core_ids=[0])
    return r.results[0]["out"].reshape(1, S, D)
```

```python
import math
from contextlib import ExitStack

import numpy as np

import concourse.bass as bass
from concourse import mybir

F32 = mybir.dt.float32
F32R = mybir.dt.float32r
ACT = mybir.ActivationFunctionType
ALU = mybir.AluOpType
AX = mybir.AxisListType

P = 128
D = 1024
S = 512
DEPTH = 2
DFF = ((8 * D // 3 + 127) // 128) * 128
H = 4
DV = 128
CH = 64
DD = 64
EPS = 1e-6
KD = D // P
KF = DFF // P
NT = S // P
NCH = S // CH
COL_Q, COL_GATE = 0, 3 * H * P
COL_AB = COL_GATE + H * P
COL_DQ = COL_AB + 2 * H
COL_DV = COL_DQ + 2 * H * P
CONV_K = 4

UP_PAIRS = KF
DOWN_PAIRS = KF // 2
PROJ_PAIRS = 14
OUT_PAIRS = KD // 2
PAIR_UP = [0, UP_PAIRS + DOWN_PAIRS + PROJ_PAIRS + OUT_PAIRS]
PAIR_DOWN = [PAIR_UP[0] + UP_PAIRS, PAIR_UP[1] + UP_PAIRS]
PAIR_PROJ = PAIR_DOWN[0] + DOWN_PAIRS
PAIR_OUT = PAIR_PROJ + PROJ_PAIRS
PAIRS = PAIR_DOWN[1] + DOWN_PAIRS

ROW_CONV, ROW_G1, ROW_GM, ROW_G2, ROW_GDN, ROW_DIFF, ROW_FINAL = 0, 48, 56, 64, 72, 73, 74
ROWS = 82

CONV_OF = {0: 4, 1: 5, 2: 6, 3: 7, 4: 0, 5: 1, 6: 2, 7: 3, 12: 8, 13: 9, 14: 10, 15: 11}
ROPE_OF = {8: 0, 9: 1, 10: 2, 11: 3, 16: 4, 17: 5, 18: 6, 19: 7}
PROJ_COLS = [2 * P * c for c in (2, 3, 0, 1)] + [COL_DQ, COL_DQ + 2 * P, 8 * P, 10 * P] + \
            [COL_DQ + 2 * P * c for c in (2, 3, 4, 5)] + [COL_GATE, COL_GATE + 2 * P]
V_PAIR, GATE_PAIR = 10, 12
CONV_ORDER = {u: i for i, u in enumerate(CONV_OF)}
ROPE_ORDER = {u: i for i, u in enumerate(ROPE_OF)}
L2_BANKS = [4, 5, 7, 6]
SUM_BANK = 6
LN_EXP = "natural_log_exp_and_others"

CONSTS = ["ones", "ident", "tri", "suffix", "rot", "causal"] + [f"level{i}" for i in range(6)]


def shape_constants():
    i = np.arange(P)
    same = (i[:, None] // CH) == (i[None, :] // CH)
    c = {
        "ones": np.ones((P, P)),
        "ident": np.eye(P),
        "tri": same & (i[:, None] <= i[None, :]),
        "suffix": same & (i[:, None] > i[None, :]),
        "causal": np.where(i[None, :] > i[:, None], -1e30, 0.0),
    }
    rot = np.zeros((P, P))
    half = DD // 2
    for o in range(P):
        if o % DD < half:
            rot[o + half, o] = -1.0
        else:
            rot[o - half, o] = 1.0
    c["rot"] = rot
    for lv in range(6):
        b = 1 << lv
        c[f"level{lv}"] = (i[:, None] // (2 * b) == i[None, :] // (2 * b)) & (i[:, None] % (2 * b) >= b) & (i[None, :] % (2 * b) < b)
    masks = np.stack([np.asarray(c[n], np.float32) for n in CONSTS], 1)
    inv = (1.0 / (np.float32(10000.0) ** (np.arange(0, DD, 2, dtype=np.float32) / np.float32(DD)))).astype(np.float32)
    ang = (np.arange(S, dtype=np.float32)[:, None] * inv[None, :]).astype(np.float32)
    angle = np.stack([np.tile(np.cos(ang).T, (4, 1)), np.tile(np.sin(ang).T, (4, 1))], 1).astype(np.float32)
    init = [0.8 - 0.6 * math.exp(-0.3 * layer) for layer in range(DEPTH)]
    lam = np.tile(np.array([[v, 1.0 - v] for v in init], np.float32)[:, None, :], (1, P, 1))
    return masks, angle, lam


SCAN_STEPS = [0, 0] + [1] * 16


def item_of(i):
    return i % H, NT - 1 - i // H


def mixer_steps():
    steps = [("first",), ("absplit",), ("conv", 0), ("conv", 1), ("rests", 2),
             ("proj", 2, 0), ("proj", 2, 1), ("ab",),
             ("proj", 3, 0), ("l2sum", 0), ("proj", 3, 1), ("rests", 3), ("abturn",),
             ("proj", 4, 0), ("l2sum", 1), ("proj", 4, 1),
             ("proj", 5, 0), ("l2sum", 2), ("proj", 5, 1), ("rests", 4),
             ("proj", 6, 0), ("l2sum", 3), ("softplus",), ("l2norm", 0), ("proj", 6, 1),
             ("proj", 7, 0), ("logdecay",), ("proj", 7, 1), ("rests", 5), ("l2sq", 4), ("l2sq", 5),
             ("proj", 8, 0), ("decay",), ("proj", 8, 1), ("l2sum", 4), ("l2sum", 5), ("l2sq", 6), ("l2sq", 7), ("decayed",),
             ("proj", 9, 0), ("proj", 9, 1), ("l2sum", 6), ("l2sum", 7), ("rests", 6),
             ("proj", 10, 0), ("rope", 8), ("l2norm", 1), ("proj", 10, 1), ("rope", 9)]
    solve = []
    for g in range(2):
        solve += [("prep", g), ("prepqk", g), ("level0", g)]
        for lv in range(1, 6):
            solve += [("right", g, lv), ("left", g, lv)]
        solve += [("turnkv", g), ("solved", g)]
    fill = [("proj", u, half) for u in range(11, 2 * PROJ_PAIRS) for half in range(2)]
    last = [solve.pop(), solve.pop()]
    rests = []
    while fill or solve:
        late = []
        kind = solve[0][0] if solve else ""
        if solve:
            steps.append(solve.pop(0))
            steps += rests
            rests = []
        for _ in range(2 if kind in ("prep", "prepqk", "level0") else 1):
            if fill:
                f = fill.pop(0)
                if f[2] == 1 and f[1] - 1 in ROPE_OF:
                    late.append(("rope", f[1] - 1))
                steps.append(f)
                if f[2] == 1 and f[1] % 2:
                    rests.append(("rests", f[1] // 2 + 2))
        steps += late
    steps += rests
    scan = [(kind, j) for j in range(NCH) for kind in ("scan", "update")]
    ready, squared, summed, norms = [], [], [], []
    i = 0
    while i < H * NT + 3 or scan or ready or squared or summed:
        if i < H * NT + 3:
            if last:
                steps.append(last.pop())
            steps.append(("attend", i))
            if i >= 3 and (i - 3) % H == H - 1:
                ready.append(("attention", NT - 1 - (i - 3) // H))
        for _ in range(SCAN_STEPS[i] if i < len(SCAN_STEPS) else 1):
            if scan:
                steps.append(scan.pop(0))
                if steps[-1][0] == "update" and steps[-1][1] % 2:
                    ready.append(("delta", steps[-1][1] // 2))
        for o in summed[:]:
            steps.append(("normed", o))
            summed.remove(o)
        for o in squared[:]:
            steps.append(("normsum", o))
            squared.remove(o)
            summed.append(o)
        if ready:
            norms.append(ready.pop(0))
            steps.append(("normsq", len(norms) - 1))
            squared.append(len(norms) - 1)
        i += 1
    return steps, norms


def build(nc, x_in, ffn1_w_gate, ffn1_w_up, ffn1_w_down, w_in, w_out, ffn2_w_gate, ffn2_w_up, ffn2_w_down,
          params_in, a_log, dt_bias, lambda_q1, lambda_k1, lambda_q2, lambda_k2, masks_in, angle_in, lam_in, out):
    ctx = ExitStack()
    with ctx:
        top = [16512]

        def at(name, cols, dt=F32, where=None):
            n = math.prod(cols)
            place = top[0] if where is None else where[0]
            t = nc.alloc_sbuf_tensor_at(name, [P] + list(cols), dt, offset=place)
            size = -(-n * 4 // 32) * 32
            if where is None:
                top[0] += size
            else:
                where[0] += size
            return t

        def sem(name):
            s = ctx.enter_context(nc.semaphore(name))
            layer_sems.append(s)
            return s

        layer_sems = []
        x = at("x", [KD, S])
        xh = at("xh", [KD, S], F32R)
        xl = at("xl", [KD, S], F32R)
        raw = at("raw", [2, 16, P])
        wh = at("wh", [2, 16, P], F32R)
        wl = at("wl", [2, 16, P], F32R)
        rstd = at("rstd", [S])
        acc = at("acc", [S])
        sq = at("sq", [S])
        ones = at("ones", [P])
        par = at("par", [ROWS])
        eps_c = at("eps_c", [2])
        w = [top[0]]
        hh = at("hh", [KF, S], F32R, w)
        hl = at("hl", [KF, S], F32R, w)
        tg = at("tg", [S], F32, w)
        tu = at("tu", [S], F32, w)
        ffn_end = w[0]
        w = [top[0]]
        qkv = at("qkv", [3 * H, S], F32, w)
        wT = at("wT", [NT, H, P], F32, w)
        qkT = at("qkT", [NT, H, P], F32, w)
        dqk = at("dqk", [2 * H, S], F32, w)
        V = at("V", [NT, H * P], F32, w)
        gate_at = w[0]
        gate = at("gate", [H, S], F32, w)
        state_at = w[0]
        state = at("state", [H, P], F32, w)
        vnew = at("vnew", [H, P], F32, w)
        solve = [w[0]]
        bM = [at(f"bM{s}", [H, P], F32, w) for s in range(2)]
        bT = [at(f"bT{s}", [H, P], F32, w) for s in range(2)]
        bB = [at(f"bB{s}", [H, P], F32, w) for s in range(2)]
        bU = [at(f"bU{s}", [H, P], F32, w) for s in range(2)]
        mixer_end = w[0]
        early = [gate_at]
        xin = at("xin", [S + CONV_K], F32, early)
        yconv = [at(f"yconv{s}", [S], F32, early) for s in range(2)]
        assert early[0] <= state_at
        early = [solve[0]]
        abw = at("abw", [KD, 2 * H], F32, early)
        abh = at("abh", [KD, 2 * H], F32R, early)
        abl = at("abl", [KD, 2 * H], F32R, early)
        abf = at("abf", [S], F32, early)
        solve = [top[0] + (mixer_end - 8 * S * 4 - top[0])]
        prob = [at(f"prob{b}", [2, S], F32, solve) for b in range(3)]
        attT = [at(f"attT{b}", [NT, P], F32, solve) for b in range(2)]
        assert solve[0] <= mixer_end
        w = [max(ffn_end, mixer_end)]
        angle = at("angle", [2, S], F32, w)
        masks = at("masks", [len(CONSTS) - 1, P], F32, w)
        turned = at("turned", [S], F32, w)
        rtok = at("rtok", [NT], F32, w)
        ab = at("ab", [NT, 2 * H], F32, w)
        gl = at("gl", [NT, H], F32, w)
        gt = at("gt", [NT, H], F32, w)
        beta = at("beta", [NT, H], F32, w)
        gcol = at("gcol", [NT, H], F32, w)
        ecol = at("ecol", [NT, H], F32, w)
        esuf = at("esuf", [NT, H], F32, w)
        egl = at("egl", [NT, H, 2], F32, w)
        hpar = at("hpar", [2, H], F32, w)
        lam = at("lam", [4], F32, w)
        lsum = at("lsum", [2], F32, w)
        dnorm = at("dnorm", [1], F32, w)
        mx = at("mx", [3, 2], F32, w)
        ssum = at("ssum", [3, 2], F32, w)
        rsum = at("rsum", [3, 2], F32, w)
        assert w[0] <= nc.sbuf_usable_end, (w[0], nc.sbuf_usable_end)

        def mask(name):
            return masks[:, CONSTS.index(name) - 1, :]

        def over_heads(ap):
            return ap.unsqueeze(1).broadcast_to([P, H, P])

        def over_cols(ap):
            return ap.unsqueeze(2).broadcast_to([P, H, P])

        psum = ctx.enter_context(nc.psum_tensor("psum", [P, 8, S], F32))
        ps = [psum[:, i] for i in range(8)]

        def heads(bank):
            return ps[bank][:].rearrange("p (h c) -> p h c", h=H)

        xtok = hh[:, 0:8, :].bitcast(F32)

        s_in = [ctx.enter_context(nc.semaphore(f"x_loaded{t}")) for t in range(NT)]
        s_const = ctx.enter_context(nc.semaphore("const_loaded"))
        s_turn = ctx.enter_context(nc.semaphore("turned"))
        s_kept = ctx.enter_context(nc.semaphore("turned_kept"))
        s_memset = ctx.enter_context(nc.semaphore("memset_done"))
        xstage = nc.alloc_sbuf_tensor_at("xstage", [P, NT, D], F32, offset=top[0])
        ident0 = nc.alloc_sbuf_tensor_at("ident0", [P, P], F32, offset=top[0] + NT * D * 4)
        with nc.Block() as block:
            @block.sync
            def _(sp):
                sp.dma_start(ident0[:], masks_in[:, CONSTS.index("ident"), :]).then_inc(s_const, 16)
                sp.dma_start(ones[:], masks_in[:, CONSTS.index("ones"), :]).then_inc(s_const, 16)
                sp.dma_start(masks[:], masks_in[:, 1:, :]).then_inc(s_const, 16)
                sp.dma_start(angle[:], angle_in).then_inc(s_const, 16)
                for t in range(NT):
                    sp.dma_start(xstage[:, t, :], x_in[t * P:(t + 1) * P, :]).then_inc(s_in[t], 16)

            @block.tensor
            def _(pe):
                pe.wait_ge(s_const, 64)
                for t in range(NT):
                    pe.wait_ge(s_in[t], 16)
                    for q in range(2):
                        for j in range(4):
                            last = pe.transpose(ps[2 * t + q][:, j * P:(j + 1) * P],
                                                xstage[:, t, (4 * q + j) * P:(4 * q + j + 1) * P], ident0[:])
                        last.then_inc(s_turn, 1)

            @block.vector
            def _(dve):
                dve.memset(eps_c[:, 0:1], EPS).then_inc(s_memset, 1)
                dve.memset(eps_c[:, 1:2], -0.5 * math.log(P)).then_inc(s_memset, 1)
                for t in range(NT):
                    for q in range(2):
                        dve.wait_ge(s_turn, 2 * t + q + 1)
                        dve.tensor_copy(x[:, 4 * q:4 * q + 4, t * P:(t + 1) * P],
                                        ps[2 * t + q][:].rearrange("p (j c) -> p j c", j=4)).then_inc(s_kept, 1)

        raw_in = [sem(f"raw_in{s}") for s in range(2)]
        hi_done = sem("hi_done")
        lo_done = sem("lo_done")
        pair_done = sem("pair_done")
        down_done = sem("down_done")
        out_done = sem("out_done")
        half_done = sem("half_done")
        x_new = sem("x_new")
        xh_done = sem("xh_done")
        x_chunk = sem("x_chunk")
        sq_done = sem("sq_done")
        acc_done = sem("acc_done")
        norm_mm = sem("norm_mm")
        ln_done = sem("ln_done")
        rstd_done = sem("rstd_done")
        tg_done, sg_done, up_evac = sem("tg_done"), sem("sg_done"), sem("up_evac")
        h_new, hh_done, h_done = sem("h_new"), sem("hh_done"), sem("h_done")
        par_in = sem("par_in")
        mix_in = sem("mix_in")
        act_chain, dve_chain, pool_chain = sem("act_chain"), sem("dve_chain"), sem("pool_chain")
        ab_hi, ab_split, ab_mm, ab_scaled = sem("ab_hi"), sem("ab_split"), sem("ab_mm"), sem("ab_scaled")
        ab_turned, ab_by_token = sem("ab_turned"), sem("ab_by_token")
        spe_in, spe_exp, spe_ln = sem("spe_in"), sem("spe_exp"), sem("spe_ln")
        g_done, gcol_mm, gcol_exp, gcol_done = sem("g_done"), sem("gcol_mm"), sem("gcol_exp"), sem("gcol_done")
        mix_evac, v_evac = sem("mix_evac"), sem("v_evac")
        conv_done, silu_done, gate_done = sem("conv_done"), sem("silu_done"), sem("gate_done")
        rope_mm, rope_sin, rope_cos, rope_done = sem("rope_mm"), sem("rope_sin"), sem("rope_cos"), sem("rope_done")
        l2_sq, l2_mm, l2_r, l2_done = sem("l2_sq"), sem("l2_mm"), sem("l2_r"), sem("l2_done")
        grow_mm, e_done = sem("grow_mm"), sem("e_done")
        dx_done, dexp_done, sb_done = sem("dx_done"), sem("dexp_done"), sem("sb_done")
        kk_mm, qk_mm, qdec_done, egl_done = sem("kk_mm"), sem("qk_mm"), sem("qdec_done"), sem("egl_done")
        qkT_done = sem("qkT_done")
        t0_done, t0_turn, u0_done = sem("t0_done"), sem("t0_turn"), sem("u0_done")
        b_done, r_mm, r_done, du_mm, tu_done = (sem("b_done"), sem("r_mm"), sem("r_done"), sem("du_mm"),
                                                sem("tu_done"))
        kturn, vturn, kb_done, vb_done = sem("kturn"), sem("vturn"), sem("kb_done"), sem("vb_done")
        w_mm, u_mm, w_done, u_done = sem("w_mm"), sem("u_mm"), sem("w_done"), sem("u_done")
        ws_mm, vnew_done, sup_mm, s_done, o_mm, o_done = (sem("ws_mm"), sem("vnew_done"), sem("sup_mm"),
                                                          sem("s_done"), sem("o_mm"), sem("o_done"))
        sc_mm, mx_done, p_done, a_done = sem("sc_mm"), sem("mx_done"), sem("p_done"), sem("a_done")
        at_mm, at_done, pv_mm, pv_done = sem("at_mm"), sem("at_done"), sem("pv_mm"), sem("pv_done")
        hn_sq, hn_mm, hn_r, hn_out, hn_hi, hn_done = (sem("hn_sq"), sem("hn_mm"), sem("hn_r"), sem("hn_out"),
                                                      sem("hn_hi"), sem("hn_done"))
        hn_gated, hn_ln = sem("hn_gated"), sem("hn_ln")
        lam_prod, lam_exp = sem("lam_prod"), sem("lam_exp")

        steps, norms = mixer_steps()
        att_last = max(o for o, n in enumerate(norms) if n[0] == "attention")
        delta_last = max(o for o, n in enumerate(norms) if n[0] == "delta")
        out_order = [2, 3, 0, 1] if att_last < delta_last else [0, 1, 2, 3]
        MIX_PARTS = 1 + 2 + 1 + 4

        def normed(o):
            kind, t = norms[o]
            tok = slice(t * P, (t + 1) * P)
            src, first = (qkv, 0) if kind == "delta" else (dqk, H)
            return (kind, t, src[:, 0:H, tok], xh[:, first:first + H, tok], xl[:, first:first + H, tok],
                    6 if o < 2 * NT - 1 else 4, (sq, acc)[o % 2])

        def norms_before(j):
            return sum(st[0] == "normsum" for st in steps[:steps.index(("update", j))])

        def updates_before(o):
            return sum(st[0] == "update" for st in steps[:steps.index(("normsum", o))])

        def flat(ap):
            return ap.rearrange("p h c -> p (h c)")

        def wait_half(engine, u):
            if u % 2 == 0:
                engine.wait_ge(half_done, u // 2 + 1)
            else:
                engine.wait_ge(pair_done, 2 + PAIR_PROJ + u // 2 + 1)

        def body(l):
            with nc.Block() as block:
                @block.sync
                def _(sp):
                    sp.dma_start(par[:], params_in[l]).then_inc(par_in, 16)

                    def load(n, slot, parts):
                        sp.wait_ge(lo_done, n + 1)
                        for dst, src in parts:
                            sp.dma_start(dst, src).then_inc(raw_in[slot], 16)

                    def load_up(f, i, slot):
                        mats = (ffn1_w_gate, ffn1_w_up) if f == 0 else (ffn2_w_gate, ffn2_w_up)
                        load(i + PAIR_UP[f], slot, [
                            (raw[:, slot, KD * a:KD * a + KD, :],
                             m[l].rearrange("(k p) (n c) -> n p k c", p=P, c=P)[i]) for a, m in enumerate(mats)])

                    def load_rows(n, slot, m, j):
                        rows_of = m[l].rearrange("(j k p) n -> j k p n", k=2, p=P)[j]
                        load(n, slot, [
                            (raw[:, slot, KD * a:KD * a + KD, :].rearrange("p m c -> p (m c)"), rows_of[a])
                            for a in range(2)])

                    def load_cols(n, slot, mat, col):
                        src = mat[l].rearrange("(k p) n -> p k n", p=P)
                        dst = raw[:, slot, :, :].rearrange("p (k a) c -> p k (a c)", a=2)
                        load(n, slot, [(dst[:, 4 * a:4 * a + 4, :], src[:, 4 * a:4 * a + 4, col:col + 2 * P])
                                       for a in range(2)])

                    def ffn(f):
                        down = ffn1_w_down if f == 0 else ffn2_w_down
                        with sp.Fori(0, UP_PAIRS // 2) as it:
                            for u in range(2):
                                load_up(f, it * 2 + u, (PAIR_UP[f] + u) % 2)
                        with sp.Fori(0, DOWN_PAIRS // 2) as it:
                            for u in range(2):
                                load_rows(it * 2 + u + PAIR_DOWN[f], (PAIR_DOWN[f] + u) % 2, down, it * 2 + u)
                        last = PAIR_DOWN[f] + DOWN_PAIRS - 1
                        load_rows(last, last % 2, down, DOWN_PAIRS - 1)

                    ffn(0)
                    for p in range(PROJ_PAIRS):
                        load_cols(PAIR_PROJ + p, (PAIR_PROJ + p) % 2, w_in, PROJ_COLS[p])
                        if p == 1:
                            sp.wait_ge(pair_done, 2 + PAIR_PROJ)
                            sp.dma_start(abw[:], w_in[l].rearrange("(k p) n -> p k n", p=P)[:, :, COL_AB:COL_AB + 2 * H])\
                              .then_inc(mix_in, 16)
                            sp.dma_start(hpar[:, 0, :], a_log[l].unsqueeze(0).broadcast_to([P, H])).then_inc(mix_in, 16)
                            sp.dma_start(hpar[:, 1, :], dt_bias[l].unsqueeze(0).broadcast_to([P, H])).then_inc(mix_in, 16)
                            sp.dma_start(lam[:, 0:2], lam_in[l]).then_inc(mix_in, 16)
                            for i, v in enumerate((lambda_q1, lambda_k1, lambda_q2, lambda_k2)):
                                sp.dma_start(state[:, i, 0:DD], v[l].unsqueeze(0).broadcast_to([P, DD])).then_inc(mix_in, 16)
                    for p in range(OUT_PAIRS):
                        load_rows(PAIR_OUT + p, (PAIR_OUT + p) % 2, w_out, out_order[p])
                    ffn(1)

                @block.scalar
                def _(act):
                    def chained(counter=[0]):
                        counter[0] += 1
                        act.wait_ge(act_chain, counter[0])

                    def split(n, slot, k):
                        act.wait_ge(raw_in[slot], (k + 1) * 32)
                        act.wait_ge(pair_done, n + 1)
                        act.activation(wh[:, slot], raw[:, slot], ACT.Copy).then_inc(hi_done, 1)

                    def split_static(n):
                        if n < PAIRS:
                            split(n, n % 2, n // 2)

                    def heads_of_x(s, gain_row):
                        for m in range(KD):
                            if s:
                                act.wait_ge(x_new, KD * (s - 1) + m + 1)
                            if s == 2 and m == 0:
                                act.wait_ge(pair_done, 2 + PAIR_OUT + OUT_PAIRS)
                            act.activation(xh[:, m], x[:, m], ACT.Copy, scale=par[:, gain_row + m:gain_row + m + 1])\
                               .then_inc(xh_done, 1)
                            if m >= 2:
                                act.wait_ge(acc_done, (KD - 1) * s + max(m - 2, 1))
                            elif s and m == 0:
                                act.wait_ge(norm_mm, s)
                            act.activation((sq, rstd)[m % 2][:], x[:, m], ACT.Square).then_inc(sq_done, 1)
                        act.preload_act_table(ACT.Ln)

                    def norm_factor(s):
                        act.wait_ge(norm_mm, s + 1)
                        act.activation(sq[:], ps[7][:], ACT.Ln, scale=1.0 / D, bias=eps_c[:, 0:1]).then_inc(ln_done, 1)
                        act.wait_ge(ln_done, s + 1)
                        act.activation(rstd[:], sq[:], ACT.Exp, scale=-0.5).then_inc(rstd_done, 1)

                    def up_step(f, i):
                        q = i + UP_PAIRS * f
                        act.wait_ge(tg_done, q + 1)
                        act.activation(tg[:], tg[:], ACT.Silu).then_inc(sg_done, 1)
                        act.wait_ge(h_new, q + 1)
                        at_i = hh[:, i] if isinstance(i, int) else hh[:, bass.ds(i, 1)].rearrange("p a c -> p (a c)")
                        act.activation(at_i, tu[:], ACT.Copy).then_inc(hh_done, 1)

                    def ffn(f):
                        norm_factor(2 * f)
                        for i in range(2):
                            up_step(f, i)
                            split_static(PAIR_UP[f] + i + 2)
                        with act.Fori(1, UP_PAIRS // 2) as it:
                            for u in range(2):
                                n = PAIR_UP[f] + u + 2
                                up_step(f, it * 2 + u)
                                split(it * 2 + n, n % 2, it + n // 2)
                        for j in range(DOWN_PAIRS - 1):
                            split_static(PAIR_DOWN[f] + j + 2)

                    act.wait_ge(par_in, 16)
                    split_static(0)
                    heads_of_x(0, ROW_G1)
                    split_static(1)
                    ffn(0)
                    heads_of_x(1, ROW_GM)
                    split_static(PAIR_PROJ + 1)

                    def act_step(kind, *a):
                        if kind == "first":
                            norm_factor(1)
                        elif kind == "conv" or kind == "proj" and a[1] == 1:
                            u = a[0]
                            if u % 2:
                                split_static(PAIR_PROJ + u // 2 + 2)
                            if u in CONV_OF:
                                c, n = CONV_OF[u], CONV_ORDER[u]
                                act.wait_ge(conv_done, n + 1)
                                act.activation(qkv[:, c], yconv[n % 2][:], ACT.Silu).then_inc(silu_done, 1)
                                if n < H:
                                    if n == 0:
                                        act.wait_ge(rstd_done, 2)
                                    elif n == 1:
                                        act.wait_ge(norm_mm, 2)
                                    else:
                                        act.wait_ge(l2_mm, n - 1)
                                    act.wait_ge(silu_done, n + 1)
                                    act.activation((sq, acc)[n % 2][:], qkv[:, c], ACT.Square).then_inc(l2_sq, 1)
                            elif u // 2 in (V_PAIR, V_PAIR + 1):
                                j, p = u % 2, u // 2 - V_PAIR
                                wait_half(act, u)
                                for b in range(2):
                                    i = act.activation(V[:, 2 * j + b, p * 256:(p + 1) * 256],
                                                       ps[u % 4][:, b * 256:(b + 1) * 256], ACT.Copy,
                                                       scale=rtok[:, 2 * j + b:2 * j + b + 1])
                                i.then_inc(v_evac, 1)
                            elif u // 2 >= GATE_PAIR:
                                c = u - 2 * GATE_PAIR
                                act.wait_ge(mix_evac, 20 + c + 1)
                                act.activation(gate[:, c], gate[:, c], ACT.Silu).then_inc(gate_done, 1)
                        elif kind == "l2sq":
                            n, = a
                            act.wait_ge(l2_mm, n - 1)
                            act.wait_ge(silu_done, n + 1)
                            act.activation((sq, acc)[n % 2][:], qkv[:, n - H], ACT.Square).then_inc(l2_sq, 1)
                        elif kind == "absplit":
                            act.wait_ge(mix_in, 16 * MIX_PARTS)
                            act.activation(abh[:], abw[:], ACT.Copy).then_inc(ab_hi, 1)
                        elif kind == "softplus":
                            act.preload_act_table_set(LN_EXP)
                            act.wait_ge(lam_prod, 2)
                            act.activation(lsum[:], lsum[:], ACT.Exp).then_inc(lam_exp, 1)
                            act.activation(hpar[:, 0, :], hpar[:, 0, :], ACT.Exp).then_inc(spe_exp, 1)
                            act.wait_ge(spe_in, 1)
                            act.activation(gt[:], gt[:], ACT.Exp, scale=-1.0).then_inc(act_chain, 1)
                            act.activation(beta[:], ab[:, :, H:2 * H], ACT.Exp, scale=-1.0).then_inc(spe_exp, 1)
                            chained()
                            act.activation(gt[:], gt[:], ACT.Ln, bias=1.0).then_inc(spe_ln, 1)
                        elif kind == "decayed":
                            act.preload_act_table_set(LN_EXP)
                            act.wait_ge(gcol_mm, 1)
                            act.activation(ecol[:], ps[SUM_BANK][:, 128:128 + NT * H].rearrange("p (t h) -> p t h", h=H),
                                           ACT.Exp).then_inc(gcol_exp, 1)
                            act.activation(gcol[:], ps[SUM_BANK][:, 128:128 + NT * H].rearrange("p (t h) -> p t h", h=H),
                                           ACT.Copy).then_inc(gcol_exp, 1)
                            act.activation(esuf[:], ps[SUM_BANK][:, 192:192 + NT * H].rearrange("p (t h) -> p t h", h=H),
                                           ACT.Exp).then_inc(gcol_exp, 1)
                        elif kind == "l2norm":
                            act.preload_act_table_set(LN_EXP)
                            for n in range(4 * a[0], 4 * a[0] + 4):
                                bank = L2_BANKS[n % 4]
                                act.wait_ge(l2_mm, n + 1)
                                act.activation(ps[bank][:], ps[bank][:], ACT.Ln, bias=eps_c[:, 0:1]).then_inc(act_chain, 1)
                            for n in range(4 * a[0], 4 * a[0] + 4):
                                bank = L2_BANKS[n % 4]
                                chained()
                                bias = eps_c[:, 1:2] if n >= 4 else 0.0
                                act.activation(ps[bank][:], ps[bank][:], ACT.Exp, scale=-0.5, bias=bias).then_inc(l2_r, 1)
                        elif kind == "prep":
                            g, = a
                            act.preload_act_table_set(LN_EXP)
                            for s in range(2):
                                o = 2 * g + s
                                act.wait_ge(dx_done, o + 1)
                                if g:
                                    act.wait_ge(w_done, o - 1)
                                    act.wait_ge(u_done, o - 1)
                                act.activation(bU[s][:], heads(4 + 2 * s), ACT.Exp).then_inc(e_done, 1)
                            for s in range(2):
                                o = 2 * g + s
                                act.wait_ge(dx_done, o + 1)
                                act.activation(bM[s][:], bM[s][:], ACT.Abs).then_inc(act_chain, 1)
                                chained()
                                act.activation(bM[s][:], bM[s][:], ACT.Exp, scale=-1.0).then_inc(dexp_done, 1)
                        elif kind == "level0":
                            g, = a
                            for s in range(2):
                                o = 2 * g + s
                                act.wait_ge(t0_turn, o + 1)
                                act.wait_ge(qdec_done, o + 1)
                                act.wait_ge(egl_done, o + 1)
                                act.activation(bU[s][:], heads(4 + 2 * s), ACT.Copy).then_inc(u0_done, 1)
                        elif kind == "right":
                            g, lv = a
                            for s in range(2):
                                o = (g * 5 + lv - 1) * 2 + s
                                act.wait_ge(r_mm, o + 1)
                                act.activation(wT[:, 2 * g + s], heads(4 + 2 * s), ACT.Copy).then_inc(r_done, 1)
                        elif kind == "solved":
                            g, = a
                            for s in range(2):
                                t, o = 2 * g + s, 2 * g + s
                                act.wait_ge(w_mm, o + 1)
                                act.activation(wT[:, t], heads(4 + 2 * s), ACT.Copy).then_inc(w_done, 1)
                                act.wait_ge(u_mm, o + 1)
                                act.activation(qkv[:, 2 * H:3 * H, t * P:(t + 1) * P], heads(5 + 2 * s), ACT.Copy)\
                                   .then_inc(u_done, 1)
                        elif kind == "update":
                            j, = a
                            act.wait_ge(o_mm, j + 1)
                            act.activation(qkv[:, 0:H, j * CH:(j + 1) * CH],
                                           ps[6][:, 0:H * CH].rearrange("p (h c) -> p h c", h=H), ACT.Copy)\
                               .then_inc(o_done, 1)
                        elif kind == "attend":
                            i, = a
                            if i == 0:
                                act.preload_act_table_set(LN_EXP)
                            q = i - 2
                            if 0 <= q < H * NT:
                                n = (item_of(q)[1] + 1) * P
                                if q >= 2:
                                    act.wait_ge(pv_mm, q - 1)
                                act.wait_ge(at_mm, q + 1)
                                act.activation(flat(attT[q % 2][:])[:, 0:n], ps[5][:, 0:n], ACT.Copy).then_inc(at_done, 1)
                            if i < H * NT:
                                n, b = (item_of(i)[1] + 1) * P, i % 3
                                if i == 0:
                                    act.wait_ge(b_done, 20)
                                elif i == 1:
                                    act.wait_ge(tu_done, 36)
                                act.wait_ge(mx_done, i + 1)
                                for s in range(2):
                                    act.activation(prob[b][:, s, 0:n], ps[2 * (i % 2) + s][:, 0:n], ACT.Exp,
                                                   bias=mx[:, b, s:s + 1], accum_out=ssum[:, b, s:s + 1]).then_inc(p_done, 1)
                            q = i - 3
                            if q >= 0:
                                h, t = item_of(q)
                                act.wait_ge(pv_mm, q + 1)
                                act.activation(dqk[:, h, t * P:(t + 1) * P], ps[7][:, 0:P], ACT.Copy).then_inc(pv_done, 1)
                        elif kind == "normsq":
                            o, = a
                            which, t, src = normed(o)[:3]
                            if which == "delta":
                                act.wait_ge(o_done, 2 * t + 2)
                            else:
                                act.wait_ge(pv_done, H * (NT - t))
                            if o >= 2:
                                act.wait_ge(hn_out, o - 1)
                            elif o == 0:
                                act.wait_ge(l2_mm, 2 * H)
                            dst = (sq, acc)[o % 2]
                            act.activation(dst[:].rearrange("p (h c) -> p h c", h=H), src, ACT.Square).then_inc(hn_sq, 1)
                        elif kind == "normsum":
                            o, = a
                            bank, place = normed(o)[5:]
                            act.wait_ge(hn_mm, o + 1)
                            act.activation(place[:], ps[bank][:], ACT.Ln, scale=1.0 / P, bias=eps_c[:, 0:1])\
                               .then_inc(hn_ln, 1)
                            act.wait_ge(hn_ln, o + 1)
                            act.activation(place[:], place[:], ACT.Exp, scale=-0.5).then_inc(hn_r, 1)
                        elif kind == "normed":
                            o, = a
                            src, hi = normed(o)[2:4]
                            act.wait_ge(hn_out, o + 1)
                            act.activation(hi, src, ACT.Copy).then_inc(hn_hi, 1)

                    for st in steps:
                        act_step(*st)
                    for p in range(OUT_PAIRS - 1):
                        split_static(PAIR_OUT + p + 2)
                    heads_of_x(2, ROW_G2)
                    split_static(PAIR_OUT + OUT_PAIRS + 1)
                    ffn(1)

                @block.vector
                def _(dve):
                    counter = [0]

                    def link(ins):
                        counter[0] += 1
                        ins.then_inc(dve_chain, 1)
                        dve.wait_ge(dve_chain, counter[0])

                    def split(n, slot):
                        dve.wait_ge(hi_done, n + 1)
                        dve.tensor_tensor(wl[:, slot], raw[:, slot], wh[:, slot].bitcast(F32), ALU.subtract)\
                           .then_inc(lo_done, 1)

                    def split_static(n):
                        if n < PAIRS:
                            split(n, n % 2)

                    def rest_of_x(s, gain_row, m):
                        dve.wait_ge(xh_done, KD * s + m + 1)
                        dve.scalar_tensor_tensor(xl[:, m], x[:, m], par[:, gain_row + m:gain_row + m + 1],
                                                 xh[:, m].bitcast(F32), ALU.mult, ALU.subtract).then_inc(x_chunk, 1)

                    def add_to_x(s, factor, gain_row, ready, lag=1):
                        for m in range(KD):
                            ready(m)
                            dve.scalar_tensor_tensor(x[:, m], ps[m][:], factor, x[:, m], ALU.mult, ALU.add)\
                               .then_inc(x_new, 1)
                            if gain_row is not None and m >= lag:
                                rest_of_x(s, gain_row, m - lag)
                        if gain_row is not None:
                            for m in range(KD - lag, KD):
                                rest_of_x(s, gain_row, m)

                    def up_step(f, i, n):
                        q = i + UP_PAIRS * f
                        bank = 2 * ((n - PAIR_UP[f]) % 2)
                        dve.wait_ge(pair_done, (i + PAIR_UP[f]) + 3)
                        dve.tensor_tensor(tg[:], ps[bank][:], rstd[:], ALU.mult).then_inc(tg_done, 1)
                        dve.wait_ge(h_done, q)
                        dve.tensor_tensor(tu[:], ps[bank + 1][:], rstd[:], ALU.mult).then_inc(up_evac, 1)
                        dve.wait_ge(sg_done, q + 1)
                        dve.wait_ge(up_evac, q + 1)
                        dve.tensor_tensor(tu[:], tg[:], tu[:], ALU.mult).then_inc(h_new, 1)
                        dve.wait_ge(hh_done, q + 1)
                        if isinstance(i, int):
                            hi_i, lo_i = hh[:, i], hl[:, i]
                        else:
                            hi_i, lo_i = (b[:, bass.ds(i, 1)].rearrange("p a c -> p (a c)") for b in (hh, hl))
                        dve.tensor_tensor(lo_i, tu[:], hi_i.bitcast(F32), ALU.subtract).then_inc(h_done, 1)

                    def ffn(f, s, gain_row):
                        dve.wait_ge(rstd_done, 2 * f + 1)
                        for i in range(2):
                            up_step(f, i, PAIR_UP[f] + i)
                            split_static(PAIR_UP[f] + i + 2)
                        with dve.Fori(1, UP_PAIRS // 2) as it:
                            for u in range(2):
                                n = PAIR_UP[f] + u
                                up_step(f, it * 2 + u, n)
                                split(it * 2 + (n + 2), n % 2)
                        for j in range(DOWN_PAIRS - 1):
                            split_static(PAIR_DOWN[f] + j + 2)

                        def ready(m):
                            if m < KD - 1:
                                dve.wait_ge(down_done, (KD - 1) * f + m + 1)
                            else:
                                dve.wait_ge(pair_done, 2 + PAIR_DOWN[f] + DOWN_PAIRS)

                        add_to_x(s, 0.5, gain_row, ready)

                    dve.sem_inc(lo_done, 2)
                    split_static(0)
                    for m in range(KD):
                        rest_of_x(0, ROW_G1, m)
                    split_static(1)
                    ffn(0, 1, ROW_GM)
                    split_static(PAIR_PROJ + 1)

                    def dve_step(kind, *a):
                        if kind == "conv" or kind == "proj" and a[1] == 1:
                            u = a[0]
                            bank = u % 4
                            if u // 2 not in (V_PAIR, V_PAIR + 1):
                                wait_half(dve, u)
                            if u in CONV_OF:
                                c, n = CONV_OF[u], CONV_ORDER[u]
                                y = yconv[n % 2]
                                if n == 0:
                                    dve.wait_ge(rstd_done, 2)
                                    link(dve.memset(xin[:, 0:CONV_K], 0.0))
                                else:
                                    dve.wait_ge(conv_done, n)
                                dve.tensor_tensor(xin[:, CONV_K:CONV_K + S], ps[bank][:], rstd[:], ALU.mult)\
                                   .then_inc(mix_evac, 1)
                                dve.wait_ge(mix_evac, u + 1)
                                if n >= 2:
                                    dve.wait_ge(silu_done, n - 1)
                                for k in range(CONV_K):
                                    tap = par[:, ROW_CONV + 12 * k + c:ROW_CONV + 12 * k + c + 1]
                                    src = xin[:, k + 1:k + 1 + S]
                                    if k == 0:
                                        ins = dve.tensor_scalar(y[:], src, tap, None, ALU.mult)
                                    else:
                                        ins = dve.scalar_tensor_tensor(y[:], src, tap, y[:], ALU.mult, ALU.add)
                                    if k < CONV_K - 1:
                                        link(ins)
                                ins.then_inc(conv_done, 1)
                            elif u in ROPE_OF:
                                dve.scalar_tensor_tensor(dqk[:, ROPE_OF[u]], ps[bank][:], DD ** -0.5 if ROPE_OF[u] < H else 1.0,
                                                         rstd[:], ALU.mult, ALU.mult).then_inc(mix_evac, 1)
                            elif u // 2 >= GATE_PAIR:
                                if u == 2 * GATE_PAIR:
                                    dve.wait_ge(silu_done, 3 * H)
                                dve.tensor_tensor(gate[:, u - 2 * GATE_PAIR], ps[bank][:], rstd[:], ALU.mult)\
                                   .then_inc(mix_evac, 1)
                        elif kind == "rests":
                            split_static(PAIR_PROJ + a[0])
                        elif kind == "rope":
                            u, = a
                            o = ROPE_ORDER[u]
                            dve.wait_ge(rope_mm, o + 1)
                            if o:
                                dve.wait_ge(rope_done, o)
                            dve.tensor_tensor(turned[:], ps[u % 4][:], angle[:, 1], ALU.mult).then_inc(rope_sin, 1)
                        elif kind == "absplit":
                            dve.wait_ge(ab_hi, 1)
                            dve.tensor_tensor(abl[:], abw[:], abh[:].bitcast(F32), ALU.subtract).then_inc(ab_split, 1)
                            for i in range(2):
                                link(dve.tensor_tensor(state[:, 2 * i, 0:DD], state[:, 2 * i, 0:DD],
                                                       state[:, 2 * i + 1, 0:DD], ALU.mult))
                                dve.reduce_sum(lsum[:, i:i + 1], state[:, 2 * i, 0:DD], AX.X).then_inc(lam_prod, 1)
                        elif kind == "ab":
                            dve.wait_ge(ab_mm, 1)
                            dve.tensor_tensor(abf[0:2 * H, :], ps[SUM_BANK][0:2 * H, :], rstd[0:2 * H, :], ALU.mult)\
                               .then_inc(ab_scaled, 1)
                        elif kind == "abturn":
                            dve.wait_ge(ab_turned, 1)
                            by_token = ps[SUM_BANK][:, 0:16 * NT].rearrange("p (t c) -> p t c", t=NT)
                            link(dve.tensor_copy(ab[:], by_token[:, :, 0:2 * H]))
                            dve.tensor_copy(rtok[:], by_token[:, :, 2 * H]).then_inc(ab_by_token, 1)
                            alpha = ab[:, :, 0:H]
                            link(dve.tensor_tensor(alpha, alpha, hpar[:, 1, :].unsqueeze(1).broadcast_to([P, NT, H]),
                                                   ALU.add))
                            dve.scalar_tensor_tensor(gt[:], alpha, -1.0, alpha, ALU.mult, ALU.max).then_inc(spe_in, 1)
                        elif kind == "logdecay":
                            dve.wait_ge(spe_ln, 1)
                            link(dve.scalar_tensor_tensor(gl[:], ab[:, :, 0:H], 0.0, gt[:], ALU.max, ALU.add))
                            dve.wait_ge(spe_exp, 2)
                            dve.scalar_tensor_tensor(gl[:], gl[:], -1.0, hpar[:, 0, :].unsqueeze(1).broadcast_to([P, NT, H]),
                                                     ALU.mult, ALU.mult).then_inc(g_done, 1)
                            link(dve.tensor_scalar(beta[:], beta[:], 1.0, None, ALU.add))
                            dve.reciprocal(beta[:], beta[:]).then_inc(g_done, 1)
                            dve.wait_ge(lam_exp, 1)
                            link(dve.tensor_tensor(lam[:, 2:3], lsum[:, 1:2], lsum[:, 0:1], ALU.subtract))
                            link(dve.tensor_tensor(lam[:, 2:3], lam[:, 2:3], lam[:, 0:1], ALU.subtract))
                            link(dve.tensor_tensor(dnorm[:], par[:, ROW_DIFF:ROW_DIFF + 1], lam[:, 1:2], ALU.mult))
                        elif kind == "decayed":
                            dve.wait_ge(gcol_exp, 3)
                            dve.wait_ge(g_done, 2)
                            dve.tensor_tensor(ecol[:], ecol[:], beta[:], ALU.mult).then_inc(gcol_done, 1)
                        elif kind == "l2norm":
                            for n in range(4 * a[0], 4 * a[0] + 4):
                                c = n + 4 if n < 4 else n - 4
                                dve.wait_ge(l2_r, n + 1)
                                dve.tensor_tensor(qkv[:, c], qkv[:, c], ps[L2_BANKS[n % 4]][:], ALU.mult).then_inc(l2_done, 1)
                        elif kind == "prep":
                            g, = a
                            for s in range(2):
                                t, o = 2 * g + s, 2 * g + s
                                dve.wait_ge(grow_mm, o + 1)
                                if o == 0:
                                    dve.wait_ge(gcol_done, 1)
                                dve.tensor_tensor(bM[s][:], heads(4 + 2 * s), over_cols(gcol[:, t]), ALU.subtract)\
                                   .then_inc(dx_done, 1)
                        elif kind == "prepqk":
                            g, = a
                            for s in range(2):
                                t, o = 2 * g + s, 2 * g + s
                                dve.wait_ge(dexp_done, o + 1)
                                dve.tensor_tensor(bT[s][:], bM[s][:], over_heads(mask("tri")), ALU.mult)\
                                   .then_inc(dve_chain, 1)
                                counter[0] += 1
                                dve.wait_ge(sb_done, o + 1)
                                link(dve.tensor_tensor(bM[s][:], bM[s][:], wT[:, t], ALU.mult))
                                dve.wait_ge(kk_mm, o + 1)
                                link(dve.tensor_tensor(bM[s][:], heads(5 + 2 * s), bM[s][:], ALU.mult))
                                dve.wait_ge(e_done, o + 1)
                                dve.tensor_copy(egl[:, t], bU[s][:, :, CH - 1:P:CH]).then_inc(egl_done, 1)
                                dve.tensor_tensor(bB[s][:], bM[s][:], over_heads(mask("level0")), ALU.mult)\
                                   .then_inc(dve_chain, 1)
                                counter[0] += 1
                                dve.wait_ge(qk_mm, o + 1)
                                dve.tensor_tensor(qkT[:, t], heads(4 + 2 * s), bT[s][:], ALU.mult).then_inc(qkT_done, 1)
                                dve.wait_ge(qkT_done, o + 1)
                                dve.wait_ge(dve_chain, counter[0])
                                dve.tensor_tensor(bT[s][:], over_heads(mask("ident")), bB[s][:], ALU.subtract)\
                                   .then_inc(t0_done, 1)
                        elif kind == "left":
                            g, lv = a
                            for s in range(2):
                                o = (g * 5 + lv - 1) * 2 + s
                                dve.wait_ge(du_mm, o + 1)
                                if lv == 1:
                                    dve.wait_ge(u0_done, 2 * g + s + 1)
                                    dve.wait_ge(t0_done, 2 * g + s + 1)
                                else:
                                    dve.wait_ge(tu_done, g * 18 + (lv - 2) * 4 + 2 * s + 2)
                                if lv < 5:
                                    dve.tensor_tensor(bT[s][:], bT[s][:], heads(5 + 2 * s), ALU.subtract).then_inc(tu_done, 1)
                                dve.tensor_tensor(bU[s][:], bU[s][:], heads(4 + 2 * s), ALU.subtract).then_inc(tu_done, 1)
                        elif kind == "turnkv":
                            g, = a
                            for s in range(2):
                                t, o = 2 * g + s, 2 * g + s
                                dve.wait_ge(kturn, o + 1)
                                dve.tensor_tensor(bB[s][:], heads(4 + 2 * s), over_cols(ecol[:, t]), ALU.mult).then_inc(kb_done, 1)
                                dve.tensor_tensor(qkv[:, H:2 * H, t * P:(t + 1) * P], heads(4 + 2 * s),
                                                  over_cols(esuf[:, t]), ALU.mult).then_inc(kb_done, 1)
                                dve.wait_ge(vturn, o + 1)
                                dve.tensor_tensor(qkv[:, 2 * H:3 * H, t * P:(t + 1) * P], heads(5 + 2 * s),
                                                  over_cols(beta[:, t]), ALU.mult).then_inc(vb_done, 1)
                        elif kind == "scan":
                            j, = a
                            t, r = j // 2, CH * (j % 2)
                            if j == 0:
                                dve.memset(state[:], 0.0).then_inc(s_done, 1)
                            dve.wait_ge(ws_mm, j + 1)
                            if j % 2 == 0:
                                dve.wait_ge(u_done, t + 1)
                            if j >= 2:
                                dve.wait_ge(o_mm, j - 1)
                            dve.tensor_tensor(vnew[r:r + CH], qkv[r:r + CH, 2 * H:3 * H, t * P:(t + 1) * P],
                                              ps[4][r:r + CH, :].rearrange("p (h c) -> p h c", h=H), ALU.subtract)\
                               .then_inc(vnew_done, 1)
                        elif kind == "update":
                            j, = a
                            t = j // 2
                            if j == NCH - 1:
                                return
                            dve.wait_ge(sup_mm, j + 1)
                            dve.wait_ge(s_done, j + 1)
                            dve.wait_ge(o_mm, j + 1)
                            for h in range(H):
                                ins = dve.scalar_tensor_tensor(state[:, h], state[:, h], egl[:, t, h, j % 2:j % 2 + 1],
                                                               ps[4][:, h * P:(h + 1) * P], ALU.mult, ALU.add)
                            ins.then_inc(s_done, 1)
                        elif kind == "attend":
                            i, = a
                            if i < H * NT:
                                t = item_of(i)[1]
                                n, b = (t + 1) * P, i % 3
                                both = psum[:, 2 * (i % 2):2 * (i % 2) + 2, :]
                                dve.wait_ge(sc_mm, i + 1)
                                link(dve.tensor_tensor(both[:, :, t * P:n], both[:, :, t * P:n],
                                                       mask("causal").unsqueeze(1).broadcast_to([P, 2, P]), ALU.add))
                                dve.tensor_reduce(mx[:, b, :], both[:, :, 0:n], AX.X, ALU.max, negate=True)\
                                   .then_inc(mx_done, 1)
                            q = i - 1
                            if 0 <= q < H * NT:
                                n, b = (item_of(q)[1] + 1) * P, q % 3
                                dve.wait_ge(p_done, 2 * (q + 1))
                                link(dve.reciprocal(rsum[:, b, :], ssum[:, b, :]))
                                dve.tensor_tensor(rsum[:, b, 1:2], rsum[:, b, 1:2], lam[:, 2:3], ALU.mult).then_inc(dve_chain, 1)
                                counter[0] += 1
                                link(dve.tensor_scalar(prob[b][:, 0, 0:n], prob[b][:, 0, 0:n], rsum[:, b, 0:1], None, ALU.mult))
                                dve.scalar_tensor_tensor(prob[b][:, 0, 0:n], prob[b][:, 1, 0:n], rsum[:, b, 1:2],
                                                         prob[b][:, 0, 0:n], ALU.mult, ALU.add).then_inc(a_done, 1)
                        elif kind == "normed":
                            o, = a
                            which, t, src, hi, lo, _, place = normed(o)
                            gain = par[:, ROW_GDN:ROW_GDN + 1] if which == "delta" else dnorm[:, 0:1]
                            dve.wait_ge(hn_r, o + 1)
                            if which == "delta":
                                dve.wait_ge(hn_gated, t + 1)
                            dve.scalar_tensor_tensor(src, src, gain, place[:].rearrange("p (h c) -> p h c", h=H), ALU.mult,
                                                     ALU.mult).then_inc(hn_out, 1)
                            dve.wait_ge(hn_hi, o + 1)
                            dve.tensor_tensor(lo, src, hi.bitcast(F32), ALU.subtract).then_inc(hn_done, 1)

                    for st in steps:
                        dve_step(*st)
                    for p in range(OUT_PAIRS - 1):
                        split_static(PAIR_OUT + p + 2)
                    add_to_x(2, 1.0, ROW_G2,
                             lambda m: dve.wait_ge(out_done, m + 1) if m < KD - 1
                             else dve.wait_ge(pair_done, 2 + PAIR_OUT + OUT_PAIRS), lag=KD)
                    split_static(PAIR_OUT + OUT_PAIRS + 1)
                    ffn(1, 3, None)

                @block.gpsimd
                def _(pool):
                    def sums_of_squares(s):
                        if s == 2:
                            pool.wait_ge(hn_done, 2 * NT)
                        for m in range(1, KD):
                            o = KD * s + m + 1
                            pool.wait_ge(sq_done, o)
                            if m == 1:
                                pool.tensor_tensor(acc[:], sq[:], rstd[:], ALU.add).then_inc(acc_done, 1)
                            else:
                                pool.wait_ge(acc_done, (KD - 1) * s + m - 1)
                                pool.tensor_tensor(acc[:], acc[:], (sq, rstd)[m % 2][:], ALU.add).then_inc(acc_done, 1)

                    def pool_step(kind, *a):
                        if kind == "rope":
                            u, = a
                            c, o = ROPE_OF[u], ROPE_ORDER[u]
                            pool.wait_ge(rope_mm, o + 1)
                            pool.tensor_tensor(dqk[:, c], dqk[:, c], angle[:, 0], ALU.mult).then_inc(rope_cos, 1)
                            pool.wait_ge(rope_cos, o + 1)
                            pool.wait_ge(rope_sin, o + 1)
                            pool.tensor_tensor(dqk[:, c], dqk[:, c], turned[:], ALU.add).then_inc(rope_done, 1)
                        elif kind == "prep":
                            g, = a
                            for s in range(2):
                                t = 2 * g + s
                                pool.wait_ge(g_done, 2)
                                pool.tensor_tensor(wT[:, t], over_heads(mask("suffix")), over_cols(beta[:, t]), ALU.mult)\
                                    .then_inc(sb_done, 1)
                        elif kind == "prepqk":
                            g, = a
                            for s in range(2):
                                t, o = 2 * g + s, 2 * g + s
                                pool.wait_ge(qk_mm, o + 1)
                                pool.wait_ge(e_done, o + 1)
                                q_tile = qkv[:, 0:H, t * P:(t + 1) * P]
                                pool.tensor_tensor(q_tile, q_tile, bU[s][:], ALU.mult).then_inc(qdec_done, 1)
                        elif kind == "level0" or kind == "left" and a[1] < 5:
                            g, lv = a if kind == "left" else (a[0], 0)
                            for s in range(2):
                                if lv == 0:
                                    pool.wait_ge(t0_done, 2 * g + s + 1)
                                else:
                                    pool.wait_ge(r_mm, (g * 5 + lv - 1) * 2 + s + 1)
                                pool.tensor_tensor(bB[s][:], bM[s][:], over_heads(mask(f"level{lv + 1}")), ALU.mult)\
                                    .then_inc(b_done, 1)
                        elif kind == "normsum" and norms[a[0]][0] == "delta":
                            o, = a
                            _, t, src = normed(o)[:3]
                            pool.wait_ge(hn_sq, o + 1)
                            pool.wait_ge(gate_done, H)
                            pool.tensor_tensor(src, src, gate[:, :, t * P:(t + 1) * P], ALU.mult).then_inc(hn_gated, 1)
                    sums_of_squares(0)
                    sums_of_squares(1)
                    for st in steps:
                        pool_step(*st)
                    sums_of_squares(2)

                @block.tensor
                def _(pe):
                    def three(o, wh_t, wl_t, mh, ml, start, stop):
                        pe.matmul(o, wh_t, mh, start=start, stop=False)
                        pe.matmul(o, wh_t, ml, start=False, stop=False)
                        return pe.matmul(o, wl_t, mh, start=False, stop=stop)

                    def up_pair(f, i, n, first=False):
                        slot, bank = n % 2, 2 * ((n - PAIR_UP[f]) % 2)
                        pe.wait_ge(lo_done, (i + PAIR_UP[f]) + 3)
                        if not first and not (isinstance(i, int) and i < 2):
                            pe.wait_ge(up_evac, i + UP_PAIRS * f - 1)
                        for k in range(KD):
                            for a in range(2):
                                if first:
                                    pe.wait_ge(x_chunk, KD * 2 * f + min(max(k + 1, a + 1), KD))
                                last = three(ps[bank + a][:], wh[:, slot, KD * a + k], wl[:, slot, KD * a + k],
                                             xh[:, k], xl[:, k], k == 0, k == KD - 1)
                        last.then_inc(pair_done, 1)

                    def down_pair(f, j, n, first=False, final=False):
                        slot = n % 2
                        pe.wait_ge(lo_done, (j + PAIR_DOWN[f]) + 3)
                        pe.wait_ge(h_done, KF * f + 2 * j + 2)
                        for m in range(KD):
                            if first and m == 0:
                                pe.wait_ge(up_evac, UP_PAIRS * f + UP_PAIRS - 1)
                            if first and m == 2:
                                pe.wait_ge(up_evac, UP_PAIRS * f + UP_PAIRS)
                            for a in range(2):
                                k = 2 * j + a
                                if isinstance(j, int):
                                    mh, ml = hh[:, k], hl[:, k]
                                else:
                                    mh, ml = (b[:, bass.ds(k, 1)].rearrange("p a c -> p (a c)") for b in (hh, hl))
                                last = three(ps[m][:], wh[:, slot, KD * a + m], wl[:, slot, KD * a + m], mh, ml,
                                             first and a == 0, final and a == 1)
                            if final and m < KD - 1:
                                last.then_inc(down_done, 1)
                        last.then_inc(pair_done, 1)

                    def norm_product(s):
                        pe.wait_ge(acc_done, (KD - 1) * (s + 1))
                        pe.matmul(ps[7][:], ones[:], acc[:], start=True, stop=True).then_inc(norm_mm, 1)

                    def ffn(f):
                        up_pair(f, 0, PAIR_UP[f], first=True)
                        norm_product(2 * f)
                        up_pair(f, 1, PAIR_UP[f] + 1)
                        with pe.Fori(1, UP_PAIRS // 2) as it:
                            for u in range(2):
                                up_pair(f, it * 2 + u, PAIR_UP[f] + u)
                        down_pair(f, 0, PAIR_DOWN[f], first=True)
                        for j in range(1, DOWN_PAIRS - 1):
                            down_pair(f, j, PAIR_DOWN[f] + j)
                        down_pair(f, DOWN_PAIRS - 1, PAIR_DOWN[f] + DOWN_PAIRS - 1, final=True)

                    pe.sem_inc(pair_done, 2)
                    ffn(0)

                    def pe_step(kind, *a):
                        if kind == "first":
                            n = PAIR_PROJ
                            pe.wait_ge(lo_done, n + 3)
                            ch, cl = (wt[:, n % 2].rearrange("p (k a) c -> p k (a c)", a=2) for wt in (wh, wl))
                            for k in range(KD):
                                for b in range(2):
                                    pe.wait_ge(x_chunk, KD + min(max(k + 1, b + 1), KD))
                                    last = three(ps[b][:], ch[:, k, b * P:(b + 1) * P], cl[:, k, b * P:(b + 1) * P],
                                                 xh[:, k], xl[:, k], k == 0, k == KD - 1)
                                    if k == KD - 1:
                                        last.then_inc(half_done if b == 0 else pair_done, 1)
                            norm_product(1)
                        elif kind == "proj":
                            u, part = a
                            p, j = divmod(u, 2)
                            n = PAIR_PROJ + p
                            slot, bank = n % 2, u % 4
                            if j == 0 and part == 0:
                                pe.wait_ge(lo_done, n + 3)
                            if part == 0 and u >= 4:
                                q = u - 4
                                if q in ROPE_OF:
                                    pe.wait_ge(rope_sin, ROPE_ORDER[q] + 1)
                                elif q // 2 in (V_PAIR, V_PAIR + 1):
                                    pe.wait_ge(v_evac, q - 2 * V_PAIR + 1)
                                else:
                                    pe.wait_ge(mix_evac, q + 1)
                            ch, cl = (wt[:, slot].rearrange("p (k a) c -> p k (a c)", a=2) for wt in (wh, wl))
                            if p in (V_PAIR, V_PAIR + 1):
                                tok = slice((2 * j + part) * P, (2 * j + part + 1) * P)
                                for k in range(KD):
                                    last = three(ps[bank][:, part * 256:(part + 1) * 256], xh[:, k, tok], xl[:, k, tok],
                                                 ch[:, k, :], cl[:, k, :], k == 0, k == KD - 1)
                            else:
                                for k in range(4 * part, 4 * part + 4):
                                    last = three(ps[bank][:], ch[:, k, j * P:(j + 1) * P], cl[:, k, j * P:(j + 1) * P],
                                                 xh[:, k], xl[:, k], k == 0, k == KD - 1)
                            if part == 1:
                                last.then_inc(half_done if j == 0 else pair_done, 1)
                        elif kind == "rope":
                            u, = a
                            pe.wait_ge(mix_evac, u + 1)
                            pe.matmul(ps[u % 4][:], mask("rot"), dqk[:, ROPE_OF[u]], start=True, stop=True)\
                              .then_inc(rope_mm, 1)
                        elif kind == "ab":
                            pe.wait_ge(ab_split, 1)
                            for k in range(KD):
                                last = three(ps[SUM_BANK][0:2 * H, :], abh[:, k], abl[:, k], xh[:, k], xl[:, k], k == 0,
                                             k == KD - 1)
                            last.then_inc(ab_mm, 1)
                        elif kind == "abturn":
                            pe.wait_ge(ab_scaled, 1)
                            ident = mask("ident")
                            for t in range(NT):
                                tok = slice(t * P, (t + 1) * P)
                                pe.transpose(ps[SUM_BANK][:, 16 * t:16 * t + 2 * H], abf[0:2 * H, tok], ident[0:2 * H, 0:2 * H])
                                last = pe.transpose(ps[SUM_BANK][:, 16 * t + 2 * H:16 * t + 2 * H + 1], rstd[0:1, tok],
                                                    ident[0:1, 0:1])
                            last.then_inc(ab_turned, 1)
                        elif kind == "decay":
                            pe.wait_ge(g_done, 1)
                            pe.wait_ge(l2_done, 4)
                            pe.matmul(ps[SUM_BANK][:, 128:128 + NT * H], mask("tri"), gl[:].rearrange("p t h -> p (t h)"),
                                      start=True, stop=True)
                            pe.matmul(ps[SUM_BANK][:, 192:192 + NT * H], mask("suffix"), gl[:].rearrange("p t h -> p (t h)"),
                                      start=True, stop=True).then_inc(gcol_mm, 1)
                        elif kind == "l2sum":
                            n, = a
                            pe.wait_ge(l2_sq, n + 1)
                            if n >= 4:
                                pe.wait_ge(l2_done, n - 3)
                            if n == 2:
                                pe.wait_ge(rstd_done, 2)
                            if n == 3:
                                pe.wait_ge(ab_by_token, 1)
                            if n == 7:
                                pe.wait_ge(gcol_exp, 3)
                            pe.matmul(ps[L2_BANKS[n % 4]][:], ones[:], (sq, acc)[n % 2][:], start=True, stop=True)\
                              .then_inc(l2_mm, 1)
                        elif kind == "prep":
                            g, = a
                            if g == 0:
                                pe.wait_ge(l2_done, 2 * H)
                            for s in range(2):
                                t, o = 2 * g + s, 2 * g + s
                                if g:
                                    pe.wait_ge(w_done, o - 1)
                                    pe.wait_ge(u_done, o - 1)
                                for h in range(H):
                                    last = pe.matmul(ps[4 + 2 * s][:, h * P:(h + 1) * P],
                                                     gl[:, t, h:h + 1].broadcast_to([P, P]), mask("tri"),
                                                     start=True, stop=True)
                                last.then_inc(grow_mm, 1)
                                tok = slice(t * P, (t + 1) * P)
                                for h in range(H):
                                    last = pe.matmul(ps[5 + 2 * s][:, h * P:(h + 1) * P], qkv[:, H + h, tok],
                                                     qkv[:, H + h, tok], start=True, stop=True)
                                last.then_inc(kk_mm, 1)
                        elif kind == "prepqk":
                            g, = a
                            for s in range(2):
                                o = 2 * g + s
                                tok = slice(o * P, (o + 1) * P)
                                pe.wait_ge(dx_done, o + 1)
                                pe.wait_ge(e_done, o + 1)
                                for h in range(H):
                                    last = pe.matmul(ps[4 + 2 * s][:, h * P:(h + 1) * P], qkv[:, H + h, tok],
                                                     qkv[:, h, tok], start=True, stop=True)
                                last.then_inc(qk_mm, 1)
                        elif kind == "level0":
                            g, = a
                            for s in range(2):
                                o = 2 * g + s
                                pe.wait_ge(t0_done, o + 1)
                                for h in range(H):
                                    last = pe.transpose(ps[4 + 2 * s][:, h * P:(h + 1) * P], bT[s][:, h], mask("ident"))
                                last.then_inc(t0_turn, 1)
                        elif kind == "right":
                            g, lv = a
                            for s in range(2):
                                o = (g * 5 + lv - 1) * 2 + s
                                pe.wait_ge(b_done, o + 1)
                                if lv == 1:
                                    pe.wait_ge(u0_done, 2 * g + s + 1)
                                else:
                                    pe.wait_ge(tu_done, g * 18 + (lv - 2) * 4 + 2 * s + 2)
                                for h in range(H):
                                    last = pe.matmul(ps[4 + 2 * s][:, h * P:(h + 1) * P], bB[s][:, h], bU[s][:, h],
                                                     start=True, stop=True)
                                last.then_inc(r_mm, 1)
                        elif kind == "left":
                            g, lv = a
                            for s in range(2):
                                t, o = 2 * g + s, (g * 5 + lv - 1) * 2 + s
                                pe.wait_ge(r_done, o + 1)
                                if lv < 5:
                                    for h in range(H):
                                        pe.matmul(ps[5 + 2 * s][:, h * P:(h + 1) * P], wT[:, t, h], bT[s][:, h],
                                                  start=True, stop=True)
                                for h in range(H):
                                    last = pe.matmul(ps[4 + 2 * s][:, h * P:(h + 1) * P], bT[s][:, h], wT[:, t, h],
                                                     start=True, stop=True)
                                last.then_inc(du_mm, 1)
                        elif kind == "turnkv":
                            g, = a
                            if g == 0:
                                pe.wait_ge(silu_done, 3 * H)
                            for s in range(2):
                                o = 2 * g + s
                                tok = slice(o * P, (o + 1) * P)
                                pe.wait_ge(tu_done, g * 18 + 16 + s + 1)
                                for h in range(H):
                                    last = pe.transpose(ps[4 + 2 * s][:, h * P:(h + 1) * P], qkv[:, H + h, tok], mask("ident"))
                                last.then_inc(kturn, 1)
                                for h in range(H):
                                    last = pe.transpose(ps[5 + 2 * s][:, h * P:(h + 1) * P], qkv[:, 2 * H + h, tok], mask("ident"))
                                last.then_inc(vturn, 1)
                        elif kind == "solved":
                            g, = a
                            for s in range(2):
                                o = 2 * g + s
                                tok = slice(o * P, (o + 1) * P)
                                pe.wait_ge(kb_done, 2 * (o + 1))
                                for h in range(H):
                                    last = pe.matmul(ps[4 + 2 * s][:, h * P:(h + 1) * P], bB[s][:, h], bU[s][:, h],
                                                     start=True, stop=True)
                                last.then_inc(w_mm, 1)
                                pe.wait_ge(vb_done, o + 1)
                                for h in range(H):
                                    last = pe.matmul(ps[5 + 2 * s][:, h * P:(h + 1) * P], bU[s][:, h], qkv[:, 2 * H + h, tok],
                                                     start=True, stop=True)
                                last.then_inc(u_mm, 1)
                        elif kind == "scan":
                            j, = a
                            t, r = j // 2, CH * (j % 2)
                            rows = slice(r, r + CH)
                            if j == 0:
                                pe.wait_ge(w_done, NT)
                                pe.wait_ge(u_done, NT)
                            pe.wait_ge(s_done, j + 1)
                            for h in range(H):
                                last = pe.matmul(ps[4][rows, h * P:(h + 1) * P], wT[:, t, h, rows], state[:, h],
                                                 start=True, stop=True)
                            last.then_inc(ws_mm, 1)
                        elif kind == "update":
                            j, = a
                            t, r = j // 2, CH * (j % 2)
                            rows, cols = slice(r, r + CH), slice(j * CH, (j + 1) * CH)
                            tok = slice(t * P, (t + 1) * P)
                            if j >= 1:
                                pe.wait_ge(o_done, j)
                            if norms_before(j):
                                pe.wait_ge(hn_ln, norms_before(j))
                            pe.wait_ge(vnew_done, j + 1)
                            for h in range(H):
                                pe.matmul(ps[6][:, h * CH:(h + 1) * CH], state[:, h], qkv[:, h, cols], start=True, stop=False)
                                last = pe.matmul(ps[6][:, h * CH:(h + 1) * CH], vnew[rows, h], qkT[rows, t, h, rows],
                                                 start=False, stop=True)
                            last.then_inc(o_mm, 1)
                            for h in range(H if j < NCH - 1 else 0):
                                last = pe.matmul(ps[4][:, h * P:(h + 1) * P], qkv[rows, H + h, tok], vnew[rows, h],
                                                 start=True, stop=True)
                            if j < NCH - 1:
                                last.then_inc(sup_mm, 1)
                        elif kind == "attend":
                            i, = a
                            if i < H * NT:
                                h, t = item_of(i)
                                if i == 0:
                                    pe.wait_ge(mix_evac, 24)
                                    pe.wait_ge(rope_done, 2 * H)
                                elif i >= 2:
                                    pe.wait_ge(p_done, 2 * (i - 1))
                                for s in range(2):
                                    half = slice(DD * s, DD * s + DD)
                                    last = pe.matmul(ps[2 * (i % 2) + s][:, 0:(t + 1) * P], dqk[half, h, t * P:(t + 1) * P],
                                                     dqk[half, H + h, 0:(t + 1) * P], start=True, stop=True)
                                last.then_inc(sc_mm, 1)
                            q = i - 2
                            if 0 <= q < H * NT:
                                t = item_of(q)[1]
                                pe.wait_ge(a_done, q + 1)
                                if q >= 1:
                                    pe.wait_ge(at_done, q)
                                else:
                                    pe.wait_ge(u_done, NT)
                                for k in range(t + 1):
                                    last = pe.transpose(ps[5][:, k * P:(k + 1) * P], prob[q % 3][:, 0, k * P:(k + 1) * P],
                                                        mask("ident"))
                                last.then_inc(at_mm, 1)
                            q = i - 3
                            if q >= 0:
                                h, t = item_of(q)
                                pe.wait_ge(at_done, q + 1)
                                if q:
                                    pe.wait_ge(pv_done, q)
                                else:
                                    pe.wait_ge(v_evac, 4)
                                for k in range(t + 1):
                                    last = pe.matmul(ps[7][:, 0:P],
                                                     V[:, k, h * P:(h + 1) * P], attT[q % 2][:, k], start=k == 0, stop=k == t)
                                last.then_inc(pv_mm, 1)
                        elif kind == "normsum":
                            o, = a
                            pe.wait_ge(hn_sq, o + 1)
                            if o == 2 * NT - 1:
                                pe.wait_ge(vnew_done, NCH)
                            else:
                                if updates_before(o):
                                    pe.wait_ge(o_done, updates_before(o))
                                if o:
                                    pe.wait_ge(hn_ln, o)
                            pe.matmul(ps[normed(o)[5]][:], ones[:], (sq, acc)[o % 2][:], start=True, stop=True)\
                              .then_inc(hn_mm, 1)

                    for st in steps:
                        pe_step(*st)
                    for p in range(OUT_PAIRS):
                        n = PAIR_OUT + p
                        pe.wait_ge(lo_done, n + 3)
                        pe.wait_ge(hn_done, (min(att_last, delta_last) if p < 2 else 2 * NT - 1) + 1)
                        for m in range(KD):
                            if p == 0 and m == 4:
                                pe.wait_ge(hn_ln, 2 * NT)
                            for a in range(2):
                                k = 2 * out_order[p] + a
                                last = three(ps[m][:], wh[:, n % 2, KD * a + m], wl[:, n % 2, KD * a + m], xh[:, k],
                                             xl[:, k], p == 0 and a == 0, p == OUT_PAIRS - 1 and a == 1)
                            if p == OUT_PAIRS - 1 and m < KD - 1:
                                last.then_inc(out_done, 1)
                        last.then_inc(pair_done, 1)
                    ffn(1)

        with nc.Fori(0, DEPTH) as l:
            body(l)
            nc.all_engine_barrier()
            engines = (nc.sync, nc.scalar, nc.vector, nc.gpsimd, nc.tensor)
            for i, s in enumerate(layer_sems):
                engines[i % len(engines)].sem_clear(s)
            nc.all_engine_barrier()

        f_sq, f_acc, f_mm, f_ln, f_r, f_y, f_turn, f_kept, f_out, f_id = (
            ctx.enter_context(nc.semaphore(n)) for n in
            ("f_sq", "f_acc", "f_mm", "f_ln", "f_r", "f_y", "f_turn", "f_kept", "f_out", "f_id"))
        with nc.Block() as block:
            @block.sync
            def _(sp):
                sp.dma_start(ident0[:], masks_in[:, CONSTS.index("ident"), :]).then_inc(f_id, 16)
                for t in range(NT):
                    sp.wait_ge(f_kept, 2 * (t + 1))
                    sp.dma_start(out[t * P:(t + 1) * P, :], xstage[:, t, :]).then_inc(f_out, 16)
                sp.wait_ge(f_out, 16 * NT)

            @block.scalar
            def _(act):
                for m in range(KD):
                    if m >= 2:
                        act.wait_ge(f_acc, m - 1)
                    dst = (sq, rstd)[m % 2]
                    act.activation(dst[:], x[:, m], ACT.Square).then_inc(f_sq, 1)
                act.wait_ge(f_mm, 1)
                act.wait_ge(f_acc, KD)
                act.activation(sq[:], ps[0][:], ACT.Ln, scale=1.0 / D, bias=eps_c[:, 0:1]).then_inc(f_ln, 1)
                act.wait_ge(f_ln, 1)
                act.activation(rstd[:], sq[:], ACT.Exp, scale=-0.5).then_inc(f_r, 1)

            @block.vector
            def _(dve):
                for m in range(KD):
                    dve.wait_ge(f_sq, m + 1)
                    src = (sq, rstd)[m % 2]
                    if m == 0:
                        dve.tensor_copy(acc[:], src[:]).then_inc(f_acc, 1)
                    else:
                        dve.wait_ge(f_acc, m)
                        dve.tensor_tensor(acc[:], acc[:], src[:], ALU.add).then_inc(f_acc, 1)
                dve.wait_ge(f_r, 1)
                for m in range(KD):
                    dve.scalar_tensor_tensor(x[:, m], x[:, m], par[:, ROW_FINAL + m:ROW_FINAL + m + 1], rstd[:],
                                             ALU.mult, ALU.mult).then_inc(f_y, 1)
                for t in range(NT):
                    for q in range(2):
                        dve.wait_ge(f_turn, 2 * t + q + 1)
                        dve.tensor_copy(xstage[:, t, 4 * q * P:4 * (q + 1) * P], ps[2 * t + q][:]).then_inc(f_kept, 1)

            @block.tensor
            def _(pe):
                pe.wait_ge(f_acc, KD)
                pe.matmul(ps[0][:], ones[:], acc[:], start=True, stop=True).then_inc(f_mm, 1)
                pe.wait_ge(f_id, 16)
                pe.wait_ge(f_ln, 1)
                for t in range(NT):
                    for q in range(2):
                        pe.wait_ge(f_y, 4 * (q + 1))
                        for j in range(4):
                            last = pe.transpose(ps[2 * t + q][:, j * P:(j + 1) * P], x[:, 4 * q + j, t * P:(t + 1) * P],
                                                ident0[:])
                        last.then_inc(f_turn, 1)


_INS = ["x", "ffn1_w_gate", "ffn1_w_up", "ffn1_w_down", "w_in", "w_out", "ffn2_w_gate", "ffn2_w_up", "ffn2_w_down"]
_SMALL = ["a_log", "dt_bias", "lambda_q1", "lambda_k1", "lambda_q2", "lambda_k2"]


def params_of(inputs):
    cols = [inputs["conv_w"], inputs["ffn1_norm"], inputs["mix_norm"], inputs["ffn2_norm"], inputs["gdn_norm"],
            inputs["diff_norm"], np.broadcast_to(inputs["final_norm"], (DEPTH, D))]
    rows = np.concatenate([np.asarray(c).reshape(DEPTH, -1, P) for c in cols], 1)
    return np.ascontiguousarray(rows.transpose(0, 2, 1))


def kernel(**inputs):
    import concourse.bacc as bacc
    from concourse.bass_utils import run_bass_kernel_spmd

    nc = bacc.Bacc("TRN2", target_bir_lowering=False, num_devices=1)
    arrays, args = {}, []
    masks, angle, lam = shape_constants()
    given = [(n, np.ascontiguousarray(inputs[n])) for n in _INS]
    given[0] = ("x", given[0][1].reshape(S, D))
    given += [("params", params_of(inputs))] + [(n, np.ascontiguousarray(inputs[n])) for n in _SMALL]
    for name, a in given + [("masks", masks), ("angle", angle), ("lam", lam)]:
        arrays[f"in_{name}"] = a
        args.append(nc.dram_tensor(f"in_{name}", a.shape, mybir.dt.from_np(a.dtype), kind="ExternalInput").ap())
    args.append(nc.dram_tensor("out", [S, D], F32, kind="ExternalOutput").ap())
    build(nc, *args)
    r = run_bass_kernel_spmd(nc, [arrays], core_ids=[0])
    return r.results[0]["out"].reshape(1, S, D)
```

```python
import math
from contextlib import ExitStack

import numpy as np

import concourse.bass as bass
from concourse import mybir

F32 = mybir.dt.float32
F32R = mybir.dt.float32r
ACT = mybir.ActivationFunctionType
ALU = mybir.AluOpType
AX = mybir.AxisListType

P = 128
D = 1024
S = 512
DEPTH = 2
DFF = ((8 * D // 3 + 127) // 128) * 128
H = 4
CH = 64
DD = 64
EPS = 1e-6
KD = D // P
KF = DFF // P
NT = S // P
NCH = S // CH
COL_GATE = 3 * H * P
COL_AB = COL_GATE + H * P
COL_DQ = COL_AB + 2 * H
CONV_K = 4

UP_PAIRS = KF
DOWN_PAIRS = KF // 2
PROJ_PAIRS = 14
OUT_PAIRS = KD // 2
PAIR_UP = [0, UP_PAIRS + DOWN_PAIRS + PROJ_PAIRS + OUT_PAIRS]
PAIR_DOWN = [PAIR_UP[0] + UP_PAIRS, PAIR_UP[1] + UP_PAIRS]
PAIR_PROJ = PAIR_DOWN[0] + DOWN_PAIRS
PAIR_OUT = PAIR_PROJ + PROJ_PAIRS
PAIRS = PAIR_DOWN[1] + DOWN_PAIRS

ROW_CONV, ROW_G1, ROW_GM, ROW_G2, ROW_GDN, ROW_DIFF, ROW_FINAL = 0, 48, 56, 64, 72, 73, 74
ROWS = 82

CONV_OF = {0: 4, 1: 5, 2: 6, 3: 7, 4: 0, 5: 1, 6: 2, 7: 3, 14: 8, 15: 9, 16: 10, 17: 11}
ROPE_OF = {8: 0, 9: 1, 10: 2, 11: 3, 12: 4, 13: 5, 18: 6, 19: 7}
PROJ_COLS = [2 * P * c for c in (2, 3, 0, 1)] + [COL_DQ + 2 * P * c for c in (0, 1, 2)] + [8 * P, 10 * P] + \
            [COL_DQ + 2 * P * c for c in (3, 4, 5)] + [COL_GATE, COL_GATE + 2 * P]
V_PAIR, GATE_PAIR = 10, 12
CONV_ORDER = {u: i for i, u in enumerate(CONV_OF)}
ROPE_ORDER = {u: i for i, u in enumerate(ROPE_OF)}
L2_BANKS = [4, 5, 7, 6]
SUM_BANK = 6
SWAP_LAG = 4
LN_EXP = "natural_log_exp_and_others"

CONSTS = ["ones", "ident", "tri", "suffix", "causal"] + [f"level{i}" for i in range(6)]


def shape_constants():
    i = np.arange(P)
    same = (i[:, None] // CH) == (i[None, :] // CH)
    c = {
        "ones": np.ones((P, P)),
        "ident": np.eye(P),
        "tri": same & (i[:, None] <= i[None, :]),
        "suffix": same & (i[:, None] > i[None, :]),
        "causal": np.where(i[None, :] > i[:, None], -1e30, 0.0),
    }
    for lv in range(6):
        b = 1 << lv
        c[f"level{lv}"] = (i[:, None] // (2 * b) == i[None, :] // (2 * b)) & (i[:, None] % (2 * b) >= b) & (i[None, :] % (2 * b) < b)
    masks = np.stack([np.asarray(c[n], np.float32) for n in CONSTS], 1)
    inv = (1.0 / (np.float32(10000.0) ** (np.arange(0, DD, 2, dtype=np.float32) / np.float32(DD)))).astype(np.float32)
    ang = (np.arange(S, dtype=np.float32)[:, None] * inv[None, :]).astype(np.float32)
    angle = np.stack([np.tile(np.cos(ang).T, (4, 1)), np.tile(np.concatenate([-np.sin(ang).T, np.sin(ang).T]), (2, 1))],
                     1).astype(np.float32)
    init = [0.8 - 0.6 * math.exp(-0.3 * layer) for layer in range(DEPTH)]
    lam = np.tile(np.array([[v, 1.0 - v] for v in init], np.float32)[:, None, :], (1, P, 1))
    return masks, angle, lam


SCAN_STEPS = [0, 0] + [1] * 16


TILES = [2] * H + [3] * H + [1] * H + [0] * H


def item_of(i):
    return TILES[:i].count(TILES[i]), TILES[i]


def tile_end(t):
    return len(TILES) - TILES[::-1].index(t)


def mixer_steps():
    steps = [("first",), ("absplit",), ("conv", 0), ("heads", 2), ("conv", 1), ("rests", 2),
             ("proj", 2, 0), ("proj", 2, 1), ("ab",),
             ("proj", 3, 0), ("l2sum", 0), ("heads", 3), ("proj", 3, 1), ("rests", 3), ("abturn",),
             ("proj", 4, 0), ("l2sum", 1), ("proj", 4, 1),
             ("proj", 5, 0), ("l2sum", 2), ("heads", 4), ("proj", 5, 1), ("rests", 4),
             ("proj", 6, 0), ("l2sum", 3), ("softplus",), ("l2norm", 0), ("l2sq", 4), ("l2sq", 5), ("proj", 6, 1),
             ("proj", 7, 0), ("logdecay",), ("heads", 5), ("proj", 7, 1), ("rests", 5),
             ("proj", 8, 0), ("l2sum", 4), ("l2sum", 5), ("l2sq", 6), ("l2sq", 7),
             ("proj", 8, 1), ("decay",), ("decayed",),
             ("proj", 9, 0), ("l2sum", 6), ("heads", 6), ("proj", 9, 1), ("l2sum", 7), ("rests", 6),
             ("proj", 10, 0), ("rope", 8), ("l2norm", 1), ("proj", 10, 1)]
    solve = []
    for g in range(2):
        solve += [("prep", g), ("prepqk", g), ("level0", g)]
        for lv in range(1, 6):
            solve += [("right", g, lv), ("left", g, lv)]
        solve += [("turnkv", g), ("solved", g)]
    fill = [("proj", u, half) for u in range(11, 2 * PROJ_PAIRS) for half in range(2)]
    steps += [fill.pop(0), ("rope", 9)]
    last = [solve.pop(), solve.pop()]
    rests, heads = [], []
    while fill or solve:
        late = []
        kind = solve[0][0] if solve else ""
        if solve:
            steps.append(solve.pop(0))
            steps += rests
            rests = [("rests", p) for _, p in heads]
            steps += heads
            heads = []
            if kind == "prepqk":
                steps += rests
                rests = []
        for _ in range(2 if kind in ("prep", "prepqk", "level0", "turnkv") else 1):
            if fill:
                f = fill.pop(0)
                if f[2] == 0 and f[1] - 2 in ROPE_OF:
                    late.append(("rope", f[1] - 2))
                steps.append(f)
                if f[2] == 1 and f[1] % 2:
                    heads.append(("heads", f[1] // 2 + 2))
        steps += late
    steps += rests + heads + [("rests", p) for _, p in heads]
    scan = [(kind, j) for j in range(NCH) for kind in ("scan", "update")]
    parts = {"normsum": 1, "normexp": 2, "normmul": 2, "normhi": 3, "normlo": 4}
    ready, due, norms = [], {kind: [] for kind in parts}, []
    i = 0
    while i < H * NT + 3 or scan:
        steps += [("normexp", o) for at, o in due["normexp"] if at == i]
        if i < H * NT + 3:
            if last:
                steps.append(last.pop())
            steps.append(("attend", i))
            ready += [("attention", t) for t in range(NT) if i - 2 == tile_end(t)]
        for _ in range(SCAN_STEPS[i] if i < len(SCAN_STEPS) else 1):
            if scan:
                steps.append(scan.pop(0))
                if steps[-1][0] == "update" and steps[-1][1] % 2:
                    ready.append(("delta", steps[-1][1] // 2))
        for kind in ("normlo", "normhi", "normmul", "normsum"):
            steps += [(kind, o) for at, o in due[kind] if at == i]
        for kind in parts:
            due[kind] = [(at, o) for at, o in due[kind] if at > i]
        if ready:
            norms.append(ready.pop(0))
            steps.append(("normsq", len(norms) - 1))
            for kind, late in parts.items():
                due[kind].append((i + late, len(norms) - 1))
        i += 1
    for n in ready:
        norms.append(n)
        steps.append(("normsq", len(norms) - 1))
        for kind in parts:
            due[kind].append((i, len(norms) - 1))
    steps += [("normsum", o) for _, o in due["normsum"]]
    for o in range(len(norms)):
        steps += [(kind, o) for kind in ("normexp", "normmul", "normhi", "normlo") if o in [n for _, n in due[kind]]]
    return steps, norms


def build(nc, x_in, ffn1_w_gate, ffn1_w_up, ffn1_w_down, w_in, w_out, ffn2_w_gate, ffn2_w_up, ffn2_w_down,
          params_in, a_log, dt_bias, lambda_q1, lambda_k1, lambda_q2, lambda_k2, masks_in, angle_in, lam_in, out):
    ctx = ExitStack()
    with ctx:
        top = [16512]

        def at(name, cols, dt=F32, where=None):
            n = math.prod(cols)
            place = top[0] if where is None else where[0]
            t = nc.alloc_sbuf_tensor_at(name, [P] + list(cols), dt, offset=place)
            size = -(-n * 4 // 32) * 32
            if where is None:
                top[0] += size
            else:
                where[0] += size
            return t

        def sem(name):
            s = ctx.enter_context(nc.semaphore(name))
            layer_sems.append(s)
            return s

        layer_sems = []
        x = at("x", [KD, S])
        xh = at("xh", [KD, S], F32R)
        xl = at("xl", [KD, S], F32R)
        raw = at("raw", [2, 16, P])
        wh = at("wh", [2, 16, P], F32R)
        wl = at("wl", [2, 16, P], F32R)
        rstd = at("rstd", [S])
        acc = at("acc", [S])
        sq = at("sq", [S])
        ones = at("ones", [P])
        par = at("par", [ROWS])
        eps_c = at("eps_c", [2])
        w = [top[0]]
        hh = at("hh", [KF, S], F32R, w)
        hl = at("hl", [KF, S], F32R, w)
        tg = at("tg", [S], F32, w)
        tu = at("tu", [S], F32, w)
        ffn_end = w[0]
        w = [top[0]]
        qkv = at("qkv", [3 * H, S], F32, w)
        wT = at("wT", [NT, H, P], F32, w)
        qkT = at("qkT", [NT, H, P], F32, w)
        dqk = at("dqk", [2 * H, S], F32, w)
        V = at("V", [NT, H * P], F32, w)
        gate_at = w[0]
        gate = at("gate", [H, S], F32, w)
        state_at = w[0]
        state = at("state", [H, P], F32, w)
        vnew = at("vnew", [H, P], F32, w)
        solve = [w[0]]
        bM = [at(f"bM{s}", [H, P], F32, w) for s in range(2)]
        bT = [at(f"bT{s}", [H, P], F32, w) for s in range(2)]
        bB = [at(f"bB{s}", [H, P], F32, w) for s in range(2)]
        bU = [at(f"bU{s}", [H, P], F32, w) for s in range(2)]
        mixer_end = w[0]
        early = [gate_at]
        xin = at("xin", [S + CONV_K], F32, early)
        yconv = [at(f"yconv{s}", [S], F32, early) for s in range(2)]
        assert early[0] <= state_at
        early = [solve[0]]
        abw = at("abw", [KD, 2 * H], F32, early)
        abh = at("abh", [KD, 2 * H], F32R, early)
        abl = at("abl", [KD, 2 * H], F32R, early)
        abf = at("abf", [S], F32, early)
        solve = [top[0] + (mixer_end - 8 * S * 4 - top[0])]
        prob = [at(f"prob{b}", [2, S], F32, solve) for b in range(3)]
        attT = [at(f"attT{b}", [NT, P], F32, solve) for b in range(2)]
        assert solve[0] <= mixer_end
        w = [max(ffn_end, mixer_end)]
        angle = at("angle", [2, S], F32, w)
        masks = at("masks", [len(CONSTS) - 1, P], F32, w)
        turned = at("turned", [S], F32, w)
        rtok = at("rtok", [NT], F32, w)
        ab = at("ab", [NT, 2 * H], F32, w)
        gl = at("gl", [NT, H], F32, w)
        gt = at("gt", [NT, H], F32, w)
        beta = at("beta", [NT, H], F32, w)
        gcol = at("gcol", [NT, H], F32, w)
        ecol = at("ecol", [NT, H], F32, w)
        esuf = at("esuf", [NT, H], F32, w)
        egl = at("egl", [NT, H, 2], F32, w)
        hpar = at("hpar", [2, H], F32, w)
        lam = at("lam", [4], F32, w)
        lsum = at("lsum", [2], F32, w)
        dnorm = at("dnorm", [1], F32, w)
        mx = at("mx", [3, 2], F32, w)
        ssum = at("ssum", [3, 2], F32, w)
        rsum = at("rsum", [3, 2], F32, w)
        assert w[0] <= nc.sbuf_usable_end, (w[0], nc.sbuf_usable_end)

        def mask(name):
            return masks[:, CONSTS.index(name) - 1, :]

        def over_heads(ap):
            return ap.unsqueeze(1).broadcast_to([P, H, P])

        def over_cols(ap):
            return ap.unsqueeze(2).broadcast_to([P, H, P])

        psum = ctx.enter_context(nc.psum_tensor("psum", [P, 8, S], F32))
        ps = [psum[:, i] for i in range(8)]

        def heads(bank):
            return ps[bank][:].rearrange("p (h c) -> p h c", h=H)

        s_in = [ctx.enter_context(nc.semaphore(f"x_loaded{t}")) for t in range(NT)]
        s_const = ctx.enter_context(nc.semaphore("ident_loaded"))
        s_kept_in = ctx.enter_context(nc.semaphore("constants_loaded"))
        s_turn = ctx.enter_context(nc.semaphore("turned"))
        s_kept = ctx.enter_context(nc.semaphore("turned_kept"))
        s_memset = ctx.enter_context(nc.semaphore("memset_done"))
        xstage = nc.alloc_sbuf_tensor_at("xstage", [P, NT, D], F32, offset=top[0])
        ident0 = nc.alloc_sbuf_tensor_at("ident0", [P, P], F32, offset=top[0] + NT * D * 4)
        ahead_par = ctx.enter_context(nc.semaphore("ahead_par"))
        ahead_raw = [ctx.enter_context(nc.semaphore(f"ahead_raw{s}")) for s in range(2)]

        def load_ahead(sp, layer, raw_free=None, par_free=None):
            if par_free:
                par_free()
            sp.dma_start(par[:], params_in[layer]).then_inc(ahead_par, 16)
            for i in range(2):
                if raw_free:
                    raw_free(i)
                for a, m in enumerate((ffn1_w_gate, ffn1_w_up)):
                    sp.dma_start(raw[:, i, KD * a:KD * a + KD, :],
                                 m[layer].rearrange("(k p) (n c) -> n p k c", p=P, c=P)[i]).then_inc(ahead_raw[i], 16)

        with nc.Block() as block:
            @block.sync
            def _(sp):
                sp.dma_start(ident0[:], masks_in[:, CONSTS.index("ident"), :]).then_inc(s_const, 16)
                sp.dma_start(ones[:], masks_in[:, CONSTS.index("ones"), :]).then_inc(s_const, 16)
                for t in range(NT):
                    sp.dma_start(xstage[:, t, :], x_in[t * P:(t + 1) * P, :]).then_inc(s_in[t], 16)
                load_ahead(sp, 0)
                sp.dma_start(masks[:], masks_in[:, 1:, :]).then_inc(s_kept_in, 16)
                sp.dma_start(angle[:], angle_in).then_inc(s_kept_in, 16)

            @block.tensor
            def _(pe):
                pe.wait_ge(s_const, 32)
                for t in range(NT):
                    pe.wait_ge(s_in[t], 16)
                    for q in range(2):
                        for j in range(4):
                            last = pe.transpose(ps[2 * t + q][:, j * P:(j + 1) * P],
                                                xstage[:, t, (4 * q + j) * P:(4 * q + j + 1) * P], ident0[:])
                        last.then_inc(s_turn, 1)

            @block.scalar
            def _(act):
                for t in range(NT):
                    act.wait_ge(s_turn, 2 * t + 2)
                    act.activation(x[:, 4:8, t * P:(t + 1) * P], ps[2 * t + 1][:].rearrange("p (j c) -> p j c", j=4),
                                   ACT.Copy).then_inc(s_kept, 1)

            @block.vector
            def _(dve):
                dve.memset(eps_c[:, 0:1], EPS).then_inc(s_memset, 1)
                dve.memset(eps_c[:, 1:2], -0.5 * math.log(P)).then_inc(s_memset, 1)
                for t in range(NT):
                    dve.wait_ge(s_turn, 2 * t + 1)
                    dve.tensor_copy(x[:, 0:4, t * P:(t + 1) * P],
                                    ps[2 * t][:].rearrange("p (j c) -> p j c", j=4)).then_inc(s_kept, 1)

        raw_in = [sem(f"raw_in{s}") for s in range(2)]
        hi_first, lo_first = sem("hi_first"), sem("lo_first")
        hi_done, lo_done = sem("hi_done"), sem("lo_done")
        pair_done = sem("pair_done")
        half_done = sem("half_done")
        down_done, out_done = sem("down_done"), sem("out_done")
        x_new = sem("x_new")
        xh_done, x_chunk = sem("xh_done"), sem("x_chunk")
        sq_done, acc_done = sem("sq_done"), sem("acc_done")
        norm_mm, ln_done, rstd_done = sem("norm_mm"), sem("ln_done"), sem("rstd_done")
        tg_done, sg_done, up_evac = sem("tg_done"), sem("sg_done"), sem("up_evac")
        h_new, hh_done, h_done = sem("h_new"), sem("hh_done"), sem("h_done")
        mix_in = sem("mix_in")
        act_chain, dve_chain = sem("act_chain"), sem("dve_chain")
        ab_hi, ab_split, ab_mm, ab_scaled = sem("ab_hi"), sem("ab_split"), sem("ab_mm"), sem("ab_scaled")
        ab_turned, ab_by_token = sem("ab_turned"), sem("ab_by_token")
        spe_in, spe_exp, spe_ln = sem("spe_in"), sem("spe_exp"), sem("spe_ln")
        g_done, gcol_mm, gcol_exp, gcol_done = sem("g_done"), sem("gcol_mm"), sem("gcol_exp"), sem("gcol_done")
        lam_prod, lam_exp = sem("lam_prod"), sem("lam_exp")
        mix_evac, v_evac = sem("mix_evac"), sem("v_evac")
        conv_done, silu_done, gate_done = sem("conv_done"), sem("silu_done"), sem("gate_done")
        rope_swapped, rope_sin, rope_cos, rope_done = sem("rope_swapped"), sem("rope_sin"), sem("rope_cos"), sem("rope_done")
        l2_sq, l2_mm, l2_r, l2_done = sem("l2_sq"), sem("l2_mm"), sem("l2_r"), sem("l2_done")
        grow_mm, dx_done, e_done, dexp_done, sb_done = (sem("grow_mm"), sem("dx_done"), sem("e_done"),
                                                        sem("dexp_done"), sem("sb_done"))
        kk_mm, qk_mm, qkT_done = sem("kk_mm"), sem("qk_mm"), sem("qkT_done")
        qdec_done, egl_done = sem("qdec_done"), sem("egl_done")
        t0_done, t0_turn, u0_done = sem("t0_done"), sem("t0_turn"), sem("u0_done")
        b_done, r_mm, r_done, du_mm, tu_done = (sem("b_done"), sem("r_mm"), sem("r_done"), sem("du_mm"),
                                                sem("tu_done"))
        kturn, vturn, kb_done, vb_done = sem("kturn"), sem("vturn"), sem("kb_done"), sem("vb_done")
        w_mm, u_mm, w_done, u_done = sem("w_mm"), sem("u_mm"), sem("w_done"), sem("u_done")
        ws_mm, vnew_done, sup_mm, s_done, o_mm, o_done = (sem("ws_mm"), sem("vnew_done"), sem("sup_mm"),
                                                          sem("s_done"), sem("o_mm"), sem("o_done"))
        sc_mm, mx_done, p_done, a_done = sem("sc_mm"), sem("mx_done"), sem("p_done"), sem("a_done")
        at_mm, at_done, pv_mm, pv_done = sem("at_mm"), sem("at_done"), sem("pv_mm"), sem("pv_done")
        hn_sq, hn_mm, hn_ln, hn_r = sem("hn_sq"), sem("hn_mm"), sem("hn_ln"), sem("hn_r")
        hn_gated, hn_out, hn_hi, hn_done = sem("hn_gated"), sem("hn_out"), sem("hn_hi"), sem("hn_done")

        steps, norms = mixer_steps()
        att_last = max(o for o, n in enumerate(norms) if n[0] == "attention")
        delta_last = max(o for o, n in enumerate(norms) if n[0] == "delta")
        out_order = [2, 3, 0, 1] if att_last < delta_last else [0, 1, 2, 3]
        MIX_PARTS = 1 + 2 + 1 + 4

        def normed(o):
            kind, t = norms[o]
            tok = slice(t * P, (t + 1) * P)
            src, first = (qkv, 0) if kind == "delta" else (dqk, H)
            return (kind, t, src[:, 0:H, tok], xh[:, first:first + H, tok], xl[:, first:first + H, tok],
                    6 if o < 2 * NT - 1 else 4, (sq, acc)[o % 2])

        def norms_before(j):
            return sum(st[0] == "normsum" for st in steps[:steps.index(("update", j))])

        def updates_before(o):
            return sum(st[0] == "update" for st in steps[:steps.index(("normsum", o))])

        def of_pair(weights, slot):
            return weights[:, slot].rearrange("p (a k) c -> p a k c", a=2)

        def flat(ap):
            return ap.rearrange("p h c -> p (h c)")

        def wait_half(engine, u):
            if u % 2 == 0:
                engine.wait_ge(half_done, u // 2 + 1)
            else:
                engine.wait_ge(pair_done, 2 + PAIR_PROJ + u // 2 + 1)

        def body(l):
            with nc.Block() as block:
                @block.sync
                def _(sp):
                    def load(n, slot, parts):
                        sp.wait_ge(lo_done, n + 1)
                        for dst, src in parts:
                            sp.dma_start(dst, src).then_inc(raw_in[slot], 16)

                    def load_up(f, i, slot):
                        mats = (ffn1_w_gate, ffn1_w_up) if f == 0 else (ffn2_w_gate, ffn2_w_up)
                        load(i + PAIR_UP[f], slot, [
                            (raw[:, slot, KD * a:KD * a + KD, :],
                             m[l].rearrange("(k p) (n c) -> n p k c", p=P, c=P)[i]) for a, m in enumerate(mats)])

                    def load_rows(n, slot, m, j):
                        rows_of = m[l].rearrange("(j k p) n -> j k p n", k=2, p=P)[j]
                        load(n, slot, [
                            (raw[:, slot, KD * a:KD * a + KD, :].rearrange("p m c -> p (m c)"), rows_of[a])
                            for a in range(2)])

                    def load_cols(n, slot, mat, col):
                        src = mat[l].rearrange("(k p) n -> p k n", p=P)
                        dst = raw[:, slot, :, :].rearrange("p (k a) c -> p k (a c)", a=2)
                        load(n, slot, [(dst[:, 4 * a:4 * a + 4, :], src[:, 4 * a:4 * a + 4, col:col + 2 * P])
                                       for a in range(2)])

                    def ffn(f):
                        down = ffn1_w_down if f == 0 else ffn2_w_down
                        with sp.Fori(1 if f == 0 else 0, UP_PAIRS // 2) as it:
                            for u in range(2):
                                load_up(f, it * 2 + u, (PAIR_UP[f] + u) % 2)
                        with sp.Fori(0, DOWN_PAIRS // 2) as it:
                            for u in range(2):
                                load_rows(it * 2 + u + PAIR_DOWN[f], (PAIR_DOWN[f] + u) % 2, down, it * 2 + u)
                        last = PAIR_DOWN[f] + DOWN_PAIRS - 1
                        load_rows(last, last % 2, down, DOWN_PAIRS - 1)

                    ffn(0)
                    def swap_halves(u):
                        o = ROPE_ORDER[u]
                        sp.wait_ge(mix_evac, u + 1)
                        if o:
                            sp.wait_ge(rope_done, o)
                        half = DD // 2
                        for b in range(P // half):
                            a = b + 1 if b % 2 == 0 else b - 1
                            sp.dma_start(turned[b * half:(b + 1) * half, :],
                                         dqk[a * half:(a + 1) * half, ROPE_OF[u], :]).then_inc(rope_swapped, 16)

                    for p in range(PROJ_PAIRS):
                        if 2 * (p - SWAP_LAG) in ROPE_OF:
                            swap_halves(2 * (p - SWAP_LAG))
                            swap_halves(2 * (p - SWAP_LAG) + 1)
                        load_cols(PAIR_PROJ + p, (PAIR_PROJ + p) % 2, w_in, PROJ_COLS[p])
                        if p == 1:
                            sp.wait_ge(pair_done, 2 + PAIR_PROJ)
                            sp.wait_ge(s_kept_in, 32)
                            sp.dma_start(abw[:], w_in[l].rearrange("(k p) n -> p k n", p=P)[:, :, COL_AB:COL_AB + 2 * H])\
                              .then_inc(mix_in, 16)
                            sp.dma_start(hpar[:, 0, :], a_log[l].unsqueeze(0).broadcast_to([P, H])).then_inc(mix_in, 16)
                            sp.dma_start(hpar[:, 1, :], dt_bias[l].unsqueeze(0).broadcast_to([P, H])).then_inc(mix_in, 16)
                            sp.dma_start(lam[:, 0:2], lam_in[l]).then_inc(mix_in, 16)
                            for i, v in enumerate((lambda_q1, lambda_k1, lambda_q2, lambda_k2)):
                                sp.dma_start(state[:, i, 0:DD], v[l].unsqueeze(0).broadcast_to([P, DD])).then_inc(mix_in, 16)
                    for p in range(OUT_PAIRS):
                        load_rows(PAIR_OUT + p, (PAIR_OUT + p) % 2, w_out, out_order[p])
                    ffn(1)
                    load_ahead(sp, (l + 1) % DEPTH, lambda i: sp.wait_ge(lo_done, 2 + PAIRS - 1 + i),
                               lambda: sp.wait_ge(x_chunk, 3 * KD))

                @block.scalar
                def _(act):
                    def chained(counter=[0]):
                        counter[0] += 1
                        act.wait_ge(act_chain, counter[0])

                    def split(n, slot, k):
                        if isinstance(k, int) and k == 0:
                            act.wait_ge(ahead_raw[slot], l * 32 + 32)
                        else:
                            act.wait_ge(raw_in[slot], k * 32)
                        act.wait_ge(pair_done, n + 1)
                        act.activation(wh[:, slot], raw[:, slot], ACT.Copy).then_inc(hi_done, 1)

                    def split_static(n):
                        if n < PAIRS:
                            split(n, n % 2, n // 2)

                    def split_first():
                        act.wait_ge(ahead_raw[0], l * 32 + 32)
                        act.wait_ge(pair_done, 1)
                        for b, done in enumerate((hi_first, hi_done)):
                            act.activation(of_pair(wh, 0)[:, :, 4 * b:4 * b + 4], of_pair(raw, 0)[:, :, 4 * b:4 * b + 4],
                                           ACT.Copy).then_inc(done, 1)

                    def heads_of_x(s, gain_row, n=None):
                        for m in range(KD):
                            if m == 4 and n:
                                split_static(n)
                            if s:
                                act.wait_ge(x_new, KD * (s - 1) + m + 1)
                            if s == 2:
                                last_read = m // 2 == out_order[-1]
                                act.wait_ge(pair_done, 2 + PAIR_OUT + OUT_PAIRS - (0 if last_read else 1))
                            if gain_row is not None:
                                act.activation(xh[:, m], x[:, m], ACT.Copy, scale=par[:, gain_row + m:gain_row + m + 1])\
                                   .then_inc(xh_done, 1)
                            if m >= 3:
                                act.wait_ge(acc_done, (KD - 1) * s + max(m - 3, 1))
                            elif s and m == 0:
                                act.wait_ge(norm_mm, s)
                            act.activation((sq, rstd, turned)[m % 3][:], x[:, m], ACT.Square).then_inc(sq_done, 1)
                        act.preload_act_table(ACT.Ln)

                    def norm_factor(s):
                        act.wait_ge(norm_mm, s + 1)
                        act.activation(sq[:], ps[7][:], ACT.Ln, scale=1.0 / D, bias=eps_c[:, 0:1]).then_inc(ln_done, 1)
                        act.wait_ge(ln_done, s + 1)
                        act.activation(rstd[:], sq[:], ACT.Exp, scale=-0.5).then_inc(rstd_done, 1)

                    def up_step(f, i):
                        q = i + UP_PAIRS * f
                        act.wait_ge(tg_done, q + 1)
                        act.activation(tg[:], tg[:], ACT.Silu).then_inc(sg_done, 1)
                        act.wait_ge(h_new, q + 1)
                        at_i = hh[:, i] if isinstance(i, int) else hh[:, bass.ds(i, 1)].rearrange("p a c -> p (a c)")
                        act.activation(at_i, tu[:], ACT.Copy).then_inc(hh_done, 1)

                    def ffn(f):
                        norm_factor(2 * f)
                        for i in range(2):
                            up_step(f, i)
                            split_static(PAIR_UP[f] + i + 2)
                        with act.Fori(1, UP_PAIRS // 2) as it:
                            for u in range(2):
                                n = PAIR_UP[f] + u + 2
                                up_step(f, it * 2 + u)
                                split(it * 2 + n, n % 2, it + n // 2)
                        for j in range(DOWN_PAIRS - 1):
                            split_static(PAIR_DOWN[f] + j + 2)

                    act.wait_ge(ahead_par, l * 16 + 16)
                    split_first()
                    heads_of_x(0, ROW_G1, 1)
                    ffn(0)
                    heads_of_x(1, ROW_GM)
                    split_static(PAIR_PROJ + 1)

                    def act_step(kind, *a):
                        if kind == "first":
                            norm_factor(1)
                        elif kind == "conv" or kind == "proj" and a[1] == 1:
                            u = a[0]
                            if u in CONV_OF:
                                c, n = CONV_OF[u], CONV_ORDER[u]
                                act.wait_ge(conv_done, n + 1)
                                act.activation(qkv[:, c], yconv[n % 2][:], ACT.Silu).then_inc(silu_done, 1)
                                if n < H:
                                    if n == 0:
                                        act.wait_ge(rstd_done, 2)
                                    elif n == 1:
                                        act.wait_ge(norm_mm, 2)
                                    else:
                                        act.wait_ge(l2_mm, n - 1)
                                    act.wait_ge(silu_done, n + 1)
                                    act.activation((sq, acc)[n % 2][:], qkv[:, c], ACT.Square).then_inc(l2_sq, 1)
                            elif u // 2 in (V_PAIR, V_PAIR + 1):
                                j, p = u % 2, u // 2 - V_PAIR
                                wait_half(act, u)
                                for b in range(2):
                                    i = act.activation(V[:, 2 * j + b, p * 256:(p + 1) * 256],
                                                       ps[u % 4][:, b * 256:(b + 1) * 256], ACT.Copy,
                                                       scale=rtok[:, 2 * j + b:2 * j + b + 1])
                                i.then_inc(v_evac, 1)
                            elif u // 2 >= GATE_PAIR:
                                c = u - 2 * GATE_PAIR
                                act.wait_ge(mix_evac, 20 + c + 1)
                                act.activation(gate[:, c], gate[:, c], ACT.Silu).then_inc(gate_done, 1)
                        elif kind == "l2sq":
                            n, = a
                            act.wait_ge(l2_mm, n - 1)
                            act.wait_ge(silu_done, n + 1)
                            act.activation((sq, acc)[n % 2][:], qkv[:, n - H], ACT.Square).then_inc(l2_sq, 1)
                        elif kind == "absplit":
                            act.wait_ge(mix_in, 16 * MIX_PARTS)
                            act.activation(abh[:], abw[:], ACT.Copy).then_inc(ab_hi, 1)
                        elif kind == "heads":
                            split_static(PAIR_PROJ + a[0])
                        elif kind == "softplus":
                            act.preload_act_table_set(LN_EXP)
                            act.wait_ge(lam_prod, 2)
                            act.activation(lsum[:], lsum[:], ACT.Exp).then_inc(lam_exp, 1)
                            act.activation(hpar[:, 0, :], hpar[:, 0, :], ACT.Exp).then_inc(spe_exp, 1)
                            act.wait_ge(spe_in, 1)
                            act.activation(gt[:], gt[:], ACT.Exp, scale=-1.0).then_inc(act_chain, 1)
                            act.activation(beta[:], ab[:, :, H:2 * H], ACT.Exp, scale=-1.0).then_inc(spe_exp, 1)
                            chained()
                            act.activation(gt[:], gt[:], ACT.Ln, bias=1.0).then_inc(spe_ln, 1)
                        elif kind == "decayed":
                            act.preload_act_table_set(LN_EXP)
                            act.wait_ge(gcol_mm, 1)
                            act.activation(ecol[:], ps[SUM_BANK][:, 128:128 + NT * H].rearrange("p (t h) -> p t h", h=H),
                                           ACT.Exp).then_inc(gcol_exp, 1)
                            act.activation(gcol[:], ps[SUM_BANK][:, 128:128 + NT * H].rearrange("p (t h) -> p t h", h=H),
                                           ACT.Copy).then_inc(gcol_exp, 1)
                            act.activation(esuf[:], ps[SUM_BANK][:, 192:192 + NT * H].rearrange("p (t h) -> p t h", h=H),
                                           ACT.Exp).then_inc(gcol_exp, 1)
                        elif kind == "l2norm":
                            act.preload_act_table_set(LN_EXP)
                            for n in range(4 * a[0], 4 * a[0] + 4):
                                bank = L2_BANKS[n % 4]
                                act.wait_ge(l2_mm, n + 1)
                                act.activation(ps[bank][:], ps[bank][:], ACT.Ln, bias=eps_c[:, 0:1]).then_inc(act_chain, 1)
                            for n in range(4 * a[0], 4 * a[0] + 4):
                                bank = L2_BANKS[n % 4]
                                chained()
                                bias = eps_c[:, 1:2] if n >= 4 else 0.0
                                act.activation(ps[bank][:], ps[bank][:], ACT.Exp, scale=-0.5, bias=bias).then_inc(l2_r, 1)
                        elif kind == "prep":
                            g, = a
                            act.preload_act_table_set(LN_EXP)
                            for s in range(2):
                                o = 2 * g + s
                                act.wait_ge(dx_done, o + 1)
                                if g:
                                    act.wait_ge(w_done, o - 1)
                                    act.wait_ge(u_done, o - 1)
                                act.activation(bU[s][:], heads(4 + 2 * s), ACT.Exp).then_inc(e_done, 1)
                            for s in range(2):
                                o = 2 * g + s
                                act.wait_ge(dx_done, o + 1)
                                act.activation(bM[s][:], bM[s][:], ACT.Abs).then_inc(act_chain, 1)
                                chained()
                                act.activation(bM[s][:], bM[s][:], ACT.Exp, scale=-1.0).then_inc(dexp_done, 1)
                        elif kind == "level0":
                            g, = a
                            for s in range(2):
                                o = 2 * g + s
                                act.wait_ge(t0_turn, o + 1)
                                act.wait_ge(qdec_done, o + 1)
                                act.wait_ge(egl_done, o + 1)
                                act.activation(bU[s][:], heads(4 + 2 * s), ACT.Copy).then_inc(u0_done, 1)
                        elif kind == "right":
                            g, lv = a
                            for s in range(2):
                                o = (g * 5 + lv - 1) * 2 + s
                                act.wait_ge(r_mm, o + 1)
                                act.activation(wT[:, 2 * g + s], heads(4 + 2 * s), ACT.Copy).then_inc(r_done, 1)
                        elif kind == "solved":
                            g, = a
                            for s in range(2):
                                t, o = 2 * g + s, 2 * g + s
                                act.wait_ge(w_mm, o + 1)
                                act.activation(wT[:, t], heads(4 + 2 * s), ACT.Copy).then_inc(w_done, 1)
                                act.wait_ge(u_mm, o + 1)
                                act.activation(qkv[:, 2 * H:3 * H, t * P:(t + 1) * P], heads(5 + 2 * s), ACT.Copy)\
                                   .then_inc(u_done, 1)
                        elif kind == "update":
                            j, = a
                            act.wait_ge(o_mm, j + 1)
                            act.activation(qkv[:, 0:H, j * CH:(j + 1) * CH],
                                           ps[6][:, 0:H * CH].rearrange("p (h c) -> p h c", h=H), ACT.Copy)\
                               .then_inc(o_done, 1)
                        elif kind == "attend":
                            i, = a
                            if i == 0:
                                act.preload_act_table_set(LN_EXP)
                            q = i - 2
                            if 0 <= q < H * NT:
                                n = (item_of(q)[1] + 1) * P
                                if q >= 2:
                                    act.wait_ge(pv_mm, q - 1)
                                act.wait_ge(at_mm, q + 1)
                                act.activation(flat(attT[q % 2][:])[:, 0:n], ps[5][:, 0:n], ACT.Copy).then_inc(at_done, 1)
                            if i < H * NT:
                                n, b = (item_of(i)[1] + 1) * P, i % 3
                                if i == 0:
                                    act.wait_ge(b_done, 20)
                                elif i == 1:
                                    act.wait_ge(tu_done, 36)
                                act.wait_ge(mx_done, i + 1)
                                for s in range(2):
                                    act.activation(prob[b][:, s, 0:n], ps[2 * (i % 2) + s][:, 0:n], ACT.Exp,
                                                   bias=mx[:, b, s:s + 1], accum_out=ssum[:, b, s:s + 1]).then_inc(p_done, 1)
                            q = i - 3
                            if q >= 0:
                                h, t = item_of(q)
                                act.wait_ge(pv_mm, q + 1)
                                act.activation(dqk[:, h, t * P:(t + 1) * P], ps[7][:, 0:P], ACT.Copy).then_inc(pv_done, 1)
                        elif kind == "normsq":
                            o, = a
                            which, t, src = normed(o)[:3]
                            if which == "delta":
                                act.wait_ge(o_done, 2 * t + 2)
                            else:
                                act.wait_ge(pv_done, tile_end(t))
                            if o >= 2:
                                act.wait_ge(hn_out, o - 1)
                            elif o == 0:
                                act.wait_ge(l2_mm, 2 * H)
                            dst = (sq, acc)[o % 2]
                            act.activation(dst[:].rearrange("p (h c) -> p h c", h=H), src, ACT.Square).then_inc(hn_sq, 1)
                        elif kind == "normexp":
                            o, = a
                            bank, place = normed(o)[5:]
                            act.wait_ge(hn_mm, o + 1)
                            act.activation(place[:], ps[bank][:], ACT.Ln, scale=1.0 / P, bias=eps_c[:, 0:1])\
                               .then_inc(hn_ln, 1)
                            act.wait_ge(hn_ln, o + 1)
                            act.activation(place[:], place[:], ACT.Exp, scale=-0.5).then_inc(hn_r, 1)
                        elif kind == "normhi":
                            o, = a
                            src, hi = normed(o)[2:4]
                            act.wait_ge(hn_out, o + 1)
                            act.activation(hi, src, ACT.Copy).then_inc(hn_hi, 1)

                    for st in steps:
                        act_step(*st)
                    for p in range(OUT_PAIRS - 1):
                        split_static(PAIR_OUT + p + 2)
                    heads_of_x(2, ROW_G2)
                    split_static(PAIR_OUT + OUT_PAIRS + 1)
                    ffn(1)
                    heads_of_x(3, None)

                @block.vector
                def _(dve):
                    counter = [0]

                    def link(ins):
                        counter[0] += 1
                        ins.then_inc(dve_chain, 1)
                        dve.wait_ge(dve_chain, counter[0])

                    def split(n, slot):
                        dve.wait_ge(hi_done, n + 1)
                        dve.tensor_tensor(wl[:, slot], raw[:, slot], wh[:, slot].bitcast(F32), ALU.subtract)\
                           .then_inc(lo_done, 1)

                    def split_static(n):
                        if n < PAIRS:
                            split(n, n % 2)

                    def rest_of_x(s, gain_row, m):
                        dve.wait_ge(xh_done, KD * s + m + 1)
                        dve.scalar_tensor_tensor(xl[:, m], x[:, m], par[:, gain_row + m:gain_row + m + 1],
                                                 xh[:, m].bitcast(F32), ALU.mult, ALU.subtract).then_inc(x_chunk, 1)

                    def add_to_x(s, factor, gain_row, ready):
                        for m in range(KD):
                            ready(m)
                            dve.scalar_tensor_tensor(x[:, m], ps[m][:], factor, x[:, m], ALU.mult, ALU.add)\
                               .then_inc(x_new, 1)
                            if gain_row is not None and m:
                                rest_of_x(s, gain_row, m - 1)
                        if gain_row is not None:
                            rest_of_x(s, gain_row, KD - 1)

                    def up_step(f, i, n):
                        q = i + UP_PAIRS * f
                        bank = 2 * ((n - PAIR_UP[f]) % 2)
                        dve.wait_ge(pair_done, (i + PAIR_UP[f]) + 3)
                        dve.tensor_tensor(tg[:], ps[bank][:], rstd[:], ALU.mult).then_inc(tg_done, 1)
                        dve.wait_ge(h_done, q)
                        dve.tensor_tensor(tu[:], ps[bank + 1][:], rstd[:], ALU.mult).then_inc(up_evac, 1)
                        dve.wait_ge(sg_done, q + 1)
                        dve.wait_ge(up_evac, q + 1)
                        dve.tensor_tensor(tu[:], tg[:], tu[:], ALU.mult).then_inc(h_new, 1)
                        dve.wait_ge(hh_done, q + 1)
                        if isinstance(i, int):
                            hi_i, lo_i = hh[:, i], hl[:, i]
                        else:
                            hi_i, lo_i = (b[:, bass.ds(i, 1)].rearrange("p a c -> p (a c)") for b in (hh, hl))
                        dve.tensor_tensor(lo_i, tu[:], hi_i.bitcast(F32), ALU.subtract).then_inc(h_done, 1)

                    def ffn(f, s, gain_row):
                        dve.wait_ge(rstd_done, 2 * f + 1)
                        for i in range(2):
                            up_step(f, i, PAIR_UP[f] + i)
                            split_static(PAIR_UP[f] + i + 2)
                        with dve.Fori(1, UP_PAIRS // 2) as it:
                            for u in range(2):
                                n = PAIR_UP[f] + u
                                up_step(f, it * 2 + u, n)
                                split(it * 2 + (n + 2), n % 2)
                        for j in range(DOWN_PAIRS - 1):
                            split_static(PAIR_DOWN[f] + j + 2)

                        def ready(m):
                            if m < KD - 1:
                                dve.wait_ge(down_done, (KD - 1) * f + m + 1)
                            else:
                                dve.wait_ge(pair_done, 2 + PAIR_DOWN[f] + DOWN_PAIRS)

                        add_to_x(s, 0.5, gain_row, ready)

                    dve.sem_inc(lo_done, 2)
                    for b, (ready, done) in enumerate(((hi_first, lo_first), (hi_done, lo_done))):
                        dve.wait_ge(ready, 1)
                        part = (slice(None), slice(None), slice(4 * b, 4 * b + 4))
                        dve.tensor_tensor(of_pair(wl, 0)[part], of_pair(raw, 0)[part], of_pair(wh, 0)[part].bitcast(F32),
                                          ALU.subtract).then_inc(done, 1)
                        if b == 0:
                            rest_of_x(0, ROW_G1, 0)
                    for m in range(1, KD):
                        if m == 5:
                            split_static(1)
                        rest_of_x(0, ROW_G1, m)
                    ffn(0, 1, ROW_GM)
                    split_static(PAIR_PROJ + 1)

                    def dve_step(kind, *a):
                        if kind == "conv" or kind == "proj" and a[1] == 1:
                            u = a[0]
                            bank = u % 4
                            if u // 2 not in (V_PAIR, V_PAIR + 1):
                                wait_half(dve, u)
                            if u in CONV_OF:
                                c, n = CONV_OF[u], CONV_ORDER[u]
                                y = yconv[n % 2]
                                if n == 0:
                                    dve.wait_ge(rstd_done, 2)
                                    link(dve.memset(xin[:, 0:CONV_K], 0.0))
                                else:
                                    dve.wait_ge(conv_done, n)
                                dve.tensor_tensor(xin[:, CONV_K:CONV_K + S], ps[bank][:], rstd[:], ALU.mult)\
                                   .then_inc(mix_evac, 1)
                                dve.wait_ge(mix_evac, u + 1)
                                if n >= 2:
                                    dve.wait_ge(silu_done, n - 1)
                                for k in range(CONV_K):
                                    tap = par[:, ROW_CONV + 12 * k + c:ROW_CONV + 12 * k + c + 1]
                                    src = xin[:, k + 1:k + 1 + S]
                                    if k == 0:
                                        ins = dve.tensor_scalar(y[:], src, tap, None, ALU.mult)
                                    else:
                                        ins = dve.scalar_tensor_tensor(y[:], src, tap, y[:], ALU.mult, ALU.add)
                                    if k < CONV_K - 1:
                                        link(ins)
                                ins.then_inc(conv_done, 1)
                            elif u in ROPE_OF:
                                dve.scalar_tensor_tensor(dqk[:, ROPE_OF[u]], ps[bank][:], DD ** -0.5 if ROPE_OF[u] < H else 1.0,
                                                         rstd[:], ALU.mult, ALU.mult).then_inc(mix_evac, 1)
                            elif u // 2 >= GATE_PAIR:
                                if u == 2 * GATE_PAIR:
                                    dve.wait_ge(silu_done, 3 * H)
                                dve.tensor_tensor(gate[:, u - 2 * GATE_PAIR], ps[bank][:], rstd[:], ALU.mult)\
                                   .then_inc(mix_evac, 1)
                        elif kind == "rests":
                            split_static(PAIR_PROJ + a[0])
                        elif kind == "rope":
                            u, = a
                            o = ROPE_ORDER[u]
                            dve.wait_ge(rope_swapped, 64 * (o + 1))
                            dve.tensor_tensor(turned[:], turned[:], angle[:, 1], ALU.mult).then_inc(rope_sin, 1)
                        elif kind == "absplit":
                            dve.wait_ge(ab_hi, 1)
                            dve.tensor_tensor(abl[:], abw[:], abh[:].bitcast(F32), ALU.subtract).then_inc(ab_split, 1)
                            for i in range(2):
                                link(dve.tensor_tensor(state[:, 2 * i, 0:DD], state[:, 2 * i, 0:DD],
                                                       state[:, 2 * i + 1, 0:DD], ALU.mult))
                                dve.reduce_sum(lsum[:, i:i + 1], state[:, 2 * i, 0:DD], AX.X).then_inc(lam_prod, 1)
                        elif kind == "ab":
                            dve.wait_ge(ab_mm, 1)
                            dve.tensor_tensor(abf[0:2 * H, :], ps[SUM_BANK][0:2 * H, :], rstd[0:2 * H, :], ALU.mult)\
                               .then_inc(ab_scaled, 1)
                        elif kind == "abturn":
                            dve.wait_ge(ab_turned, 1)
                            by_token = ps[SUM_BANK][:, 0:16 * NT].rearrange("p (t c) -> p t c", t=NT)
                            link(dve.tensor_copy(ab[:], by_token[:, :, 0:2 * H]))
                            dve.tensor_copy(rtok[:], by_token[:, :, 2 * H]).then_inc(ab_by_token, 1)
                            alpha = ab[:, :, 0:H]
                            link(dve.tensor_tensor(alpha, alpha, hpar[:, 1, :].unsqueeze(1).broadcast_to([P, NT, H]),
                                                   ALU.add))
                            dve.scalar_tensor_tensor(gt[:], alpha, -1.0, alpha, ALU.mult, ALU.max).then_inc(spe_in, 1)
                        elif kind == "logdecay":
                            dve.wait_ge(spe_ln, 1)
                            link(dve.scalar_tensor_tensor(gl[:], ab[:, :, 0:H], 0.0, gt[:], ALU.max, ALU.add))
                            dve.wait_ge(spe_exp, 2)
                            dve.scalar_tensor_tensor(gl[:], gl[:], -1.0, hpar[:, 0, :].unsqueeze(1).broadcast_to([P, NT, H]),
                                                     ALU.mult, ALU.mult).then_inc(g_done, 1)
                            link(dve.tensor_scalar(beta[:], beta[:], 1.0, None, ALU.add))
                            dve.reciprocal(beta[:], beta[:]).then_inc(g_done, 1)
                            dve.wait_ge(lam_exp, 1)
                            link(dve.tensor_tensor(lam[:, 2:3], lsum[:, 1:2], lsum[:, 0:1], ALU.subtract))
                            link(dve.tensor_tensor(lam[:, 2:3], lam[:, 2:3], lam[:, 0:1], ALU.subtract))
                            link(dve.tensor_tensor(dnorm[:], par[:, ROW_DIFF:ROW_DIFF + 1], lam[:, 1:2], ALU.mult))
                        elif kind == "decayed":
                            dve.wait_ge(gcol_exp, 3)
                            dve.wait_ge(g_done, 2)
                            dve.tensor_tensor(ecol[:], ecol[:], beta[:], ALU.mult).then_inc(gcol_done, 1)
                        elif kind == "l2norm":
                            for n in range(4 * a[0], 4 * a[0] + 4):
                                c = n + 4 if n < 4 else n - 4
                                dve.wait_ge(l2_r, n + 1)
                                dve.tensor_tensor(qkv[:, c], qkv[:, c], ps[L2_BANKS[n % 4]][:], ALU.mult).then_inc(l2_done, 1)
                        elif kind == "prep":
                            g, = a
                            for s in range(2):
                                t, o = 2 * g + s, 2 * g + s
                                dve.wait_ge(grow_mm, o + 1)
                                if o == 0:
                                    dve.wait_ge(gcol_done, 1)
                                dve.tensor_tensor(bM[s][:], heads(4 + 2 * s), over_cols(gcol[:, t]), ALU.subtract)\
                                   .then_inc(dx_done, 1)
                        elif kind == "prepqk":
                            g, = a
                            for s in range(2):
                                t, o = 2 * g + s, 2 * g + s
                                dve.wait_ge(dexp_done, o + 1)
                                dve.tensor_tensor(bT[s][:], bM[s][:], over_heads(mask("tri")), ALU.mult)\
                                   .then_inc(dve_chain, 1)
                                counter[0] += 1
                                dve.wait_ge(sb_done, o + 1)
                                link(dve.tensor_tensor(bM[s][:], bM[s][:], wT[:, t], ALU.mult))
                                dve.wait_ge(kk_mm, o + 1)
                                link(dve.tensor_tensor(bM[s][:], heads(5 + 2 * s), bM[s][:], ALU.mult))
                                dve.wait_ge(e_done, o + 1)
                                dve.tensor_copy(egl[:, t], bU[s][:, :, CH - 1:P:CH]).then_inc(egl_done, 1)
                                dve.tensor_tensor(bB[s][:], bM[s][:], over_heads(mask("level0")), ALU.mult)\
                                   .then_inc(dve_chain, 1)
                                counter[0] += 1
                                dve.wait_ge(qk_mm, o + 1)
                                dve.tensor_tensor(qkT[:, t], heads(4 + 2 * s), bT[s][:], ALU.mult).then_inc(qkT_done, 1)
                                dve.wait_ge(qkT_done, o + 1)
                                dve.wait_ge(dve_chain, counter[0])
                                dve.tensor_tensor(bT[s][:], over_heads(mask("ident")), bB[s][:], ALU.subtract)\
                                   .then_inc(t0_done, 1)
                        elif kind == "left":
                            g, lv = a
                            for s in range(2):
                                o = (g * 5 + lv - 1) * 2 + s
                                dve.wait_ge(du_mm, o + 1)
                                if lv == 1:
                                    dve.wait_ge(u0_done, 2 * g + s + 1)
                                    dve.wait_ge(t0_done, 2 * g + s + 1)
                                else:
                                    dve.wait_ge(tu_done, g * 18 + (lv - 2) * 4 + 2 * s + 2)
                                if lv < 5:
                                    dve.tensor_tensor(bT[s][:], bT[s][:], heads(5 + 2 * s), ALU.subtract).then_inc(tu_done, 1)
                                dve.tensor_tensor(bU[s][:], bU[s][:], heads(4 + 2 * s), ALU.subtract).then_inc(tu_done, 1)
                        elif kind == "turnkv":
                            g, = a
                            for s in range(2):
                                t, o = 2 * g + s, 2 * g + s
                                dve.wait_ge(kturn, o + 1)
                                dve.tensor_tensor(bB[s][:], heads(4 + 2 * s), over_cols(ecol[:, t]), ALU.mult).then_inc(kb_done, 1)
                                dve.tensor_tensor(qkv[:, H:2 * H, t * P:(t + 1) * P], heads(4 + 2 * s),
                                                  over_cols(esuf[:, t]), ALU.mult).then_inc(kb_done, 1)
                                dve.wait_ge(vturn, o + 1)
                                dve.tensor_tensor(qkv[:, 2 * H:3 * H, t * P:(t + 1) * P], heads(5 + 2 * s),
                                                  over_cols(beta[:, t]), ALU.mult).then_inc(vb_done, 1)
                        elif kind == "scan":
                            j, = a
                            t, r = j // 2, CH * (j % 2)
                            if j == 0:
                                dve.memset(state[:], 0.0).then_inc(s_done, 1)
                            dve.wait_ge(ws_mm, j + 1)
                            if j % 2 == 0:
                                dve.wait_ge(u_done, t + 1)
                            if j >= 2:
                                dve.wait_ge(o_mm, j - 1)
                            dve.tensor_tensor(vnew[r:r + CH], qkv[r:r + CH, 2 * H:3 * H, t * P:(t + 1) * P],
                                              ps[4][r:r + CH, :].rearrange("p (h c) -> p h c", h=H), ALU.subtract)\
                               .then_inc(vnew_done, 1)
                        elif kind == "update":
                            j, = a
                            t = j // 2
                            if j == NCH - 1:
                                return
                            dve.wait_ge(sup_mm, j + 1)
                            dve.wait_ge(s_done, j + 1)
                            dve.wait_ge(o_mm, j + 1)
                            for h in range(H):
                                ins = dve.scalar_tensor_tensor(state[:, h], state[:, h], egl[:, t, h, j % 2:j % 2 + 1],
                                                               ps[4][:, h * P:(h + 1) * P], ALU.mult, ALU.add)
                            ins.then_inc(s_done, 1)
                        elif kind == "attend":
                            i, = a
                            if i < H * NT:
                                t = item_of(i)[1]
                                n, b = (t + 1) * P, i % 3
                                both = psum[:, 2 * (i % 2):2 * (i % 2) + 2, :]
                                dve.wait_ge(sc_mm, i + 1)
                                link(dve.tensor_tensor(both[:, :, t * P:n], both[:, :, t * P:n],
                                                       mask("causal").unsqueeze(1).broadcast_to([P, 2, P]), ALU.add))
                                dve.tensor_reduce(mx[:, b, :], both[:, :, 0:n], AX.X, ALU.max, negate=True)\
                                   .then_inc(mx_done, 1)
                            q = i - 1
                            if 0 <= q < H * NT:
                                n, b = (item_of(q)[1] + 1) * P, q % 3
                                dve.wait_ge(p_done, 2 * (q + 1))
                                link(dve.reciprocal(rsum[:, b, :], ssum[:, b, :]))
                                dve.tensor_tensor(rsum[:, b, 1:2], rsum[:, b, 1:2], lam[:, 2:3], ALU.mult).then_inc(dve_chain, 1)
                                counter[0] += 1
                                link(dve.tensor_scalar(prob[b][:, 0, 0:n], prob[b][:, 0, 0:n], rsum[:, b, 0:1], None, ALU.mult))
                                dve.scalar_tensor_tensor(prob[b][:, 0, 0:n], prob[b][:, 1, 0:n], rsum[:, b, 1:2],
                                                         prob[b][:, 0, 0:n], ALU.mult, ALU.add).then_inc(a_done, 1)
                        elif kind == "normmul":
                            o, = a
                            which, t, src, _, _, _, place = normed(o)
                            gain = par[:, ROW_GDN:ROW_GDN + 1] if which == "delta" else dnorm[:, 0:1]
                            dve.wait_ge(hn_r, o + 1)
                            if which == "delta":
                                dve.wait_ge(hn_gated, t + 1)
                            dve.scalar_tensor_tensor(src, src, gain, place[:].rearrange("p (h c) -> p h c", h=H), ALU.mult,
                                                     ALU.mult).then_inc(hn_out, 1)
                        elif kind == "normlo":
                            o, = a
                            _, _, src, hi, lo = normed(o)[:5]
                            dve.wait_ge(hn_hi, o + 1)
                            dve.tensor_tensor(lo, src, hi.bitcast(F32), ALU.subtract).then_inc(hn_done, 1)

                    for st in steps:
                        dve_step(*st)
                    for p in range(OUT_PAIRS - 1):
                        split_static(PAIR_OUT + p + 2)
                    add_to_x(2, 1.0, ROW_G2,
                             lambda m: dve.wait_ge(out_done, m + 1) if m < KD - 1
                             else dve.wait_ge(pair_done, 2 + PAIR_OUT + OUT_PAIRS))
                    split_static(PAIR_OUT + OUT_PAIRS + 1)
                    ffn(1, 3, None)

                @block.gpsimd
                def _(pool):
                    def sums_of_squares(s):
                        if s == 2:
                            pool.wait_ge(hn_done, 2 * NT)
                        for m in range(1, KD):
                            o = KD * s + m + 1
                            pool.wait_ge(sq_done, o)
                            if m == 1:
                                pool.tensor_tensor(acc[:], sq[:], rstd[:], ALU.add).then_inc(acc_done, 1)
                            else:
                                pool.wait_ge(acc_done, (KD - 1) * s + m - 1)
                                pool.tensor_tensor(acc[:], acc[:], (sq, rstd, turned)[m % 3][:], ALU.add).then_inc(acc_done, 1)

                    def pool_step(kind, *a):
                        if kind == "rope":
                            u, = a
                            c, o = ROPE_OF[u], ROPE_ORDER[u]
                            pool.wait_ge(rope_swapped, 64 * (o + 1))
                            pool.tensor_tensor(dqk[:, c], dqk[:, c], angle[:, 0], ALU.mult).then_inc(rope_cos, 1)
                            pool.wait_ge(rope_cos, o + 1)
                            pool.wait_ge(rope_sin, o + 1)
                            pool.tensor_tensor(dqk[:, c], dqk[:, c], turned[:], ALU.add).then_inc(rope_done, 1)
                        elif kind == "prep":
                            g, = a
                            for s in range(2):
                                t = 2 * g + s
                                pool.wait_ge(g_done, 2)
                                pool.tensor_tensor(wT[:, t], over_heads(mask("suffix")), over_cols(beta[:, t]), ALU.mult)\
                                    .then_inc(sb_done, 1)
                        elif kind == "prepqk":
                            g, = a
                            for s in range(2):
                                t, o = 2 * g + s, 2 * g + s
                                pool.wait_ge(qk_mm, o + 1)
                                pool.wait_ge(e_done, o + 1)
                                q_tile = qkv[:, 0:H, t * P:(t + 1) * P]
                                pool.tensor_tensor(q_tile, q_tile, bU[s][:], ALU.mult).then_inc(qdec_done, 1)
                        elif kind == "level0" or kind == "left" and a[1] < 5:
                            g, lv = a if kind == "left" else (a[0], 0)
                            for s in range(2):
                                if lv == 0:
                                    pool.wait_ge(t0_done, 2 * g + s + 1)
                                else:
                                    pool.wait_ge(r_mm, (g * 5 + lv - 1) * 2 + s + 1)
                                pool.tensor_tensor(bB[s][:], bM[s][:], over_heads(mask(f"level{lv + 1}")), ALU.mult)\
                                    .then_inc(b_done, 1)
                        elif kind == "normsum" and norms[a[0]][0] == "delta":
                            o, = a
                            _, t, src = normed(o)[:3]
                            pool.wait_ge(hn_sq, o + 1)
                            pool.wait_ge(gate_done, H)
                            pool.tensor_tensor(src, src, gate[:, :, t * P:(t + 1) * P], ALU.mult).then_inc(hn_gated, 1)
                    sums_of_squares(0)
                    sums_of_squares(1)
                    for st in steps:
                        pool_step(*st)
                    sums_of_squares(2)
                    sums_of_squares(3)

                @block.tensor
                def _(pe):
                    def three(o, wh_t, wl_t, mh, ml, start, stop):
                        pe.matmul(o, wh_t, mh, start=start, stop=False)
                        pe.matmul(o, wh_t, ml, start=False, stop=False)
                        return pe.matmul(o, wl_t, mh, start=False, stop=stop)

                    def up_pair(f, i, n, first=False):
                        slot, bank = n % 2, 2 * ((n - PAIR_UP[f]) % 2)
                        if first and f == 0:
                            pe.wait_ge(lo_first, 1)
                        else:
                            pe.wait_ge(lo_done, (i + PAIR_UP[f]) + 3)
                        if not first and not (isinstance(i, int) and i < 2):
                            pe.wait_ge(up_evac, i + UP_PAIRS * f - 1)
                        for k in range(KD):
                            if first and f == 0 and k == 4:
                                pe.wait_ge(lo_done, 3)
                            for a in range(2):
                                if first:
                                    pe.wait_ge(x_chunk, KD * 2 * f + min(max(k + 1, a + 1), KD))
                                last = three(ps[bank + a][:], wh[:, slot, KD * a + k], wl[:, slot, KD * a + k],
                                             xh[:, k], xl[:, k], k == 0, k == KD - 1)
                        last.then_inc(pair_done, 1)

                    def down_pair(f, j, n, first=False, final=False):
                        slot = n % 2
                        pe.wait_ge(lo_done, (j + PAIR_DOWN[f]) + 3)
                        pe.wait_ge(h_done, KF * f + 2 * j + 2)
                        for m in range(KD):
                            if first and m == 0:
                                pe.wait_ge(up_evac, UP_PAIRS * f + UP_PAIRS - 1)
                            if first and m == 2:
                                pe.wait_ge(up_evac, UP_PAIRS * f + UP_PAIRS)
                            for a in range(2):
                                k = 2 * j + a
                                if isinstance(j, int):
                                    mh, ml = hh[:, k], hl[:, k]
                                else:
                                    mh, ml = (b[:, bass.ds(k, 1)].rearrange("p a c -> p (a c)") for b in (hh, hl))
                                last = three(ps[m][:], wh[:, slot, KD * a + m], wl[:, slot, KD * a + m], mh, ml,
                                             first and a == 0, final and a == 1)
                            if final and m < KD - 1:
                                last.then_inc(down_done, 1)
                        last.then_inc(pair_done, 1)

                    def norm_product(s):
                        pe.wait_ge(acc_done, (KD - 1) * (s + 1))
                        pe.matmul(ps[7][:], ones[:], acc[:], start=True, stop=True).then_inc(norm_mm, 1)

                    def ffn(f):
                        up_pair(f, 0, PAIR_UP[f], first=True)
                        norm_product(2 * f)
                        up_pair(f, 1, PAIR_UP[f] + 1)
                        with pe.Fori(1, UP_PAIRS // 2) as it:
                            for u in range(2):
                                up_pair(f, it * 2 + u, PAIR_UP[f] + u)
                        down_pair(f, 0, PAIR_DOWN[f], first=True)
                        for j in range(1, DOWN_PAIRS - 1):
                            down_pair(f, j, PAIR_DOWN[f] + j)
                        down_pair(f, DOWN_PAIRS - 1, PAIR_DOWN[f] + DOWN_PAIRS - 1, final=True)

                    pe.sem_inc(pair_done, 2)
                    ffn(0)

                    def scores(i):
                        h, t = item_of(i)
                        if i >= 2:
                            pe.wait_ge(p_done, 2 * (i - 1))
                        for s in range(2):
                            half = slice(DD * s, DD * s + DD)
                            last = pe.matmul(ps[2 * (i % 2) + s][:, 0:(t + 1) * P], dqk[half, h, t * P:(t + 1) * P],
                                             dqk[half, H + h, 0:(t + 1) * P], start=True, stop=True)
                        last.then_inc(sc_mm, 1)

                    def pe_step(kind, *a):
                        if kind == "first":
                            n = PAIR_PROJ
                            pe.wait_ge(lo_done, n + 3)
                            ch, cl = (wt[:, n % 2].rearrange("p (k a) c -> p k (a c)", a=2) for wt in (wh, wl))
                            for k in range(KD):
                                for b in range(2):
                                    pe.wait_ge(x_chunk, KD + min(max(k + 1, b + 1), KD))
                                    last = three(ps[b][:], ch[:, k, b * P:(b + 1) * P], cl[:, k, b * P:(b + 1) * P],
                                                 xh[:, k], xl[:, k], k == 0, k == KD - 1)
                                    if k == KD - 1:
                                        last.then_inc(half_done if b == 0 else pair_done, 1)
                            norm_product(1)
                        elif kind == "proj":
                            u, part = a
                            p, j = divmod(u, 2)
                            n = PAIR_PROJ + p
                            slot, bank = n % 2, u % 4
                            if j == 0 and part == 0:
                                pe.wait_ge(lo_done, n + 3)
                            if part == 0 and u >= 4:
                                q = u - 4
                                if q // 2 in (V_PAIR, V_PAIR + 1):
                                    pe.wait_ge(v_evac, q - 2 * V_PAIR + 1)
                                else:
                                    pe.wait_ge(mix_evac, q + 1)
                            ch, cl = (wt[:, slot].rearrange("p (k a) c -> p k (a c)", a=2) for wt in (wh, wl))
                            if p in (V_PAIR, V_PAIR + 1):
                                tok = slice((2 * j + part) * P, (2 * j + part + 1) * P)
                                for k in range(KD):
                                    last = three(ps[bank][:, part * 256:(part + 1) * 256], xh[:, k, tok], xl[:, k, tok],
                                                 ch[:, k, :], cl[:, k, :], k == 0, k == KD - 1)
                            else:
                                for k in range(4 * part, 4 * part + 4):
                                    last = three(ps[bank][:], ch[:, k, j * P:(j + 1) * P], cl[:, k, j * P:(j + 1) * P],
                                                 xh[:, k], xl[:, k], k == 0, k == KD - 1)
                            if part == 1:
                                last.then_inc(half_done if j == 0 else pair_done, 1)
                        elif kind == "ab":
                            pe.wait_ge(ab_split, 1)
                            for k in range(KD):
                                last = three(ps[SUM_BANK][0:2 * H, :], abh[:, k], abl[:, k], xh[:, k], xl[:, k], k == 0,
                                             k == KD - 1)
                            last.then_inc(ab_mm, 1)
                        elif kind == "abturn":
                            pe.wait_ge(ab_scaled, 1)
                            ident = mask("ident")
                            for t in range(NT):
                                tok = slice(t * P, (t + 1) * P)
                                pe.transpose(ps[SUM_BANK][:, 16 * t:16 * t + 2 * H], abf[0:2 * H, tok], ident[0:2 * H, 0:2 * H])
                                last = pe.transpose(ps[SUM_BANK][:, 16 * t + 2 * H:16 * t + 2 * H + 1], rstd[0:1, tok],
                                                    ident[0:1, 0:1])
                            last.then_inc(ab_turned, 1)
                        elif kind == "decay":
                            pe.wait_ge(g_done, 1)
                            pe.wait_ge(l2_done, 4)
                            pe.matmul(ps[SUM_BANK][:, 128:128 + NT * H], mask("tri"), gl[:].rearrange("p t h -> p (t h)"),
                                      start=True, stop=True)
                            pe.matmul(ps[SUM_BANK][:, 192:192 + NT * H], mask("suffix"), gl[:].rearrange("p t h -> p (t h)"),
                                      start=True, stop=True).then_inc(gcol_mm, 1)
                        elif kind == "l2sum":
                            n, = a
                            pe.wait_ge(l2_sq, n + 1)
                            if n >= 4:
                                pe.wait_ge(l2_done, n - 3)
                            if n == 2:
                                pe.wait_ge(rstd_done, 2)
                            if n == 3:
                                pe.wait_ge(ab_by_token, 1)
                            if n == 7:
                                pe.wait_ge(gcol_exp, 3)
                            pe.matmul(ps[L2_BANKS[n % 4]][:], ones[:], (sq, acc)[n % 2][:], start=True, stop=True)\
                              .then_inc(l2_mm, 1)
                        elif kind == "prep":
                            g, = a
                            if g == 0:
                                pe.wait_ge(l2_done, 2 * H)
                            for s in range(2):
                                t, o = 2 * g + s, 2 * g + s
                                if g:
                                    pe.wait_ge(w_done, o - 1)
                                    pe.wait_ge(u_done, o - 1)
                                for h in range(H):
                                    last = pe.matmul(ps[4 + 2 * s][:, h * P:(h + 1) * P],
                                                     gl[:, t, h:h + 1].broadcast_to([P, P]), mask("tri"),
                                                     start=True, stop=True)
                                last.then_inc(grow_mm, 1)
                                tok = slice(t * P, (t + 1) * P)
                                for h in range(H):
                                    last = pe.matmul(ps[5 + 2 * s][:, h * P:(h + 1) * P], qkv[:, H + h, tok],
                                                     qkv[:, H + h, tok], start=True, stop=True)
                                last.then_inc(kk_mm, 1)
                        elif kind == "prepqk":
                            g, = a
                            for s in range(2):
                                o = 2 * g + s
                                tok = slice(o * P, (o + 1) * P)
                                pe.wait_ge(dx_done, o + 1)
                                pe.wait_ge(e_done, o + 1)
                                for h in range(H):
                                    last = pe.matmul(ps[4 + 2 * s][:, h * P:(h + 1) * P], qkv[:, H + h, tok],
                                                     qkv[:, h, tok], start=True, stop=True)
                                last.then_inc(qk_mm, 1)
                        elif kind == "level0":
                            g, = a
                            for s in range(2):
                                o = 2 * g + s
                                pe.wait_ge(t0_done, o + 1)
                                for h in range(H):
                                    last = pe.transpose(ps[4 + 2 * s][:, h * P:(h + 1) * P], bT[s][:, h], mask("ident"))
                                last.then_inc(t0_turn, 1)
                        elif kind == "right":
                            g, lv = a
                            for s in range(2):
                                o = (g * 5 + lv - 1) * 2 + s
                                pe.wait_ge(b_done, o + 1)
                                if lv == 1:
                                    pe.wait_ge(u0_done, 2 * g + s + 1)
                                else:
                                    pe.wait_ge(tu_done, g * 18 + (lv - 2) * 4 + 2 * s + 2)
                                for h in range(H):
                                    last = pe.matmul(ps[4 + 2 * s][:, h * P:(h + 1) * P], bB[s][:, h], bU[s][:, h],
                                                     start=True, stop=True)
                                last.then_inc(r_mm, 1)
                        elif kind == "left":
                            g, lv = a
                            for s in range(2):
                                t, o = 2 * g + s, (g * 5 + lv - 1) * 2 + s
                                pe.wait_ge(r_done, o + 1)
                                if lv < 5:
                                    for h in range(H):
                                        pe.matmul(ps[5 + 2 * s][:, h * P:(h + 1) * P], wT[:, t, h], bT[s][:, h],
                                                  start=True, stop=True)
                                for h in range(H):
                                    last = pe.matmul(ps[4 + 2 * s][:, h * P:(h + 1) * P], bT[s][:, h], wT[:, t, h],
                                                     start=True, stop=True)
                                last.then_inc(du_mm, 1)
                        elif kind == "turnkv":
                            g, = a
                            if g == 0:
                                pe.wait_ge(silu_done, 3 * H)
                            for s in range(2):
                                o = 2 * g + s
                                tok = slice(o * P, (o + 1) * P)
                                pe.wait_ge(tu_done, g * 18 + 16 + s + 1)
                                for h in range(H):
                                    last = pe.transpose(ps[4 + 2 * s][:, h * P:(h + 1) * P], qkv[:, H + h, tok], mask("ident"))
                                last.then_inc(kturn, 1)
                                for h in range(H):
                                    last = pe.transpose(ps[5 + 2 * s][:, h * P:(h + 1) * P], qkv[:, 2 * H + h, tok], mask("ident"))
                                last.then_inc(vturn, 1)
                        elif kind == "solved":
                            g, = a
                            for s in range(2):
                                o = 2 * g + s
                                tok = slice(o * P, (o + 1) * P)
                                pe.wait_ge(kb_done, 2 * (o + 1))
                                for h in range(H):
                                    last = pe.matmul(ps[4 + 2 * s][:, h * P:(h + 1) * P], bB[s][:, h], bU[s][:, h],
                                                     start=True, stop=True)
                                last.then_inc(w_mm, 1)
                                pe.wait_ge(vb_done, o + 1)
                                for h in range(H):
                                    last = pe.matmul(ps[5 + 2 * s][:, h * P:(h + 1) * P], bU[s][:, h], qkv[:, 2 * H + h, tok],
                                                     start=True, stop=True)
                                last.then_inc(u_mm, 1)
                        elif kind == "scan":
                            j, = a
                            t, r = j // 2, CH * (j % 2)
                            rows = slice(r, r + CH)
                            if j == 0:
                                pe.wait_ge(w_done, NT)
                                pe.wait_ge(u_done, NT)
                            pe.wait_ge(s_done, j + 1)
                            for h in range(H):
                                last = pe.matmul(ps[4][rows, h * P:(h + 1) * P], wT[:, t, h, rows], state[:, h],
                                                 start=True, stop=True)
                            last.then_inc(ws_mm, 1)
                        elif kind == "update":
                            j, = a
                            t, r = j // 2, CH * (j % 2)
                            rows, cols = slice(r, r + CH), slice(j * CH, (j + 1) * CH)
                            tok = slice(t * P, (t + 1) * P)
                            if j >= 1:
                                pe.wait_ge(o_done, j)
                            if norms_before(j):
                                pe.wait_ge(hn_ln, norms_before(j))
                            pe.wait_ge(vnew_done, j + 1)
                            for h in range(H):
                                pe.matmul(ps[6][:, h * CH:(h + 1) * CH], state[:, h], qkv[:, h, cols], start=True, stop=False)
                                last = pe.matmul(ps[6][:, h * CH:(h + 1) * CH], vnew[rows, h], qkT[rows, t, h, rows],
                                                 start=False, stop=True)
                            last.then_inc(o_mm, 1)
                            for h in range(H if j < NCH - 1 else 0):
                                last = pe.matmul(ps[4][:, h * P:(h + 1) * P], qkv[rows, H + h, tok], vnew[rows, h],
                                                 start=True, stop=True)
                            if j < NCH - 1:
                                last.then_inc(sup_mm, 1)
                        elif kind == "attend":
                            i, = a
                            if i == 0:
                                pe.wait_ge(mix_evac, 24)
                                pe.wait_ge(rope_done, 2 * H)
                                scores(0)
                            q = i - 2
                            if 0 <= q < H * NT:
                                t = item_of(q)[1]
                                pe.wait_ge(a_done, q + 1)
                                if q >= 1:
                                    pe.wait_ge(at_done, q)
                                else:
                                    pe.wait_ge(u_done, NT)
                                for k in range(t + 1):
                                    last = pe.transpose(ps[5][:, k * P:(k + 1) * P], prob[q % 3][:, 0, k * P:(k + 1) * P],
                                                        mask("ident"))
                                last.then_inc(at_mm, 1)
                            q = i - 3
                            if q >= 0:
                                h, t = item_of(q)
                                pe.wait_ge(at_done, q + 1)
                                if q:
                                    pe.wait_ge(pv_done, q)
                                else:
                                    pe.wait_ge(v_evac, 4)
                                for k in range(t + 1):
                                    last = pe.matmul(ps[7][:, 0:P],
                                                     V[:, k, h * P:(h + 1) * P], attT[q % 2][:, k], start=k == 0, stop=k == t)
                                last.then_inc(pv_mm, 1)
                            if i + 1 < H * NT:
                                scores(i + 1)
                        elif kind == "normsum":
                            o, = a
                            pe.wait_ge(hn_sq, o + 1)
                            if o == 2 * NT - 1:
                                pe.wait_ge(vnew_done, NCH)
                            else:
                                if updates_before(o):
                                    pe.wait_ge(o_done, updates_before(o))
                                if o:
                                    pe.wait_ge(hn_ln, o)
                            pe.matmul(ps[normed(o)[5]][:], ones[:], (sq, acc)[o % 2][:], start=True, stop=True)\
                              .then_inc(hn_mm, 1)

                    for st in steps:
                        pe_step(*st)
                    for p in range(OUT_PAIRS):
                        n = PAIR_OUT + p
                        pe.wait_ge(lo_done, n + 3)
                        pe.wait_ge(hn_done, (min(att_last, delta_last) if p < 2 else 2 * NT - 1) + 1)
                        for m in range(KD):
                            if p == 0 and m == 4:
                                pe.wait_ge(hn_ln, 2 * NT)
                            for a in range(2):
                                k = 2 * out_order[p] + a
                                last = three(ps[m][:], wh[:, n % 2, KD * a + m], wl[:, n % 2, KD * a + m], xh[:, k],
                                             xl[:, k], p == 0 and a == 0, p == OUT_PAIRS - 1 and a == 1)
                            if p == OUT_PAIRS - 1 and m < KD - 1:
                                last.then_inc(out_done, 1)
                        last.then_inc(pair_done, 1)
                    ffn(1)

        with nc.Fori(0, DEPTH) as l:
            body(l)
            nc.all_engine_barrier()
            engines = (nc.sync, nc.scalar, nc.vector, nc.gpsimd, nc.tensor)
            for i, s in enumerate(layer_sems):
                engines[i % len(engines)].sem_clear(s)
            nc.all_engine_barrier()

        f_mm, f_ln, f_r, f_y, f_turn, f_out, f_id = (
            ctx.enter_context(nc.semaphore(n)) for n in ("f_mm", "f_ln", "f_r", "f_y", "f_turn", "f_out", "f_id"))
        f_kept = [ctx.enter_context(nc.semaphore(f"f_kept{e}")) for e in range(2)]
        with nc.Block() as block:
            @block.sync
            def _(sp):
                sp.dma_start(ident0[:], masks_in[:, CONSTS.index("ident"), :]).then_inc(f_id, 16)
                for o in range(2 * NT):
                    q, t = divmod(o, NT)
                    sp.wait_ge(f_kept[o % 2], o // 2 + 1)
                    sp.dma_start(out[t * P:(t + 1) * P, 4 * q * P:4 * (q + 1) * P],
                                 xstage[:, t, 4 * q * P:4 * (q + 1) * P]).then_inc(f_out, 16)
                sp.wait_ge(f_out, 16 * 2 * NT)
                for s in range(2):
                    sp.wait_ge(ahead_raw[s], 32 * (DEPTH + 1))

            @block.scalar
            def _(act):
                act.wait_ge(f_mm, 1)
                act.activation(rtok[:], ps[7][:, 0:NT], ACT.Ln, scale=1.0 / D, bias=eps_c[:, 0:1]).then_inc(f_ln, 1)
                act.wait_ge(f_ln, 1)
                act.activation(rtok[:], rtok[:], ACT.Exp, scale=-0.5).then_inc(f_r, 1)
                act.wait_ge(f_r, 1)
                for o in range(0, 2 * NT, 2):
                    q, t = divmod(o, NT)
                    act.wait_ge(f_turn, o + 1)
                    act.activation(xstage[:, t, 4 * q * P:4 * (q + 1) * P], ps[2 * t + q][:], ACT.Copy,
                                   scale=rtok[:, t:t + 1]).then_inc(f_kept[0], 1)

            @block.vector
            def _(dve):
                dve.wait_ge(ahead_par, 16 * (DEPTH + 1))
                for m in range(KD):
                    dve.tensor_scalar(x[:, m], x[:, m], par[:, ROW_FINAL + m:ROW_FINAL + m + 1], None, ALU.mult)\
                       .then_inc(f_y, 1)
                dve.wait_ge(f_r, 1)
                for o in range(1, 2 * NT, 2):
                    q, t = divmod(o, NT)
                    dve.wait_ge(f_turn, o + 1)
                    dve.tensor_scalar(xstage[:, t, 4 * q * P:4 * (q + 1) * P], ps[2 * t + q][:], rtok[:, t:t + 1], None,
                                      ALU.mult).then_inc(f_kept[1], 1)

            @block.tensor
            def _(pe):
                for t in range(NT):
                    last = pe.matmul(ps[7][:, t:t + 1], acc[:, t * P:(t + 1) * P], ones[:, 0:1], start=True, stop=True)
                last.then_inc(f_mm, 1)
                pe.wait_ge(f_id, 16)
                for q in range(2):
                    for t in range(NT):
                        if 2 * t + q == 7:
                            pe.wait_ge(f_ln, 1)
                        for j in range(4):
                            if t == 0:
                                pe.wait_ge(f_y, 4 * q + j + 1)
                            last = pe.transpose(ps[2 * t + q][:, j * P:(j + 1) * P], x[:, 4 * q + j, t * P:(t + 1) * P],
                                                ident0[:])
                        last.then_inc(f_turn, 1)


_INS = ["x", "ffn1_w_gate", "ffn1_w_up", "ffn1_w_down", "w_in", "w_out", "ffn2_w_gate", "ffn2_w_up", "ffn2_w_down"]
_SMALL = ["a_log", "dt_bias", "lambda_q1", "lambda_k1", "lambda_q2", "lambda_k2"]


def params_of(inputs):
    cols = [inputs["conv_w"], inputs["ffn1_norm"], inputs["mix_norm"], inputs["ffn2_norm"], inputs["gdn_norm"],
            inputs["diff_norm"], np.broadcast_to(inputs["final_norm"], (DEPTH, D))]
    rows = np.concatenate([np.asarray(c).reshape(DEPTH, -1, P) for c in cols], 1)
    return np.ascontiguousarray(rows.transpose(0, 2, 1))


def kernel(**inputs):
    import concourse.bacc as bacc
    from concourse.bass_utils import run_bass_kernel_spmd

    nc = bacc.Bacc("TRN2", target_bir_lowering=False, num_devices=1)
    arrays, args = {}, []
    masks, angle, lam = shape_constants()
    given = [(n, np.ascontiguousarray(inputs[n])) for n in _INS]
    given[0] = ("x", given[0][1].reshape(S, D))
    given += [("params", params_of(inputs))] + [(n, np.ascontiguousarray(inputs[n])) for n in _SMALL]
    for name, a in given + [("masks", masks), ("angle", angle), ("lam", lam)]:
        arrays[f"in_{name}"] = a
        args.append(nc.dram_tensor(f"in_{name}", a.shape, mybir.dt.from_np(a.dtype), kind="ExternalInput").ap())
    args.append(nc.dram_tensor("out", [S, D], F32, kind="ExternalOutput").ap())
    build(nc, *args)
    r = run_bass_kernel_spmd(nc, [arrays], core_ids=[0])
    return r.results[0]["out"].reshape(1, S, D)
```
